# Optimizing a Trainium2 kernel written in Bass

```python
import math
import jax, jax.numpy as jnp
from jax import lax
import numpy as np

D_MODEL = 1024
BATCH = 1
SEQ = 256
DEPTH = 1
DEC_BATCH = 1
DEC_SEQ = 64
PAST_LEN = 128

CHUNK = 64
GLA_HEADS = 4
GLA_DK = D_MODEL // 2 // GLA_HEADS
GLA_DV = D_MODEL // GLA_HEADS
GLA_RANK = 16
GLA_GATE_NORM = 16.0
GLA_NORM_EPS = 1e-5
RWKV_HEAD = 64
RWKV_DIM = D_MODEL
RWKV_HEADS = RWKV_DIM // RWKV_HEAD
RWKV_W_RANK = 64
RWKV_A_RANK = 64
RWKV_G_RANK = 128
RWKV_GN_EPS = 64e-5
SSM_INNER = 2 * D_MODEL
SSM_HEADDIM = 64
SSM_HEADS = SSM_INNER // SSM_HEADDIM
SSM_GROUPS = 4
SSM_STATE = 128
SSM_CONV = 4
SSM_CONV_DIM = SSM_INNER + 2 * SSM_GROUPS * SSM_STATE
SSM_NORM_EPS = 1e-5
N_EXPERTS = 64
TOP_K = 8
N_EXPERT_GROUPS = 8
TOPK_GROUPS = 4
D_EXPERT = D_MODEL // 4
D_SHARED = D_EXPERT
ROUTED_SCALE = 2.5
MOE_BLOCK = 256
DN_ALPHA = (2.0 * DEPTH) ** 0.25
DN_BETA = (8.0 * DEPTH) ** -0.25
LN_EPS = 1e-5
N_GATE = 3 * D_MODEL
GLA_PROJ = 2 * GLA_HEADS * GLA_DK + 2 * GLA_HEADS * GLA_DV + GLA_RANK
RWKV_PROJ = 3 * RWKV_DIM + RWKV_W_RANK + RWKV_A_RANK + RWKV_G_RANK
SSM_PROJ = SSM_INNER + SSM_CONV_DIM + SSM_HEADS
N_IN = N_GATE + GLA_PROJ + RWKV_PROJ + SSM_PROJ

kernel_name = 'hybrid_gla_rwkv7_ssd_moe_stream'

def _split(u, sizes):
    offs = np.cumsum(sizes)[:-1].tolist()
    return jnp.split(u, offs, axis=-1)

def _layer_norm(x, g, b):
    xf = x.astype(jnp.float32)
    mu = jnp.mean(xf, -1, keepdims=True)
    var = jnp.mean(jnp.square(xf - mu), -1, keepdims=True)
    return (xf - mu) * lax.rsqrt(var + LN_EPS) * g + b

def _rms_norm(x, g, eps):
    xf = x.astype(jnp.float32)
    return xf * lax.rsqrt(jnp.mean(xf * xf, -1, keepdims=True) + eps) * g

def _causal_conv(u, buf, w, bias):
    l = u.shape[1]
    full = jnp.concatenate([buf.astype(u.dtype), u], axis=1)
    out = lax.conv_general_dilated(full, w[:, None, :].astype(u.dtype), window_strides=(1,), padding='VALID',
                                   dimension_numbers=('NWC', 'WIO', 'NWC'),
                                   feature_group_count=w.shape[1])
    return out + bias, full[:, l:]

def _gla_chunked(q, k, v, log_a, s0):
    b, l, h, dk = q.shape
    dv = v.shape[-1]
    c = min(CHUNK, l)
    n = l // c

    def blocks(t):
        return t.astype(jnp.float32).reshape(b, n, c, h, t.shape[-1]).transpose(0, 3, 1, 2, 4)

    q, k, v, g = blocks(q), blocks(k), blocks(v), blocks(log_a)
    g = jnp.cumsum(g, axis=3)
    g_last = g[:, :, :, -1:]
    q_dec = q * jnp.exp(g) * dk ** -0.5
    k_inv = k * jnp.exp(-g)
    k_end = k * jnp.exp(g_last - g)
    causal = jnp.tril(jnp.ones((c, c), dtype=bool))
    scores = jnp.where(causal, jnp.einsum('bhnqd,bhnsd->bhnqs', q_dec, k_inv), 0.0)
    o_intra = jnp.einsum('bhnqs,bhnsv->bhnqv', scores, v)
    chunk_kv = jnp.einsum('bhnsd,bhnsv->nbhdv', k_end, v)
    chunk_decay = jnp.exp(g_last[:, :, :, 0]).transpose(2, 0, 1, 3)

    def step(s, inp):
        kv, dec = inp
        return s * dec[..., None] + kv, s

    s_final, s_prev = lax.scan(step, s0.astype(jnp.float32), (chunk_kv, chunk_decay))
    o_inter = jnp.einsum('bhnqd,nbhdv->bhnqv', q_dec, s_prev)
    o = (o_intra + o_inter).transpose(0, 2, 3, 1, 4).reshape(b, l, h, dv)
    return o, s_final

def _gla_mixer(u, s0, wa2, ba, norm_g):
    b, l, _ = u.shape
    q, k, v, r, a_low = _split(u, (GLA_HEADS * GLA_DK, GLA_HEADS * GLA_DK, GLA_HEADS * GLA_DV,
                                   GLA_HEADS * GLA_DV, GLA_RANK))
    log_a = jax.nn.log_sigmoid((a_low @ wa2 + ba).astype(jnp.float32)) / GLA_GATE_NORM
    hk = lambda t: t.reshape(b, l, GLA_HEADS, GLA_DK)
    o, s_new = _gla_chunked(hk(q), hk(k), v.reshape(b, l, GLA_HEADS, GLA_DV), hk(log_a), s0)
    o = _rms_norm(o, norm_g, GLA_NORM_EPS).reshape(b, l, GLA_HEADS * GLA_DV)
    return o * jax.nn.silu(r.astype(jnp.float32)), s_new

def _rwkv7_scan(r, w, k, v, a, bb, s0):
    def step(s, inp):
        rt, wt, kt, vt, at, bt = inp
        sa = jnp.einsum('bhvk,bhk->bhv', s, at)
        s = s * wt[:, :, None, :] + sa[..., None] * bt[:, :, None, :] + vt[..., None] * kt[:, :, None, :]
        return s, jnp.einsum('bhvk,bhk->bhv', s, rt)

    xs = tuple(t.astype(jnp.float32).transpose(1, 0, 2, 3) for t in (r, w, k, v, a, bb))
    s_final, ys = lax.scan(step, s0.astype(jnp.float32), xs)
    return ys.transpose(1, 0, 2, 3), s_final

def _rwkv7_mixer(u, shift_buf, s0, mu, w0, w2, a0, a2, g2, k_k, k_a, r_k, ln_g, ln_b):
    b, l, _ = u.shape
    full = jnp.concatenate([shift_buf.astype(u.dtype), u], axis=1)
    us = u + (full[:, :-1] - u) * mu
    r, k, v, w_low, a_low, g_low = _split(us, (RWKV_DIM, RWKV_DIM, RWKV_DIM,
                                               RWKV_W_RANK, RWKV_A_RANK, RWKV_G_RANK))
    log_w = -jax.nn.softplus(-(w0 + jnp.tanh(w_low) @ w2).astype(jnp.float32)) - 0.5
    decay = jnp.exp(-jnp.exp(log_w))
    a = jax.nn.sigmoid((a0 + a_low @ a2).astype(jnp.float32))
    gate = jax.nn.sigmoid(g_low) @ g2
    heads = lambda t: t.reshape(b, l, RWKV_HEADS, RWKV_HEAD)
    kk = heads(k * k_k).astype(jnp.float32)
    kk = kk * lax.rsqrt(jnp.maximum(jnp.sum(kk * kk, -1, keepdims=True), 1e-24))
    k = k * (1.0 + (a - 1.0) * k_a)
    y, s_new = _rwkv7_scan(heads(r), heads(decay), heads(k), heads(v), -kk, kk * heads(a), s0)
    mean = jnp.mean(y, -1, keepdims=True)
    var = jnp.mean(jnp.square(y - mean), -1, keepdims=True)
    y = ((y - mean) * lax.rsqrt(var + RWKV_GN_EPS)).reshape(b, l, RWKV_DIM) * ln_g + ln_b
    bonus = jnp.sum(heads(r) * heads(k) * r_k, -1, keepdims=True) * heads(v)
    y = (y + bonus.reshape(b, l, RWKV_DIM)) * gate
    return y, full[:, -1:], s_new

def _ssd_chunked(x, dt, a, bm, cm, s0):
    b, l, h, p = x.shape
    g, nst = bm.shape[2], bm.shape[3]
    j = h // g
    c = min(CHUNK, l)
    n = l // c
    f32 = jnp.float32
    dt = dt.astype(f32)
    acum = jnp.cumsum((dt * a).reshape(b, n, c, h).transpose(0, 3, 1, 2), axis=-1)
    xdt = (x.astype(f32) * dt[..., None]).reshape(b, n, c, g, j, p)
    bm = bm.astype(f32).reshape(b, n, c, g, nst)
    cm = cm.astype(f32).reshape(b, n, c, g, nst)
    causal = jnp.tril(jnp.ones((c, c), dtype=bool))
    seg = acum[..., :, None] - acum[..., None, :]
    decay = jnp.where(causal, jnp.exp(jnp.where(causal, seg, 0.0)), 0.0).reshape(b, g, j, n, c, c)
    cb = jnp.einsum('bnqgd,bnsgd->bgnqs', cm, bm)
    y_diag = jnp.einsum('bgjnqs,bnsgjp->bnqgjp', cb[:, :, None] * decay, xdt)
    a_last = acum[..., -1]
    dec_end = jnp.exp(a_last[..., None] - acum).reshape(b, g, j, n, c).transpose(0, 3, 4, 1, 2)
    chunk_states = jnp.einsum('bnsgd,bnsgjp->nbgjpd', bm, xdt * dec_end[..., None]).reshape(n, b, h, p, nst)
    chunk_decay = jnp.exp(a_last).transpose(2, 0, 1)

    def step(s, inp):
        st, dec = inp
        return s * dec[..., None, None] + st, s

    s_final, s_prev = lax.scan(step, s0.astype(f32), (chunk_states, chunk_decay))
    dec_in = jnp.exp(acum).reshape(b, g, j, n, c).transpose(0, 3, 4, 1, 2)
    y_off = jnp.einsum('bnqgd,nbgjpd->bnqgjp', cm, s_prev.reshape(n, b, g, j, p, nst)) * dec_in[..., None]
    return (y_diag + y_off).reshape(b, l, h, p), s_final

def _mamba2_mixer(u, conv_buf, s0, conv_w, conv_b, dt_bias, a_log, d_skip, norm_g):
    b, l, _ = u.shape
    z, xbc, dt = _split(u, (SSM_INNER, SSM_CONV_DIM, SSM_HEADS))
    xbc, conv_new = _causal_conv(xbc, conv_buf, conv_w, conv_b)
    xbc = jax.nn.silu(xbc)
    xs, bm, cm = _split(xbc, (SSM_INNER, SSM_GROUPS * SSM_STATE, SSM_GROUPS * SSM_STATE))
    xs = xs.reshape(b, l, SSM_HEADS, SSM_HEADDIM)
    dt = jax.nn.softplus((dt + dt_bias).astype(jnp.float32))
    a = -jnp.exp(a_log.astype(jnp.float32))
    y, s_new = _ssd_chunked(xs, dt, a, bm.reshape(b, l, SSM_GROUPS, SSM_STATE),
                            cm.reshape(b, l, SSM_GROUPS, SSM_STATE), s0)
    y = (y + xs * d_skip[:, None]).reshape(b, l, SSM_INNER) * jax.nn.silu(z.astype(jnp.float32))
    y = _rms_norm(y.reshape(b, l, SSM_GROUPS, SSM_INNER // SSM_GROUPS),
                  norm_g.reshape(SSM_GROUPS, SSM_INNER // SSM_GROUPS), SSM_NORM_EPS)
    return y.reshape(b, l, SSM_INNER), conv_new, s_new

def _moe(x, w_router, router_bias, exp_w1, exp_w3, exp_w2, sh_w1, sh_w3, sh_w2):
    b, l, d = x.shape
    t = x.reshape(b * l, d)
    s = jax.nn.sigmoid((t @ w_router).astype(jnp.float32))
    sb = s + router_bias
    per_group = N_EXPERTS // N_EXPERT_GROUPS
    gscore = jnp.sum(lax.top_k(sb.reshape(-1, N_EXPERT_GROUPS, per_group), 2)[0], -1)
    _, gidx = lax.top_k(gscore, TOPK_GROUPS)
    gmask = jnp.sum(jax.nn.one_hot(gidx, N_EXPERT_GROUPS, dtype=jnp.float32), 1)
    emask = jnp.repeat(gmask, per_group, axis=1) > 0
    _, eidx = lax.top_k(jnp.where(emask, sb, -jnp.inf), TOP_K)
    wsel = jnp.take_along_axis(s, eidx, axis=1)
    wsel = wsel / jnp.sum(wsel, -1, keepdims=True) * ROUTED_SCALE
    gates = jnp.einsum('tk,tke->te', wsel, jax.nn.one_hot(eidx, N_EXPERTS, dtype=jnp.float32)).astype(t.dtype)
    n_tok = t.shape[0]
    n_blk = -(-n_tok // MOE_BLOCK)
    pad = n_blk * MOE_BLOCK - n_tok
    tp = jnp.pad(t, ((0, pad), (0, 0))).reshape(n_blk, MOE_BLOCK, d)
    gp = jnp.pad(gates, ((0, pad), (0, 0))).reshape(n_blk, MOE_BLOCK, N_EXPERTS)

    def block(args):
        tb, gb = args
        hid = jax.nn.silu(jnp.einsum('td,edf->tef', tb, exp_w1)) * jnp.einsum('td,edf->tef', tb, exp_w3)
        return jnp.einsum('tef,efd->td', hid * gb[..., None], exp_w2)

    routed = lax.map(block, (tp, gp)).reshape(n_blk * MOE_BLOCK, d)[:n_tok]
    shared = (jax.nn.silu(t @ sh_w1) * (t @ sh_w3)) @ sh_w2
    return (routed + shared).reshape(b, l, d)

def _layer(x, st_gla, st_rwkv, st_shift, st_ssm, st_conv,
           w_in, gla_wa2, gla_ba, gla_norm_g, gla_wo,
           rwkv_mu, rwkv_w0, rwkv_w2, rwkv_a0, rwkv_a2, rwkv_g2, rwkv_k_k, rwkv_k_a, rwkv_r_k,
           rwkv_ln_g, rwkv_ln_b, rwkv_wo,
           ssm_conv_w, ssm_conv_b, ssm_dt_bias, ssm_a_log, ssm_d, ssm_norm_g, ssm_wo,
           w_out, ln1_g, ln1_b,
           w_router, router_bias, exp_w1, exp_w3, exp_w2, sh_w1, sh_w3, sh_w2, ln2_g, ln2_b):
    b, l, d = x.shape
    u = x @ w_in
    u_gate, u_gla, u_rwkv, u_ssm = _split(u, (N_GATE, GLA_PROJ, RWKV_PROJ, SSM_PROJ))
    o_gla, s_gla = _gla_mixer(u_gla, st_gla, gla_wa2, gla_ba, gla_norm_g)
    o_rwkv, shift_new, s_rwkv = _rwkv7_mixer(u_rwkv, st_shift, st_rwkv, rwkv_mu, rwkv_w0, rwkv_w2, rwkv_a0,
                                             rwkv_a2, rwkv_g2, rwkv_k_k, rwkv_k_a, rwkv_r_k, rwkv_ln_g, rwkv_ln_b)
    o_ssm, conv_new, s_ssm = _mamba2_mixer(u_ssm, st_conv, st_ssm, ssm_conv_w, ssm_conv_b, ssm_dt_bias,
                                           ssm_a_log, ssm_d, ssm_norm_g)
    g = jax.nn.sigmoid(u_gate.astype(jnp.float32)).reshape(b, l, 3, d)
    merged = g[:, :, 0] * (o_gla @ gla_wo) + g[:, :, 1] * (o_rwkv @ rwkv_wo) + g[:, :, 2] * (o_ssm @ ssm_wo)
    h = _layer_norm(DN_ALPHA * x + merged @ w_out, ln1_g, ln1_b).astype(x.dtype)
    h = _layer_norm(DN_ALPHA * h + _moe(h, w_router, router_bias, exp_w1, exp_w3, exp_w2, sh_w1, sh_w3, sh_w2),
                    ln2_g, ln2_b).astype(x.dtype)
    return h, s_gla, s_rwkv, shift_new, s_ssm, conv_new

def _zero_states(batch, dtype):
    return (jnp.zeros((batch, GLA_HEADS, GLA_DK, GLA_DV), jnp.float32),
            jnp.zeros((batch, RWKV_HEADS, RWKV_HEAD, RWKV_HEAD), jnp.float32),
            jnp.zeros((batch, 1, RWKV_PROJ), dtype),
            jnp.zeros((batch, SSM_HEADS, SSM_HEADDIM, SSM_STATE), jnp.float32),
            jnp.zeros((batch, SSM_CONV - 1, SSM_CONV_DIM), dtype))

def setup_inputs(seed: int = 0) -> dict:
    key = jax.random.key(seed)
    ks = iter(jax.random.split(key, 64))
    f32 = jnp.float32
    L = DEPTH

    def nrm(shape, scale):
        return jax.random.normal(next(ks), shape, f32) * scale

    def near_one(shape):
        return 1.0 + nrm(shape, 0.1)

    dt0 = jnp.exp(jax.random.uniform(next(ks), (L, SSM_HEADS), f32, math.log(1e-3), math.log(1e-1)))
    a_init = jax.random.uniform(next(ks), (L, SSM_HEADS), f32, 1.0, 16.0)
    mu_init = jax.random.uniform(next(ks), (L, RWKV_PROJ), f32)
    return {
        'x_prompt': nrm((BATCH, SEQ, D_MODEL), 1.0),
        'x_sample': nrm((DEC_BATCH, DEC_SEQ, D_MODEL), 1.0),
        'state_gla': nrm((L, DEC_BATCH, GLA_HEADS, GLA_DK, GLA_DV), 0.5),
        'state_rwkv': nrm((L, DEC_BATCH, RWKV_HEADS, RWKV_HEAD, RWKV_HEAD), 0.3),
        'state_rwkv_shift': nrm((L, DEC_BATCH, 1, RWKV_PROJ), 1.0),
        'state_ssm': nrm((L, DEC_BATCH, SSM_HEADS, SSM_HEADDIM, SSM_STATE), 0.3),
        'state_ssm_conv': nrm((L, DEC_BATCH, SSM_CONV - 1, SSM_CONV_DIM), 1.0),
        'ln_in_g': near_one((D_MODEL,)),
        'ln_in_b': nrm((D_MODEL,), 0.02),
        'w_in': nrm((L, D_MODEL, N_IN), D_MODEL ** -0.5),
        'gla_wa2': nrm((L, GLA_RANK, GLA_HEADS * GLA_DK), GLA_RANK ** -0.5),
        'gla_ba': nrm((L, GLA_HEADS * GLA_DK), 0.1),
        'gla_norm_g': near_one((L, GLA_DV)),
        'gla_wo': nrm((L, GLA_HEADS * GLA_DV, D_MODEL), (GLA_HEADS * GLA_DV) ** -0.5),
        'rwkv_mu': mu_init,
        'rwkv_w0': -1.0 + nrm((L, RWKV_DIM), 0.5),
        'rwkv_w2': nrm((L, RWKV_W_RANK, RWKV_DIM), 0.5 * RWKV_W_RANK ** -0.5),
        'rwkv_a0': nrm((L, RWKV_DIM), 0.1),
        'rwkv_a2': nrm((L, RWKV_A_RANK, RWKV_DIM), 0.5 * RWKV_A_RANK ** -0.5),
        'rwkv_g2': nrm((L, RWKV_G_RANK, RWKV_DIM), RWKV_G_RANK ** -0.5),
        'rwkv_k_k': 0.85 + nrm((L, RWKV_DIM), 0.05),
        'rwkv_k_a': near_one((L, RWKV_DIM)),
        'rwkv_r_k': nrm((L, RWKV_HEADS, RWKV_HEAD), 0.1),
        'rwkv_ln_g': near_one((L, RWKV_DIM)),
        'rwkv_ln_b': nrm((L, RWKV_DIM), 0.02),
        'rwkv_wo': nrm((L, RWKV_DIM, D_MODEL), RWKV_DIM ** -0.5),
        'ssm_conv_w': nrm((L, SSM_CONV, SSM_CONV_DIM), SSM_CONV ** -0.5),
        'ssm_conv_b': nrm((L, SSM_CONV_DIM), 0.02),
        'ssm_dt_bias': dt0 + jnp.log(-jnp.expm1(-dt0)),
        'ssm_a_log': jnp.log(a_init),
        'ssm_d': near_one((L, SSM_HEADS)),
        'ssm_norm_g': near_one((L, SSM_INNER)),
        'ssm_wo': nrm((L, SSM_INNER, D_MODEL), SSM_INNER ** -0.5),
        'w_out': nrm((L, D_MODEL, D_MODEL), DN_BETA * D_MODEL ** -0.5),
        'ln1_g': near_one((L, D_MODEL)),
        'ln1_b': nrm((L, D_MODEL), 0.02),
        'w_router': nrm((L, D_MODEL, N_EXPERTS), D_MODEL ** -0.5),
        'router_bias': nrm((L, N_EXPERTS), 0.01),
        'exp_w1': nrm((L, N_EXPERTS, D_MODEL, D_EXPERT), D_MODEL ** -0.5),
        'exp_w3': nrm((L, N_EXPERTS, D_MODEL, D_EXPERT), D_MODEL ** -0.5),
        'exp_w2': nrm((L, N_EXPERTS, D_EXPERT, D_MODEL), DN_BETA * D_EXPERT ** -0.5),
        'sh_w1': nrm((L, D_MODEL, D_SHARED), D_MODEL ** -0.5),
        'sh_w3': nrm((L, D_MODEL, D_SHARED), D_MODEL ** -0.5),
        'sh_w2': nrm((L, D_SHARED, D_MODEL), DN_BETA * D_SHARED ** -0.5),
        'ln2_g': near_one((L, D_MODEL)),
        'ln2_b': nrm((L, D_MODEL), 0.02),
    }

def reference(x_prompt, x_sample, state_gla, state_rwkv, state_rwkv_shift, state_ssm, state_ssm_conv,
              ln_in_g, ln_in_b, w_in, gla_wa2, gla_ba, gla_norm_g, gla_wo,
              rwkv_mu, rwkv_w0, rwkv_w2, rwkv_a0, rwkv_a2, rwkv_g2, rwkv_k_k, rwkv_k_a, rwkv_r_k,
              rwkv_ln_g, rwkv_ln_b, rwkv_wo,
              ssm_conv_w, ssm_conv_b, ssm_dt_bias, ssm_a_log, ssm_d, ssm_norm_g, ssm_wo,
              w_out, ln1_g, ln1_b,
              w_router, router_bias, exp_w1, exp_w3, exp_w2, sh_w1, sh_w3, sh_w2, ln2_g, ln2_b):
    layer_params = (w_in, gla_wa2, gla_ba, gla_norm_g, gla_wo,
                    rwkv_mu, rwkv_w0, rwkv_w2, rwkv_a0, rwkv_a2, rwkv_g2, rwkv_k_k, rwkv_k_a, rwkv_r_k,
                    rwkv_ln_g, rwkv_ln_b, rwkv_wo,
                    ssm_conv_w, ssm_conv_b, ssm_dt_bias, ssm_a_log, ssm_d, ssm_norm_g, ssm_wo,
                    w_out, ln1_g, ln1_b,
                    w_router, router_bias, exp_w1, exp_w3, exp_w2, sh_w1, sh_w3, sh_w2, ln2_g, ln2_b)
    h_p = _layer_norm(x_prompt, ln_in_g, ln_in_b).astype(x_prompt.dtype)
    h_s = _layer_norm(x_sample, ln_in_g, ln_in_b).astype(x_sample.dtype)
    new_p, new_s = [], []
    for i in range(DEPTH):
        lp = [t[i] for t in layer_params]
        h_p, *st_p = _layer(h_p, *_zero_states(h_p.shape[0], h_p.dtype), *lp)
        new_p.append(st_p)
        h_s, *st_s = _layer(h_s, state_gla[i], state_rwkv[i], state_rwkv_shift[i], state_ssm[i],
                            state_ssm_conv[i], *lp)
        new_s.append(st_s)
    gla_p, rwkv_p, shift_p, ssm_p, conv_p = (jnp.stack(z) for z in zip(*new_p))
    gla_s, rwkv_s, shift_s, ssm_s, conv_s = (jnp.stack(z) for z in zip(*new_s))
    return (h_p, h_s, gla_p, rwkv_p, shift_p, ssm_p, conv_p, gla_s, rwkv_s, shift_s, ssm_s, conv_s)


_drawn_inputs = setup_inputs


def setup_inputs(seed=0):
    import zlib

    import numpy as np

    out = dict(_drawn_inputs(seed))
    spreads = {}
    factors = {'rwkv_k_k': 4.198, 'rwkv_ln_b': 3.397, 'ln2_b': 2.853}
    for name, (base, spread) in spreads.items():
        noise = np.random.default_rng([zlib.crc32(name.encode()), seed]).standard_normal(out[name].shape)
        drawn = base * np.exp(spread * noise) if base else spread * noise
        out[name] = __import__('jax').numpy.asarray(drawn.astype(out[name].dtype))
    for name, factor in factors.items():
        out[name] = (out[name] * factor).astype(out[name].dtype)
    return out
```

```python
import concourse.bass as bass
from concourse import mybir
from contextlib import ExitStack, contextmanager

FP32 = mybir.dt.float32
I32 = mybir.dt.int32
ALU = mybir.AluOpType
ACT = mybir.ActivationFunctionType
AX = mybir.AxisListType

D = 1024
KT = D // 128
NTOK = 320
TT3 = 3
L = 64
NCH = NTOK // L
NPC = NCH - 1
HIST = 3
CW = HIST + L

T_RW = 0
T_MISC = 26
T_XBC = 27
T_Z = 51
T_GLA = 67
T_GATE = 91
NT = 115
RING = 4
PRE = 28
FILL = 8
PB = NT - PRE - 2 * NCH * FILL

V_MU, V_W0, V_A0, V_KK, V_KA, V_RK, V_LNG, V_LNB = 0, 26, 34, 42, 50, 58, 66, 74
V_BA, V_GNG, V_CW, V_CB, V_SNG, V_DSK, V_DTB, V_ALOG, V_TOK8 = 82, 86, 88, 184, 208, 224, 240, 241, 242
NV = 245

C_ID, C_ONE, C_BLK, C_M2, C_ML, C_E, C_RST, C_LH, C_PM, C_SEL, C_TRI, C_IOTA = (
    0, 128, 256, 384, 512, 576, 640, 1152, 1280, 1296, 1328, 1456)
NC = 1456 + NTOK

DECAY = 0.6065306597126334
GLA_SCALE = 128 ** -0.5
ALPHA = 2.0 ** 0.25
NE, TOPK, NG, DE = 64, 8, 8, 256
CAP = 64
NBLK = NTOK // CAP
SLOTS = NTOK * TOPK
YRING = 4
MRING = 4
RW_IN, SSM_IN, GLA_IN = 26, 24, 24


def hybrid_layer(nc, io):
    ctx = ExitStack()
    with ctx:
        sems = {}

        def sem(name):
            if name not in sems:
                sems[name] = ctx.enter_context(nc.semaphore(name))
            return sems[name]

        ut = nc.dram_tensor("projected", (NT, 128, NCH, CW), FP32, kind="Internal").ap()
        slots = nc.dram_tensor("expert_rows", (SLOTS, D), FP32, kind="Internal").ap()
        PS = ctx.enter_context(nc.psum_tensor("PS", [128, 8, 512], FP32))

        def sb(name, *shape):
            return ctx.enter_context(nc.sbuf_tensor(name, [128, *shape], FP32))

        CON = sb("constants", NC)
        VEC = sb("feature_vectors", NV)
        HISTS = sb("history", NT, 2, HIST)
        H0 = sb("h0", TT3, D)
        H0T = sb("h0T", KT, NTOK)
        REGION = sb("region", 53100 - (NC + NV + NT * 6 + TT3 * D + KT * NTOK))
        ID, ONE, BLK = (CON[:, c:c + 128] for c in (C_ID, C_ONE, C_BLK))
        M2, ML, E = CON[:, C_M2:C_M2 + 128], CON[:, C_ML:C_ML + 64], CON[:, C_E:C_E + 64]
        LH, PM, SEL, TRI = (CON[:, a:a + n] for a, n in ((C_LH, 128), (C_PM, 16), (C_SEL, 32), (C_TRI, 128)))
        at = [0]

        def size(shape):
            n = 1
            for k in shape:
                n *= k
            return n

        def take(*shape):
            n = size(shape)
            v = REGION[:, at[0]:at[0] + n]
            at[0] += n
            return shaped(v, *shape)

        def shaped(v, *shape):
            names = "abcd"[:len(shape)]
            if len(shape) <= 1:
                return v
            return v.rearrange(f"p ({' '.join(names)}) -> p {' '.join(names)}",
                               **{k: s for k, s in zip(names[1:], shape[1:])})

        def vec(a, n, w):
            return VEC[:, a:a + n].unsqueeze(2).to_broadcast([128, n, w])

        def over(ap, n, m, w):
            return ap.unsqueeze(1).to_broadcast([128, n, w])

        def half(ap, h):
            return ap[64 * h:64 * h + 64, :, 64 * h:64 * h + 64]

        def bank(b, *shape, n=512):
            return shaped(PS[:, b, 0:n], *shape)

        def banks(b, k, *shape):
            v = PS[:, b:b + k, :].rearrange("p b n -> p (b n)")
            return shaped(v, *shape)

        WR = take(RING, KT, 128)
        STG = take(RING, NCH, CW)
        OT = take(32, NTOK)
        mixer_base = at[0]

        UR, US = take(26, L + 1), take(26, L)
        LOW, GS = take(L), take(L)
        (WS, AS, CS, GP, G, GI, KK, SQ, K2, KA, TA, BQ, BV, YS) = (take(8, L) for _ in range(14))
        AR = take(8, 2, L)
        ABD, BBD, KBD, VBD, PBD, PTBD, AKBD, SBD, SABD = (take(8, 128) for _ in range(9))
        VS, PSK, XS, SAS, SS = (take(8, L) for _ in range(5))
        SB, SK = take(8, 2, L), take(8, 2, L)
        PTT = take(8, 2, L)
        SHO = take(26)
        assert at[0] <= REGION.shape[1], at[0]
        W2P, A2P, G2 = (OT[:, 16:].rearrange("p a b -> p (a b)")[:, k * D:k * D + D] for k in range(3))

        at[0] = mixer_base
        UX, UZ, UM = take(24, CW), take(16, L), take(L)
        XC, TMP, TMP2, XS_, XD = take(24, L), take(16, L), take(8, L), take(16, L), take(16, L)
        XTBD, XDBD, XEBD = take(16, 128), take(16, 128), take(16, 128)
        BT2, CT, BTM, CBM = take(4, 2, L), take(4, L), take(4, 128), take(4, L)
        T1, AB, LB, DT2, AC2, SELL = take(L), take(L), take(L), take(2, L), take(2, L), take(32)
        DTS, ACS, ALS, EL, NA = take(16), take(16), take(16), take(32), take(1)
        RD, SEG, EBC, YO, YC, SN = take(16, L), take(16, L), take(16, L), take(16, L), take(16, L), take(2048)
        RG, CVO = take(4, L), take(24, HIST)
        assert at[0] <= REGION.shape[1], at[0]

        at[0] = mixer_base
        UG, UA, WA2 = take(24, L), take(L), take(512)
        T4, AB4, LB4, CS4, EG, EI, EE, QD, KI, KE, SCT, RG4 = (take(4, L) for _ in range(12))
        VT, KET, SG, O8, SQO, RR = take(8, 128), take(4, 128), take(4, 256), take(8, L), take(8, L), take(8, L)

        at[0] = mixer_base
        GT, MG, MTMP, WOUT = take(24, NCH, L), take(8, NTOK), take(2, NTOK), take(KT, D)
        GTF = GT.rearrange("p t c w -> p t (c w)")
        LN1, BN1, MV1, RS1 = take(2, D), take(3, 2, 6), take(3, 2), take(3)
        assert at[0] <= REGION.shape[1], at[0]

        at[0] = 0
        MW = take(MRING, 6144)
        WRT, RB, SCO, CHO, PLACE, TIE3 = take(KT, NE), take(NE), take(3, NE), take(3, NE), take(3, NE), take(3, NE)
        SBI, TIE, TIE2, TRK, GTE, CTOT = (take(NE) for _ in range(6))
        TOP, GSC, GM, CNT, FLAGW = take(NG, 8), take(8), take(8), take(1), take(1)
        INFO, OH, XE = take(3, NE, 2), take(2, 3, CAP), take(2, KT, CAP)
        SIL, HID, SHID, Y = take(2, 2, CAP), take(2, 2, CAP), take(2, NTOK), take(YRING, D)
        ACC, GA, LN2, BN2, MV2, RS2 = take(3, D), take(YRING), take(2, D), take(3, 2, 6), take(3, 2), take(3)
        assert at[0] <= REGION.shape[1], at[0]
        IDX = ctx.enter_context(nc.sbuf_tensor("row_index", [128, YRING], I32))
        FLAG = ctx.enter_context(nc.sbuf_tensor("overflow", [128, 1], I32))
        ROWS = shaped(REGION[:, 0:16384], 2, TOPK, D)
        SKIP = 4096

        @contextmanager
        def overflow(e):
            e.wait_ge(sem("flag"), 1)
            more = e.value_load(FLAG[0:1, 0:1], min_val=0, max_val=1)
            with e.If(more > 0):
                yield

        LNB = shaped(REGION[:, mixer_base:mixer_base + 2 * D], 2, D)
        BN = shaped(REGION[:, mixer_base + 2 * D:mixer_base + 2 * D + 36], 3, 2, 6)
        MV = shaped(REGION[:, mixer_base + 2 * D + 36:mixer_base + 2 * D + 42], 3, 2)
        RS = REGION[:, mixer_base + 2 * D + 42:mixer_base + 2 * D + 45]
        MIX = REGION[:, mixer_base:]

        block = ctx.enter_context(nc.Block())
        ENG = 4

        def meet(e, k):
            e.drain().then_inc(sem("phase_over"), 1)
            e.wait_ge(sem("phase_over"), ENG * k)

        @block.sync
        def _(sp):
            sp.dma_start(H0[:, :, :], io['x'].rearrange("t p d -> p t d")).then_inc(sem("consts_in"), 16)
            sp.dma_start(CON[:, :], io['consts']).then_inc(sem("consts_in"), 16)
            for k in range(2):
                sp.dma_start(LNB[:, k, :], io['lnv'][k:k + 1, :].to_broadcast([128, D])).then_inc(sem("ln_in"), 16)
            sp.dma_start(VEC[:, :], io['vecs']).then_inc(sem("consts_in"), 16)
            sp.dma_start(HISTS[:, :, :, :], io['hist']).then_inc(sem("consts_in"), 16)
            sw = io['small_w']
            for k, t in enumerate((W2P, A2P, G2)):
                sp.dma_start(t, sw[:, k * D:k * D + D]).then_inc(sem("small_w_in"), 16)

            def weights(m, i, first=False):
                n = m * RING + i
                if not first:
                    sp.wait_ge(sem("tile_done"), n - RING + 1)
                sp.dma_start(WR[:, i, :, :], io['w_in'][n, :, :, :]).then_inc(sem(f"weights_in{i}"), 16)

            for i in range(RING):
                weights(0, i, first=True)
            with sp.Fori(1, PRE // RING) as m:
                for i in range(RING):
                    weights(m, i)

            for i in range(RING):
                sp.wait_ge(sem(f"store_done{i}"), 16 * (PRE // RING + 1))

            def rwkv(c):
                sp.wait_ge(sem("rw_ur_free"), c + 1)
                sp.dma_start(UR, ut[0:26, :, c, 2:CW].rearrange("t p w -> p t w")).then_inc(sem("rw_ur_in"), 16)
                for f in range(FILL):
                    weights(c * 2 + (PRE // RING + f // RING), f % RING)

            def rwkv_out(s):
                sp.wait_ge(sem("rw_state"), NPC * (s + 1) + 1 if s == 0 else NCH + 1)
                sp.dma_start(io['out_rwkv'][s], SS).then_inc(sem("state_out"), 16)
                sp.wait_ge(sem("last_rows"), 1 + s)
                sp.dma_start(io['out_shift'][s], SHO).then_inc(sem("last_rows_out"), 16)
                sp.wait_ge(sem("last_rows_out"), 0 + 16 * (s + 1))
                sp.wait_ge(sem("state_out"), 0 + 16 * (s + 1))

            with sp.Fori(0, NPC) as c:
                rwkv(c)
            rwkv_out(0)
            sp.dma_start(SS, io['st_rwkv']).then_inc(sem("state_in"), 16)
            rwkv(NPC)
            rwkv_out(1)
            for i in range(RING):
                sp.wait_ge(sem(f"store_done{i}"), 16 * ((PRE + NCH * FILL) // RING + 1))

            def ssm(c):
                sp.wait_ge(sem("rows_free"), c + 1)
                sp.wait_ge(sem("ss_free_pool"), c + 1)
                sp.dma_start(UM, ut[T_MISC, :, c, HIST:CW]).then_inc(sem("rows_in"), 16)
                sp.dma_start(UX, ut[T_XBC:T_XBC + 24, :, c, :].rearrange("t p w -> p t w")).then_inc(sem("rows_in"), 16)
                sp.wait_ge(sem("ss_z_free"), c + 1)
                sp.dma_start(UZ, ut[T_Z:T_Z + 16, :, c, HIST:CW].rearrange("t p w -> p t w")).then_inc(sem("ss_z_in"), 16)
                for f in range(FILL):
                    weights(c * 2 + (PRE // RING + NCH * FILL // RING + f // RING), f % RING)

            def ssm_out(s):
                sp.wait_ge(sem("ss_state"), (NPC if s == 0 else NCH) + 1)
                sp.dma_start(io['out_ssm'][s], SN).then_inc(sem("state_out"), 16)
                sp.wait_ge(sem("last_rows"), 3 + s)
                sp.dma_start(io['out_conv'][s], CVO).then_inc(sem("last_rows_out"), 16)
                sp.wait_ge(sem("state_out"), 32 + 16 * (s + 1))
                sp.wait_ge(sem("last_rows_out"), 32 + 16 * (s + 1))

            with sp.Fori(0, NPC) as c:
                ssm(c)
            ssm_out(0)
            sp.dma_start(SN, io['st_ssm']).then_inc(sem("state_in"), 16)
            ssm(NPC)
            ssm_out(1)
            for n in range(NT - PB, NT):
                weights(n // RING, n % RING)

            sp.wait_ge(sem("phase_over"), ENG * 3)
            sp.dma_start(WA2, io['small_w'][:, 3 * D:3 * D + 512]).then_inc(sem("small_w_in"), 16)
            for i in range(RING):
                sp.wait_ge(sem(f"store_done{i}"), 16 * ((NT + RING - 1 - i) // RING + 1))

            def gla(c):
                sp.wait_ge(sem("rows_free"), c + (NCH + 2))
                sp.dma_start(UA, ut[T_MISC, :, c, HIST:CW]).then_inc(sem("rows_in"), 16)
                sp.dma_start(UG, ut[T_GLA:T_GLA + 24, :, c, HIST:CW].rearrange("t p w -> p t w")).then_inc(sem("rows_in"), 16)

            def gla_out(s):
                sp.wait_ge(sem("gl_state"), (NPC if s == 0 else NCH) + 1)
                sp.dma_start(io['out_gla'][s], SG).then_inc(sem("state_out"), 16)
                sp.wait_ge(sem("state_out"), 64 + 16 * (s + 1))

            with sp.Fori(0, NPC) as c:
                gla(c)
            gla_out(0)
            sp.dma_start(SG, io['st_gla']).then_inc(sem("state_in"), 16)
            gla(NPC)
            gla_out(1)

            sp.wait_ge(sem("phase_over"), ENG * 4)
            for c in range(NCH):
                sp.dma_start(GT[:, :, c, :], ut[T_GATE:T_GATE + 24, :, c, HIST:CW].rearrange("t p w -> p t w")
                             ).then_inc(sem("gates_in"), 16)
            for q in range(4):
                sp.dma_start(WR[:, q, :, :], io['wo'][0, q, :, :, :]).then_inc(sem(f"weights_in{q}"), 16)
            sp.dma_start(WOUT, io['w_out']).then_inc(sem("w_out_in"), 16)
            with sp.Fori(1, 8) as d:
                for q in range(4):
                    sp.wait_ge(sem("tile_done"), d * 4 + (NT - 3 + q))
                    sp.dma_start(WR[:, q, :, :], io['wo'][d, q, :, :, :]).then_inc(sem(f"weights_in{q}"), 16)
            for k in range(2):
                sp.dma_start(LN1[:, k, :], io['lnv'][2 + k:3 + k, :].to_broadcast([128, D])).then_inc(sem("ln_in"), 16)

            sp.wait_ge(sem("phase_over"), ENG * 5)
            sp.dma_start(WRT, io['w_router']).then_inc(sem("router_in"), 16)
            sp.dma_start(RB, io['router_bias'].to_broadcast([128, NE])).then_inc(sem("router_in"), 16)
            for k in range(2):
                sp.dma_start(LN2[:, k, :], io['lnv'][4 + k:5 + k, :].to_broadcast([128, D])).then_inc(sem("ln_in"), 16)
            sp.dma_start(MW[:, 3, :], io['moe_w'][NE, :, :]).then_inc(sem("shared_in"), 16)

            def expert_weights(e, s):
                sp.dma_start(MW[:, s, :], io['moe_w'][e, :, :]).then_inc(sem(f"expert_in{s}"), 16)

            for s in range(3):
                expert_weights(s, s)
            sp.wait_ge(sem("shared_used"), 1)
            expert_weights(3, 3)
            with sp.Fori(1, NE // MRING) as m:
                for s in range(MRING):
                    sp.wait_ge(sem("expert_done"), m * MRING + (s - MRING + 1))
                    expert_weights(m * MRING + s, s)
            sp.wait_ge(sem("expert_done"), NE)
            with overflow(sp):
                with sp.Fori(0, NE) as e:
                    sp.wait_ge(sem("expert_done"), e * (NBLK - 1) + NE)
                    expert_weights(e, 0)
            sp.wait_ge(sem("rows_over"), 1)
            for t in range(TT3):
                w = 128 if t < 2 else 64
                sp.dma_start(ROWS[0:w, t % 2, :, :], slots[t * 1024:t * 1024 + w * 8, :].rearrange("(p k) d -> p k d", k=8)
                             ).then_inc(sem(f"slots_in{t % 2}"), 16)
                if t == 1:
                    sp.wait_ge(sem("rows_summed"), 1)
            for t in range(TT3):
                sp.wait_ge(sem("y_ready"), t + 1)
                w = 128 if t < 2 else 64
                sp.dma_start(io['out_y'][t, 0:w], ACC[0:w, t, :]).then_inc(sem("y_out"), 16)
            sp.wait_ge(sem("y_out"), 16 * TT3)

        @block.tensor
        def _(pe):
            mm = nc.tensor.matmul

            def project(m, i):
                n = m * RING + i
                pe.wait_ge(sem(f"weights_in{i}"), (m + 1) * 16)
                pe.wait_ge(sem("tile_moved"), n + 1)
                for k in range(KT):
                    last = mm(PS[:, 6 + i % 2, 0:NTOK], WR[:, i, k, :], H0T[:, k, :], start=(k == 0), stop=(k == KT - 1))
                last.then_inc(sem("tile_done"), 1)

            pe.wait_ge(sem("consts_in"), 64)
            for t in range(TT3):
                w = 128 if t < 2 else 64
                pe.wait_ge(sem("h0_ready"), t + 1)
                for k in range(KT):
                    last = mm(PS[:, 2 * t + k // 4, (k % 4) * 128:(k % 4) * 128 + w], H0[:, t, k * 128:k * 128 + 128],
                              ID[:, 0:w], start=True, stop=True)
                last.then_inc(sem("h0_turned"), 1)
            pe.wait_ge(sem("h0T_ready"), TT3)
            with pe.Fori(0, PRE // RING) as m:
                for i in range(RING):
                    project(m, i)
            meet(pe, 1)
            pe.wait_ge(sem("small_w_in"), 48)

            def pairs(out, lhs, rhs, **kw):
                for j in range(8):
                    last = mm(out(j), lhs(j), rhs(j), **kw)
                return last

            full = dict(start=True, stop=True)

            def rwkv(c):
                def fill(f):
                    project(c * 2 + (PRE // RING + f // RING), f % RING)

                one, b = c + 1, [bank(k, 8, L) for k in range(6)]
                pe.wait_ge(sem("rw_low"), one)
                pairs(lambda j: b[0][:, j], lambda j: W2P[:, j * 128:j * 128 + 128], lambda j: LOW, **full)
                pairs(lambda j: b[1][:, j], lambda j: A2P[:, j * 128:j * 128 + 128], lambda j: LOW,
                      **full).then_inc(sem("rw_pre"), 1)
                pe.wait_ge(sem("rw_sq"), one)
                mm(bank(2), BLK, SQ.rearrange("p a b -> p (a b)"), **full).then_inc(sem("rw_ss"), 1)
                pe.wait_ge(sem("rw_vbd"), one)
                pairs(lambda j: b[5][:, j], lambda j: VBD[:, j], lambda j: E, **full).then_inc(sem("rw_vtok"), 1)
                fill(0)
                pe.wait_ge(sem("rw_bq"), one)
                mm(bank(3), BLK, BQ.rearrange("p a b -> p (a b)"), **full).then_inc(sem("rw_bonus"), 1)
                fill(1)
                pe.wait_ge(sem("rw_ops"), one)
                for o, lhs in ((0, BBD), (2, KBD)):
                    w = banks(o, 2, 8, 2, L)
                    pairs(lambda j: w[:, j], lambda j: lhs[:, j], lambda j: AR[:, j], **full).then_inc(sem("rw_scores"), 1)
                fill(2)
                pe.wait_ge(sem("rw_ptbd"), one)
                pairs(lambda j: b[4][:, j], lambda j: PTBD[:, j], lambda j: E, **full).then_inc(sem("rw_p0"), 1)
                pe.wait_ge(sem("rw_masked"), c * 2 + 2)
                pairs(lambda j: b[2][:, j], lambda j: BBD[:, j], lambda j: E, **full)
                pairs(lambda j: b[3][:, j], lambda j: KBD[:, j], lambda j: E, **full).then_inc(sem("rw_bktok"), 1)
                fill(3)
                for r in range(6):
                    pe.wait_ge(sem("rw_lv"), c * 6 + (r + 1))
                    if r < 5:
                        pe.wait_ge(sem("rw_lva"), c * 5 + (r + 1))
                        pairs(lambda j: b[4][:, j], lambda j: PTBD[:, j], lambda j: PSK[:, j], **full)
                    if r < 4:
                        pairs(lambda j: b[0][:, j], lambda j: PBD[:, j], lambda j: PTT[:, j, 0], **full)
                    if r:
                        pairs(lambda j: b[1][:, j], lambda j: PBD[:, j], lambda j: PTT[:, j, 1], **full)
                    pe.drain().then_inc(sem("rw_round"), 1)
                    if r < 3:
                        fill(4 + r)
                pe.wait_ge(sem("rw_sbd"), one)
                for j in range(8):
                    mm(b[5][:, j], AKBD[:, j], VS[:, j], start=True, stop=False)
                    last = mm(b[5][:, j], ABD[:, j], SS[:, j], start=False, stop=True)
                last.then_inc(sem("rw_x"), 1)
                pe.wait_ge(sem("rw_xs"), one)
                pairs(lambda j: b[4][:, j], lambda j: PTBD[:, j], lambda j: XS[:, j], **full).then_inc(sem("rw_sa"), 1)
                fill(7)
                pe.wait_ge(sem("rw_sas"), one)
                for j in range(8):
                    mm(b[2][:, j], BBD[:, j], SAS[:, j], start=True, stop=False)
                    last = mm(b[2][:, j], KBD[:, j], VS[:, j], start=False, stop=True)
                last.then_inc(sem("rw_st"), 1)
                pe.wait_ge(sem("rw_sabd"), one)
                for j in range(8):
                    mm(b[0][:, j], SBD[:, j], AR[:, j, 1], start=True, stop=False)
                    mm(b[0][:, j], VBD[:, j], SK[:, j, 1], start=False, stop=False)
                    last = mm(b[0][:, j], SABD[:, j], SB[:, j, 1], start=False, stop=True)
                last.then_inc(sem("rw_y"), 1)
                pairs(lambda j: b[5][:, j], lambda j: G2[:, j * 128:j * 128 + 128], lambda j: GS,
                      **full).then_inc(sem("rw_gate"), 1)
                pe.wait_ge(sem("rw_ys"), one)
                mm(bank(3), BLK, YS.rearrange("p a b -> p (a b)"), **full).then_inc(sem("rw_mean"), 1)
                pe.wait_ge(sem("rw_ysq"), one)
                mm(bank(4), BLK, SQ.rearrange("p a b -> p (a b)"), **full).then_inc(sem("rw_var"), 1)

            with pe.Fori(0, NPC) as c:
                rwkv(c)
            rwkv(NPC)
            meet(pe, 2)
            def ssm(c):
                def fill(f):
                    project(c * 2 + (PRE // RING + NCH * FILL // RING + f // RING), f % RING)

                one = c + 1
                pe.wait_ge(sem("ss_ac"), one)
                mm(PS[:, 2, 0:32], DT2, SEL, **full)
                mm(PS[:, 2, 32:64], AC2, SEL, **full)
                mm(PS[:, 2, 64:96], ONE, SELL, **full)
                for k in range(2):
                    last = mm(bank(3 + k, 8, L), LH, RD[:, 8 * k:8 * k + 8, :], **full)
                last.then_inc(sem("ss_bc"), 1)
                fill(0)
                pe.wait_ge(sem("ss_xs"), one)
                w = banks(0, 2, 16, L)
                for j in range(16):
                    last = mm(w[:, j], XTBD[:, j], E, **full)
                last.then_inc(sem("ss_xtok"), 1)
                fill(1)
                pe.wait_ge(sem("ss_bcs"), one + 1)
                w = bank(5, 4, L, n=256)
                for g in range(4):
                    last = mm(w[:, g], BT2[:, g], CT[:, g], **full)
                pe.wait_ge(sem("ss_seg"), one)
                w = bank(2, 4, 128)
                for g in range(4):
                    last = mm(w[:, g], BT2[:, g], ID, **full)
                last.then_inc(sem("ss_cb"), 1)
                fill(2)
                fill(3)
                pe.wait_ge(sem("decays"), one)
                pe.wait_ge(sem("ss_state"), one)
                if c is NPC:
                    pe.wait_ge(sem("state_in"), 32)
                w = banks(3, 2, 16, L)
                for j in range(16):
                    last = mm(w[:, j], SN[:, j * 128:j * 128 + 128], CT[:, j // 4], **full)
                pe.wait_ge(sem("ss_mt"), one)
                w = banks(0, 2, 16, L)
                for j in range(16):
                    last = mm(w[:, j], XDBD[:, j], SEG[:, j], **full)
                last.then_inc(sem("mixed"), 1)
                fill(4)
                pe.wait_ge(sem("ss_yr"), one)
                pe.wait_ge(sem("ss_btm"), one)
                w = banks(0, 4, 16, 128)
                for j in range(16):
                    last = mm(w[:, j], BTM[:, j // 4], XEBD[:, j], **full)
                last.then_inc(sem("state_sums"), 1)
                fill(5)
                pe.wait_ge(sem("squares"), one)
                w = bank(5, 4, L, n=256)
                for k in range(4):
                    last = mm(w, ONE, YO.rearrange("p (g i) b -> p g i b", i=4)[:, :, k, :], start=(k == 0), stop=(k == 3))
                last.then_inc(sem("square_sums"), 1)
                fill(6)
                fill(7)

            with pe.Fori(0, NPC) as c:
                ssm(c)
            ssm(NPC)
            for n in range(NT - PB, NT):
                project(n // RING, n % RING)
            meet(pe, 3)

            def gla(c):
                one = c + 1
                if c is NPC:
                    pe.wait_ge(sem("state_in"), 48)
                pe.wait_ge(sem("rows_in"), one * 32 + 32 * NCH)
                pe.wait_ge(sem("gl_state"), one)
                for j in range(4):
                    last = mm(bank(0, 4, L, n=256)[:, j], WA2[:, j * 128:j * 128 + 128], UA, **full)
                last.then_inc(sem("gl_pre"), 1)
                w = banks(1, 2, 8, 128)
                for j in range(8):
                    last = mm(w[0:64, j], UG[:, 8 + j], ID, **full)
                last.then_inc(sem("gl_v"), 1)
                pe.wait_ge(sem("gl_ops"), one)
                for h in range(4):
                    last = mm(bank(0, 4, L, n=256)[0:64, h], KI[:, h], QD[:, h], **full)
                for h in range(4):
                    last = mm(bank(3, 4, 128)[0:64, h], KE[:, h], ID, **full)
                last.then_inc(sem("gl_sc"), 1)
                pe.wait_ge(sem("gl_scm"), one)
                pe.wait_ge(sem("gl_vt"), one)
                for j in range(8):
                    mm(bank(4, 8, L)[:, j], VT[:, j], SCT[:, j // 2], start=True, stop=False)
                    last = mm(bank(4, 8, L)[:, j], SG[:, j // 2, (j % 2) * 128:(j % 2) * 128 + 128], QD[:, j // 2],
                              start=False, stop=True)
                last.then_inc(sem("mixed"), 1)
                w = banks(1, 2, 4, 256)
                for h in range(4):
                    last = mm(w[:, h], KET[:, h], VT[:, 2 * h:2 * h + 2], **full)
                last.then_inc(sem("state_sums"), 1)
                pe.wait_ge(sem("squares"), NCH + one)
                for k in range(2):
                    last = mm(bank(5, 4, L, n=256), ONE, SQO.rearrange("p (g i) b -> p g i b", i=2)[:, :, k, :],
                              start=(k == 0), stop=(k == 1))
                last.then_inc(sem("square_sums"), 1)

            pe.wait_ge(sem("small_w_in"), 64)
            with pe.Fori(0, NPC) as c:
                gla(c)
            gla(NPC)
            meet(pe, 4)

            def outproj(d, p):
                pe.wait_ge(sem("wo_free"), d + 1)
                for q, (b, k0) in enumerate(((0, 0), (1, 8), (2, 16), (2, 24))):
                    pe.wait_ge(sem(f"weights_in{q}"), d * 16 + 16 * ((NT + RING - 1 - q) // RING + 1))
                    for k in range(KT):
                        last = mm(PS[:, 3 * p + b, 0:NTOK], WR[:, q, k, :], OT[:, k0 + k, :],
                                  start=(k == 0 and q < 3), stop=(k == KT - 1 and q != 2))
                    last.then_inc(sem("tile_done"), 1)

            with pe.Fori(0, 4) as d2:
                for p in range(2):
                    outproj(d2 * 2 + p, p)
            pe.wait_ge(sem("merged"), 8)
            pe.wait_ge(sem("w_out_in"), 16)
            for t in range(TT3):
                w = 128 if t < 2 else 64
                for h in range(2):
                    for k in range(KT):
                        last = mm(PS[0:w, 2 * t + h, :], MG[:, k, t * 128:t * 128 + w], WOUT[:, k, h * 512:h * 512 + 512],
                                  start=(k == 0), stop=(k == KT - 1))
                last.then_inc(sem("w_out_done"), 1)
            for t in range(TT3):
                w = 128 if t < 2 else 64
                pe.wait_ge(sem("h1_ready"), t + 1)
                for k in range(KT):
                    last = mm(PS[:, 2 * t + k // 4, (k % 4) * 128:(k % 4) * 128 + w], H0[:, t, k * 128:k * 128 + 128],
                              ID[:, 0:w], **full)
                last.then_inc(sem("h1_turned"), 1)
            meet(pe, 5)

            pe.wait_ge(sem("router_in"), 32)
            for t in range(TT3):
                w = 128 if t < 2 else 64
                for k in range(KT):
                    last = mm(PS[0:w, t, 0:NE], H0T[:, k, t * 128:t * 128 + w], WRT[:, k, :], start=(k == 0), stop=(k == KT - 1))
            last.then_inc(sem("logits"), 1)
            pe.wait_ge(sem("shared_in"), 16)
            w13 = shaped(MW[:, 3, 0:4096], KT, 512)
            for f in range(4):
                for k in range(KT):
                    last = mm(PS[:, 4 + f, 0:NTOK], w13[:, k, f * 128:f * 128 + 128], H0T[:, k, :],
                              start=(k == 0), stop=(k == KT - 1))
            last.then_inc(sem("shared_hid"), 1)
            pe.wait_ge(sem("chosen"), 1)
            for t in range(TT3):
                for u in range(t + 1):
                    last = mm(PS[:, 3, t * NE:t * NE + NE], TRI if u == t else ONE, CHO[:, u, :], start=(u == 0), stop=(u == t))
            for u in range(TT3):
                last = mm(PS[:, 3, 192:192 + NE], ONE, CHO[:, u, :], start=(u == 0), stop=(u == TT3 - 1))
            last.then_inc(sem("places"), 1)
            pe.wait_ge(sem("shared_act"), 1)
            w2 = shaped(MW[:, 3, 4096:6144], 2, D)
            for t in range(TT3):
                w = 128 if t < 2 else 64
                pe.wait_ge(sem("shared_free"), t + 1)
                for h in range(2):
                    for f in range(2):
                        last = mm(PS[0:w, 4 + 2 * (t % 2) + h, :], SHID[:, f, t * 128:t * 128 + w],
                                  w2[:, f, h * 512:h * 512 + 512], start=(f == 0), stop=(f == 1))
                last.then_inc(sem("shared_out"), 1)
            pe.drain().then_inc(sem("shared_used"), 1)
            pe.wait_ge(sem("shared_free"), TT3 + 2)

            def gather(n, p):
                pe.wait_ge(sem("onehot"), n + 1)
                pe.wait_ge(sem("x_moved"), n + 1)
                for k in range(KT):
                    for t in range(TT3):
                        last = mm(bank(p, KT, CAP)[:, k], H0[:, t, k * 128:k * 128 + 128], OH[:, p, t, :],
                                  start=(t == 0), stop=(t == TT3 - 1))
                last.then_inc(sem("x_done"), 1)

            def hidden(n, e, p, s, loads):
                pe.wait_ge(sem("hid_moved"), n + 1)
                pe.wait_ge(sem("x_moved"), n + 3)
                pe.wait_ge(sem(f"expert_in{s}"), loads * 16)
                w13 = shaped(MW[:, s, 0:4096], KT, 512)
                for f in range(4):
                    for k in range(KT):
                        last = mm(bank(2 + p, 8, CAP)[:, f], w13[:, k, f * 128:f * 128 + 128], XE[:, p, k, :],
                                  start=(k == 0), stop=(k == KT - 1))
                for t in range(TT3):
                    last = mm(PS[0:CAP, 2 + p, 256:258], OH[:, p, t, :], INFO[:, t, e, :], start=(t == 0), stop=(t == TT3 - 1))
                last.then_inc(sem("hid_done"), 1)

            def down(n, p, s):
                pe.wait_ge(sem("hid_ready"), n + 1)
                pe.wait_ge(sem("y_left"), n + 1)
                pe.wait_ge(sem("y_right"), n + 1)
                w2 = shaped(MW[:, s, 4096:6144], 2, D)
                for h in range(2):
                    for f in range(2):
                        last = mm(PS[0:CAP, 4 + 2 * p + h, :], HID[:, p, f, :], w2[:, f, h * 512:h * 512 + 512],
                                  start=(f == 0), stop=(f == 1))
                last.then_inc(sem("expert_done"), 1)

            gather(0, 0)
            gather(1, 1)
            hidden(0, 0, 0, 0, 1)

            def steady(m, i):
                e = m * MRING + i
                gather(e + 1, (i + 1) % 2)
                hidden(e, e, i % 2, i % MRING, m + (i // MRING + 1))
                down(m * MRING + (i - 1), (i - 1) % 2, (i - 1) % MRING)

            with pe.Fori(0, NE // MRING - 1) as m:
                for i in range(1, MRING + 1):
                    steady(m, i)
            for e in range(NE - 3, NE - 1):
                steady(e // MRING, e % MRING)
            hidden(NE - 1, NE - 1, 1, 3, NE // MRING)
            down(NE - 2, 0, 2)
            down(NE - 1, 1, 3)
            with overflow(pe):
                with pe.Fori(0, NE) as e:
                    for b in range(NBLK - 1):
                        n = e * (NBLK - 1) + (NE + b)
                        gather(n, b % 2)
                        hidden(n, e, b % 2, 0, e + (NE // MRING + 1))
                        down(n, b % 2, 0)

        @block.scalar
        def _(act):
            def a_(out, in_, f, **kw):
                return nc.scalar.activation(out, in_, f, **kw)

            def root(x, asked, n, done):
                act.wait_ge(sem(asked), n)
                a_(x, x, ACT.Sqrt)
                act.drain().then_inc(sem(done), 1)

            for t in range(TT3):
                w = 128 if t < 2 else 64
                root(RS[:, t:t + 1], "ln_var", t + 1, "ln_rstd")
                act.wait_ge(sem("h0_turned"), t + 1)
                src = banks(2 * t, 2, KT, 128)
                a_(H0T[:, :, t * 128:t * 128 + w], src[:, :, 0:w], ACT.Copy).then_inc(sem("h0T_ready"), 1)
            act.wait_ge(sem("consts_in"), 64)
            act.wait_ge(sem("stage_zero"), 1)
            for i in range(RING):
                nc.scalar.sem_inc(sem(f"store_done{i}"), 16)
            nc.scalar.sem_inc(sem("tile_moved"), 2)

            def move(m, i):
                n = m * RING + i
                act.wait_ge(sem("tile_done"), n + 1)
                act.wait_ge(sem(f"store_done{i}"), (m + 1) * 16)
                src = bank(6 + i % 2, NCH, L, n=NTOK)
                a_(STG[:, i, 1:NPC, 0:HIST], src[:, 0:NPC - 1, L - HIST:L], ACT.Copy)
                a_(STG[:, i, 0:NCH:NPC, 0:HIST], HISTS[:, n, :, :], ACT.Copy)
                a_(STG[:, i, :, HIST:CW], src, ACT.Copy)
                act.drain().then_inc(sem("tile_moved"), 1)
                act.wait_ge(sem("tile_moved"), n + 3)
                act.dma_start(ut[n, :, :, :], STG[:, i, :, :]).then_inc(sem(f"store_done{i}"), 16)

            with act.Fori(0, PRE // RING) as m:
                for i in range(RING):
                    move(m, i)
            meet(act, 1)

            def diag(out, src, func=ACT.Copy):
                for h in range(2):
                    last = a_(half(out, h), src[64 * h:64 * h + 64, :, :], func)
                return last

            def rwkv(c):
                def fill(f):
                    move(c * 2 + (PRE // RING + f // RING), f % RING)

                one, b = c + 1, [bank(k, 8, L) for k in range(6)]
                act.wait_ge(sem("rw_us"), one)
                a_(LOW[0:64, :], US[0:64, 24, :], ACT.Tanh)
                a_(LOW[64:128, :], US[64:128, 24, :], ACT.Copy)
                a_(GS, US[:, 25, :], ACT.Sigmoid)
                act.drain().then_inc(sem("rw_low"), 1)
                diag(VBD, US[:, 16:24, :])
                act.drain().then_inc(sem("rw_vbd"), 1)
                root(TA, "rw_ssc", one, "rw_rn")
                act.wait_ge(sem("rw_wa"), one)
                a_(WS, WS, ACT.Sigmoid)
                a_(AS, AS, ACT.Sigmoid)
                act.drain().then_inc(sem("rw_sig"), 1)
                act.wait_ge(sem("rw_vtok"), one)
                a_(VS, b[5], ACT.Copy)
                diag(VBD, b[5])
                fill(0)
                act.wait_ge(sem("rw_cs"), one)
                a_(G, CS, ACT.Exp, scale=-DECAY)
                a_(GI, CS, ACT.Exp, scale=DECAY)
                a_(GP, GP, ACT.Exp, scale=-DECAY)
                act.drain().then_inc(sem("rw_exp"), 1)
                act.wait_ge(sem("rw_ar"), one)
                diag(ABD, AR[:, :, 0, :])
                fill(1)
                act.wait_ge(sem("rw_masked"), c * 2 + 1)
                diag(PTBD, SB[:, :, 0, :])
                act.drain().then_inc(sem("rw_ptbd"), 1)
                act.drain().then_inc(sem("rw_lva"), 1)
                fill(2)
                act.wait_ge(sem("rw_masked"), c * 2 + 2)
                diag(AKBD, SK[:, :, 0, :])
                act.wait_ge(sem("rw_bktok"), one)
                diag(BBD, b[2])
                diag(KBD, b[3])
                act.drain()
                fill(3)
                act.wait_ge(sem("rw_state"), one)
                if c is NPC:
                    act.wait_ge(sem("state_in"), 16)
                diag(SBD, SS)
                act.drain().then_inc(sem("rw_sbd"), 1)
                for r in range(4):
                    act.wait_ge(sem("rw_round"), c * 6 + (r + 1))
                    diag(PTBD, b[0])
                    a_(PTT[:, :, 0, :], b[0], ACT.Copy)
                    act.drain().then_inc(sem("rw_lva"), 1)
                    if r < 3:
                        fill(4 + r)
                act.wait_ge(sem("rw_sas"), one)
                diag(SABD, SAS)
                act.drain().then_inc(sem("rw_sabd"), 1)
                fill(7)
                root(TA, "rw_varc", one, "rw_rstd")

            with act.Fori(0, NPC) as c:
                rwkv(c)
            rwkv(NPC)
            meet(act, 2)
            a_(NA, VEC[:, V_ALOG:V_ALOG + 1], ACT.Exp)
            act.drain().then_inc(sem("gates_ready"), 1)
            nc.scalar.sem_inc(sem("ss_bcs"), 1)

            def ssm(c):
                def fill(f):
                    move(c * 2 + (PRE // RING + NCH * FILL // RING + f // RING), f % RING)

                one = c + 1
                act.wait_ge(sem("softplus_in"), one)
                a_(LB, AB, ACT.Exp, scale=-1.0)
                act.drain()
                a_(LB, LB, ACT.Ln, bias=1.0)
                act.drain().then_inc(sem("softplus_out"), 1)
                act.wait_ge(sem("ss_cx"), one)
                a_(XS_, XC[:, 0:16], ACT.Silu)
                diag(XTBD, XC[:, 0:16], ACT.Silu)
                act.drain().then_inc(sem("ss_xs"), 1)
                act.wait_ge(sem("ss_cbc"), one)
                for k in range(2):
                    a_(BT2[:, :, k, :], XC[:, 16:20], ACT.Silu)
                a_(CT, XC[:, 20:24], ACT.Silu)
                act.drain().then_inc(sem("ss_bcs"), 1)
                fill(0)
                act.wait_ge(sem("ss_z_in"), one * 16)
                a_(UZ, UZ, ACT.Silu)
                act.drain().then_inc(sem("ss_z"), 1)
                fill(1)
                act.wait_ge(sem("ss_seg"), one)
                a_(EBC, banks(3, 2, 16, L), ACT.Exp)
                a_(SEG, SEG, ACT.Exp)
                a_(EL, EL, ACT.Exp)
                a_(ALS, ALS, ACT.Exp)
                act.drain().then_inc(sem("decays"), 1)
                fill(2)
                act.wait_ge(sem("ss_cb"), one)
                a_(BTM, bank(2, 4, 128), ACT.Copy)
                act.drain().then_inc(sem("ss_btm"), 1)
                fill(3)
                fill(4)
                act.wait_ge(sem("ss_yz"), one)
                a_(YO, YC, ACT.Square)
                act.drain().then_inc(sem("squares"), 1)
                fill(5)
                root(RG, "variance", one, "rstd")
                fill(6)
                fill(7)

            with act.Fori(0, NPC) as c:
                ssm(c)
            ssm(NPC)
            for n in range(NT - PB, NT):
                move(n // RING, n % RING)
            meet(act, 3)
            act.wait_ge(sem("zeroed"), 2)

            def gla(c):
                one = c + 1
                act.wait_ge(sem("rows_in"), one * 32 + 32 * NCH)
                act.wait_ge(sem("gl_out"), one)
                a_(RR, UG[:, 16:24, :], ACT.Silu)
                act.wait_ge(sem("gl_v"), one)
                a_(VT[0:64], banks(1, 2, 8, 128)[0:64], ACT.Copy)
                act.drain().then_inc(sem("gl_vt"), 1)
                act.wait_ge(sem("softplus_in"), NCH + one)
                a_(LB4, AB4, ACT.Exp, scale=-1.0)
                act.drain()
                a_(LB4, LB4, ACT.Ln, bias=1.0)
                act.drain().then_inc(sem("softplus_out"), 1)
                act.wait_ge(sem("gl_cs"), one)
                a_(EG, CS4, ACT.Exp, scale=1.0 / 16)
                a_(EI, CS4, ACT.Exp, scale=-1.0 / 16)
                a_(EE, EE, ACT.Exp, scale=1.0 / 16)
                act.drain().then_inc(sem("decays"), 1)
                root(RG4, "variance", NCH + one, "rstd")

            with act.Fori(0, NPC) as c:
                gla(c)
            gla(NPC)
            meet(act, 4)

            act.wait_ge(sem("gates_in"), 16 * NCH)
            for g in range(3):
                a_(GT[:, 8 * g:8 * g + 8], GT[:, 8 * g:8 * g + 8], ACT.Sigmoid)
            act.drain().then_inc(sem("gates_ready"), 1)
            for t in range(TT3):
                root(RS1[:, t:t + 1], "ln_var", TT3 + t + 1, "ln_rstd")
            for t in range(TT3):
                w = 128 if t < 2 else 64
                act.wait_ge(sem("h1_turned"), t + 1)
                a_(H0T[:, :, t * 128:t * 128 + w], banks(2 * t, 2, KT, 128)[:, :, 0:w], ACT.Copy)
            meet(act, 5)

            act.wait_ge(sem("logits"), 1)
            act.wait_ge(sem("score_room"), 1)
            for t in range(TT3):
                w = 128 if t < 2 else 64
                a_(SCO[0:w, t, :], PS[0:w, t, 0:NE], ACT.Sigmoid)
            act.drain().then_inc(sem("scores"), 1)
            act.wait_ge(sem("shared_hid"), 1)
            a_(SHID, PS[:, 4:6, 0:NTOK], ACT.Silu)
            act.drain().then_inc(sem("shared_silu"), 1)
            nc.scalar.sem_inc(sem("x_moved"), 2)

            def block_steps(n, p):
                act.wait_ge(sem("x_done"), n + 1)
                a_(XE[:, p], bank(p, KT, CAP), ACT.Copy)
                act.drain().then_inc(sem("x_moved"), 1)

            def silu_step(n, p):
                act.wait_ge(sem("hid_done"), n + 1)
                a_(SIL[:, p], bank(2 + p, 8, CAP)[:, 0:2], ACT.Silu)
                act.drain().then_inc(sem("silu_ready"), 1)

            def y_step(n, p, s):
                act.wait_ge(sem("expert_done"), n + 1)
                act.wait_ge(sem("rows_out"), n + 1)
                a_(Y[0:CAP, s, 512:D], PS[0:CAP, 5 + 2 * p, :], ACT.Copy, scale=GA[0:CAP, s:s + 1])
                act.drain().then_inc(sem("y_right"), 1)

            block_steps(0, 0)
            block_steps(1, 1)
            silu_step(0, 0)

            def steady(m, i):
                block_steps(m * MRING + (i + 1), (i + 1) % 2)
                silu_step(m * MRING + i, i % 2)
                y_step(m * MRING + (i - 1), (i - 1) % 2, (i - 1) % YRING)

            with act.Fori(0, NE // MRING - 1) as m:
                for i in range(1, MRING + 1):
                    steady(m, i)
            for e in range(NE - 3, NE - 1):
                steady(e // MRING, e % MRING)
            silu_step(NE - 1, 1)
            y_step(NE - 2, 0, 2)
            y_step(NE - 1, 1, 3)
            with overflow(act):
                with act.Fori(0, NE) as e:
                    for b in range(NBLK - 1):
                        n = e * (NBLK - 1) + (NE + b)
                        block_steps(n, b % 2)
                        silu_step(n, b % 2)
                        y_step(n, b % 2, b % YRING)
            for t in range(TT3):
                w = 128 if t < 2 else 64
                root(RS2[0:w, t:t + 1], "ln_var", 2 * TT3 + t + 1, "ln_rstd")

        @block.vector
        def _(dve):
            def tt(out, a, b, op):
                return dve.tensor_tensor(out, a, b, op)

            def ts(out, a, s1, s2, op0, op1=None):
                return dve.tensor_scalar(out, a, s1, s2, op0, op1) if op1 is not None else \
                    dve.tensor_scalar(out, a, s1, s2, op0)

            def stt(out, a, s, b, op0, op1):
                return dve.scalar_tensor_tensor(out=out, in0=a, scalar=s, in1=b, op0=op0, op1=op1)

            mul, add, sub, mx = ALU.mult, ALU.add, ALU.subtract, ALU.max

            def layer_norm(X, t, g, b, n_ln, BN=BN, MV=MV, RS=RS, w=128, eps=1e-5):
                X, BN, MV, RS, g, b = X[0:w], BN[0:w], MV[0:w], RS[0:w], g[0:w], b[0:w]
                for k in range(2):
                    dve.bn_stats(BN[:, t, k, :], X[:, t, k * 512:k * 512 + 512])
                dve.drain()
                dve.bn_aggr(MV[:, t, :], BN[:, t, :, :].rearrange("p a b -> p (a b)"))
                dve.drain()
                ts(RS[:, t:t + 1], MV[:, t, 1:2], eps, None, add)
                dve.drain()
                dve.reciprocal(RS[:, t:t + 1], RS[:, t:t + 1])
                dve.drain().then_inc(sem("ln_var"), 1)
                dve.wait_ge(sem("ln_rstd"), n_ln)
                ts(X[:, t, :], X[:, t, :], MV[:, t, 0:1], RS[:, t:t + 1], sub, mul)
                dve.drain()
                tt(X[:, t, :], X[:, t, :], g, mul)
                dve.drain()
                tt(X[:, t, :], X[:, t, :], b, add)
                return dve.drain()

            dve.memset(STG, 0.0)
            dve.drain().then_inc(sem("stage_zero"), 1)
            dve.wait_ge(sem("consts_in"), 64)
            dve.wait_ge(sem("ln_in"), 32)
            for t in range(TT3):
                layer_norm(H0, t, LNB[:, 0, :], LNB[:, 1, :], t + 1).then_inc(sem("h0_ready"), 1)
            dve.memset(MIX, 0.0)
            dve.wait_ge(sem("consts_in"), 64)
            dve.drain().then_inc(sem("rw_ur_free"), 1)
            meet(dve, 1)
            nc.vector.sem_inc(sem("rw_state"), 1)
            dve.wait_ge(sem("consts_in"), 64)

            def rwkv(c):
                one, b = c + 1, [bank(k, 8, L) for k in range(6)]
                r, k, v = US[:, 0:8, :], US[:, 8:16, :], US[:, 16:24, :]
                dve.wait_ge(sem("rw_ur_in"), (c + 1) * 16)
                tt(US, UR[:, :, 0:L], UR[:, :, 1:L + 1], sub)
                dve.drain()
                tt(US, US, vec(V_MU, 26, L), mul)
                dve.drain()
                tt(US, US, UR[:, :, 1:L + 1], add)
                if c is NPC:
                    dve.wait_ge(sem("last_rows_out"), 16)
                dve.tensor_copy(SHO, UR[:, :, L])
                dve.drain().then_inc(sem("rw_us"), 1)
                nc.vector.sem_inc(sem("rw_ur_free"), 1)
                tt(KK, k, vec(V_KK, 8, L), mul)
                dve.drain()
                tt(SQ, KK, KK, mul)
                dve.drain().then_inc(sem("rw_sq"), 1)
                dve.wait_ge(sem("rw_ss"), one)
                ts(TA, b[2], 1e-24, None, mx)
                dve.drain()
                dve.reciprocal(TA, TA)
                dve.drain().then_inc(sem("rw_ssc"), 1)
                dve.wait_ge(sem("rw_pre"), one)
                tt(WS, b[0], vec(V_W0, 8, L), add)
                tt(AS, b[1], vec(V_A0, 8, L), add)
                dve.drain().then_inc(sem("rw_wa"), 1)
                dve.wait_ge(sem("rw_rn"), one)
                tt(KK, KK, TA, mul)
                dve.wait_ge(sem("rw_sig"), one)
                dve.tensor_tensor_scan(CS.rearrange("p a b -> p (a b)"), CON[:, C_RST:C_RST + 512],
                                       WS.rearrange("p a b -> p (a b)"), 0.0, mul, add)
                dve.drain()
                tt(GP, CS, WS, sub)
                dve.drain().then_inc(sem("rw_cs"), 1)
                tt(KA, KK, AS, mul)
                stt(TA, AS, -1.0, vec(V_KA, 8, L), add, mul)
                dve.drain()
                stt(K2, TA, 1.0, k, add, mul)
                dve.drain()
                tt(BQ, r, K2, mul)
                dve.drain()
                tt(BQ, BQ, vec(V_RK, 8, L), mul)
                dve.drain().then_inc(sem("rw_bq"), 1)
                dve.wait_ge(sem("rw_exp"), one)
                stt(AR[:, :, 0, :], KK, -1.0, GP, mul, mul)
                tt(AR[:, :, 1, :], r, G, mul)
                dve.drain().then_inc(sem("rw_ar"), 1)
                for h in range(2):
                    q = slice(64 * h, 64 * h + 64)
                    tt(half(BBD, h), KA[q], GI[q], mul)
                    tt(half(KBD, h), K2[q], GI[q], mul)
                dve.wait_ge(sem("rw_bonus"), one)
                tt(BV, b[3], v, mul)
                dve.drain().then_inc(sem("rw_ops"), 1)
                dve.wait_ge(sem("rw_scores"), c * 2 + 1)
                for k2 in range(2):
                    tt(SB[:, 4 * k2:4 * k2 + 4].rearrange("p a b c -> p a (b c)"),
                       bank(k2, 4, 128), over(M2, 4, 0, 128), mul)
                dve.drain().then_inc(sem("rw_masked"), 1)
                dve.wait_ge(sem("rw_scores"), c * 2 + 2)
                for k2 in range(2):
                    tt(SK[:, 4 * k2:4 * k2 + 4].rearrange("p a b c -> p a (b c)"),
                       bank(2 + k2, 4, 128), over(M2, 4, 0, 128), mul)
                dve.drain().then_inc(sem("rw_masked"), 1)
                dve.tensor_copy(PTT[:, :, 0, :], SB[:, :, 0, :])
                tt(PTT[:, :, 1, :], SB[:, :, 0, :], over(E, 8, 0, L), add)
                dve.wait_ge(sem("rw_p0"), one)

                def power():
                    dve.tensor_copy(PSK, b[4])
                    for h in range(2):
                        dve.tensor_copy(half(PBD, h), b[4][64 * h:64 * h + 64])

                power()
                dve.drain().then_inc(sem("rw_lv"), 1)
                for rd in range(5):
                    dve.wait_ge(sem("rw_round"), c * 6 + (rd + 1))
                    if rd:
                        tt(PTT[:, :, 1, :], PTT[:, :, 1, :], b[1], add)
                    power()
                    dve.drain().then_inc(sem("rw_lv"), 1)
                dve.wait_ge(sem("rw_round"), c * 6 + 6)
                for h in range(2):
                    q = slice(64 * h, 64 * h + 64)
                    tt(half(PTBD, h), b[1][q], PTT[q, :, 1, :], add)
                dve.wait_ge(sem("rw_x"), one)
                dve.tensor_copy(XS, b[5])
                dve.drain().then_inc(sem("rw_xs"), 1)
                dve.wait_ge(sem("rw_sa"), one)
                dve.tensor_copy(SAS, b[4])
                dve.drain().then_inc(sem("rw_sas"), 1)
                dve.wait_ge(sem("rw_st"), one)
                tt(SS, SS, b[2], add)
                dve.drain()
                tt(SS, SS, G[:, :, L - 1:L].to_broadcast([128, 8, L]), mul)
                dve.drain().then_inc(sem("rw_state"), 1)
                dve.wait_ge(sem("rw_y"), one)
                dve.tensor_copy(YS, b[0])
                dve.drain().then_inc(sem("rw_ys"), 1)
                dve.wait_ge(sem("rw_mean"), one)
                stt(YS, b[3], -1.0 / 64, YS, mul, add)
                dve.drain()
                tt(SQ, YS, YS, mul)
                dve.drain().then_inc(sem("rw_ysq"), 1)
                dve.wait_ge(sem("rw_var"), one)
                ts(TA, b[4], 1.0 / 64, 64e-5, mul, add)
                dve.drain()
                dve.reciprocal(TA, TA)
                dve.drain().then_inc(sem("rw_varc"), 1)
                dve.wait_ge(sem("rw_rstd"), one)
                tt(YS, YS, TA, mul)
                dve.drain()
                tt(YS, YS, vec(V_LNG, 8, L), mul)
                dve.drain()
                tt(YS, YS, vec(V_LNB, 8, L), add)
                dve.drain()
                tt(YS, YS, BV, add)
                dve.drain()
                dve.wait_ge(sem("rw_gate"), one)
                tt(OT[:, 0:8, bass.ds(c * L, L)], YS, b[5], mul)
                dve.drain()

            with dve.Fori(0, NPC) as c:
                rwkv(c)
            nc.vector.sem_inc(sem("last_rows"), 1)
            dve.wait_ge(sem("state_in"), 16)
            rwkv(NPC)
            nc.vector.sem_inc(sem("last_rows"), 1)
            dve.wait_ge(sem("state_out"), 32)
            meet(dve, 2)
            def neg_exp_a():
                dve.wait_ge(sem("gates_ready"), 1)
                ts(NA, NA, -1.0, None, mul)

            neg_exp_a()
            dve.memset(SN, 0.0)
            dve.drain().then_inc(sem("ss_state"), 1)
            nc.vector.sem_inc(sem("rows_free"), 1)
            nc.vector.sem_inc(sem("ss_z_free"), 1)
            dve.wait_ge(sem("zeroed"), 1)

            def ssm(c):
                one = c + 1
                dve.wait_ge(sem("rows_in"), one * 32)
                ts(T1, UM, VEC[:, V_DTB:V_DTB + 1], None, add)
                dve.drain()
                stt(AB, T1, -1.0, T1, mul, mx)
                dve.drain().then_inc(sem("softplus_in"), 1)
                x = XC[:, 0:16]
                tt(x, UX[:, 0:16, 0:L], vec(V_CW, 16, L), mul)
                for k in range(1, 4):
                    tt(TMP, UX[:, 0:16, k:k + L], vec(V_CW + 24 * k, 16, L), mul)
                    dve.drain()
                    tt(x, x, TMP, add)
                    dve.drain()
                tt(x, x, vec(V_CB, 16, L), add)
                if c is NPC:
                    dve.wait_ge(sem("last_rows_out"), 48)
                dve.tensor_copy(CVO, UX[:, :, L:CW])
                dve.drain().then_inc(sem("ss_cx"), 1)
                dve.wait_ge(sem("softplus_out"), one)
                for k in range(2):
                    stt(DT2[:, k], T1, 0.0, LB, mx, add)
                dve.drain().then_inc(sem("rows_free"), 1)
                ts(T1, DT2[:, 0], NA, None, mul)
                dve.drain()
                dve.tensor_tensor_scan(AC2[:, 0], CON[:, C_RST:C_RST + L], T1, 0.0, mul, add)
                dve.drain()
                dve.tensor_copy(AC2[:, 1], AC2[:, 0])
                ts(SELL, SEL, AC2[:, 0, L - 1:L], None, mul)
                tt(RD, over(AC2[:, 0], 16, 0, L), PM.unsqueeze(2).to_broadcast([128, 16, L]), mul)
                dve.drain().then_inc(sem("ss_ac"), 1)
                dve.wait_ge(sem("ss_bc"), one)
                for h in range(2):
                    q = slice(64 * h, 64 * h + 64)
                    for out, a in ((DTS, 0), (ACS, 32), (ALS, 64)):
                        dve.tensor_copy(out[q], PS[q, 2, a + h:a + 32:2])
                dve.tensor_copy(EL, PS[:, 2, 64:96])
                dve.drain()
                tt(ALS, ALS, ACS, sub)
                tt(SEG, banks(3, 2, 16, L), ACS.unsqueeze(2).to_broadcast([128, 16, L]), sub)
                dve.drain()
                ts(SEG, SEG, 0.0, None, ALU.min)
                dve.drain().then_inc(sem("ss_seg"), 1)
                dve.wait_ge(sem("ss_xtok"), one)
                for h in range(2):
                    q = slice(64 * h, 64 * h + 64)
                    tt(half(XDBD, h), banks(0, 2, 16, L)[q], DTS[q].unsqueeze(2).to_broadcast([64, 16, L]), mul)
                dve.wait_ge(sem("ss_cb"), one)
                tt(CBM, bank(5, 4, L, n=256), over(M2[:, L:2 * L], 4, 0, L), mul)
                dve.drain()
                dve.wait_ge(sem("decays"), one)
                for g in range(4):
                    tt(SEG[:, 4 * g:4 * g + 4], SEG[:, 4 * g:4 * g + 4], over(CBM[:, g], 4, 0, L), mul)
                dve.drain().then_inc(sem("ss_mt"), 1)
                for h in range(2):
                    q = slice(64 * h, 64 * h + 64)
                    tt(half(XEBD, h), half(XDBD, h), ALS[q].unsqueeze(2).to_broadcast([64, 16, L]), mul)
                dve.wait_ge(sem("mixed"), one)
                tt(YO, banks(3, 2, 16, L), EBC, mul)
                dve.drain()
                tt(YC, banks(0, 2, 16, L), YO, add)
                dve.drain().then_inc(sem("ss_yr"), 1)
                dve.wait_ge(sem("ss_xd"), one)
                tt(YC, YC, XD, add)
                dve.drain()
                dve.wait_ge(sem("ss_z"), one)
                tt(YC, YC, UZ, mul)
                dve.drain().then_inc(sem("ss_yz"), 1)
                nc.vector.sem_inc(sem("ss_z_free"), 1)
                sn = SN.rearrange("p (h v) -> p h v", v=64)
                if c is NPC:
                    dve.wait_ge(sem("state_in"), 32)
                tt(sn, sn, EL.unsqueeze(2).to_broadcast([128, 32, 64]), mul)
                dve.drain()
                dve.wait_ge(sem("state_sums"), one)
                tt(SN, SN, banks(0, 4, 2048), add)
                dve.drain().then_inc(sem("ss_state"), 1)
                dve.wait_ge(sem("square_sums"), one)
                ts(RG, bank(5, 4, L, n=256), 1.0 / 512, 1e-5, mul, add)
                dve.drain()
                dve.reciprocal(RG, RG)
                dve.drain().then_inc(sem("variance"), 1)
                dve.wait_ge(sem("rstd"), one)
                for g in range(4):
                    tt(YC[:, 4 * g:4 * g + 4], YC[:, 4 * g:4 * g + 4], over(RG[:, g], 4, 0, L), mul)
                dve.drain()
                tt(OT[:, 16:32, bass.ds(c * L, L)], YC, vec(V_SNG, 16, L), mul)
                dve.drain()

            with dve.Fori(0, NPC) as c:
                ssm(c)
            nc.vector.sem_inc(sem("last_rows"), 1)
            ssm(NPC)
            nc.vector.sem_inc(sem("last_rows"), 1)
            dve.wait_ge(sem("state_out"), 64)
            dve.wait_ge(sem("last_rows_out"), 64)
            meet(dve, 3)

            dve.memset(SG, 0.0)
            dve.drain().then_inc(sem("gl_state"), 1)
            nc.vector.sem_inc(sem("rows_free"), 1)
            nc.vector.sem_inc(sem("gl_out"), 1)
            dve.wait_ge(sem("zeroed"), 2)

            def gla(c):
                one = c + 1
                dve.wait_ge(sem("gl_pre"), one)
                tt(T4, bank(0, 4, L, n=256), vec(V_BA, 4, L), add)
                dve.drain()
                stt(AB4, T4, -1.0, T4, mul, mx)
                dve.drain().then_inc(sem("softplus_in"), 1)
                dve.wait_ge(sem("softplus_out"), NCH + one)
                stt(T4, T4, 0.0, LB4, ALU.min, sub)
                dve.drain()
                flat = lambda x: x.rearrange("p a b -> p (a b)")
                dve.tensor_tensor_scan(flat(CS4), CON[:, C_RST:C_RST + 4 * L], flat(T4), 0.0, mul, add)
                dve.drain()
                tt(EE, CS4[:, :, L - 1:L].to_broadcast([128, 4, L]), CS4, sub)
                dve.drain().then_inc(sem("gl_cs"), 1)
                dve.wait_ge(sem("decays"), NCH + one)
                stt(QD, UG[:, 0:4], GLA_SCALE, EG, mul, mul)
                tt(KI, UG[:, 4:8], EI, mul)
                tt(KE, UG[:, 4:8], EE, mul)
                dve.drain().then_inc(sem("gl_ops"), 1)
                dve.wait_ge(sem("gl_sc"), one)
                tt(SCT[0:64], bank(0, 4, L, n=256)[0:64], M2[0:64, L:2 * L].unsqueeze(1).to_broadcast([64, 4, L]), mul)
                dve.tensor_copy(KET[0:64], bank(3, 4, 128)[0:64])
                dve.drain().then_inc(sem("gl_scm"), 1)
                nc.vector.sem_inc(sem("rows_free"), 1)
                dve.wait_ge(sem("mixed"), NCH + one)
                dve.tensor_copy(O8, bank(4, 8, L))
                dve.drain()
                tt(SQO, O8, O8, mul)
                dve.drain().then_inc(sem("squares"), 1)
                if c is NPC:
                    dve.wait_ge(sem("state_in"), 48)
                tt(SG, SG, EG[:, :, L - 1:L].to_broadcast([128, 4, 256]), mul)
                dve.drain()
                dve.wait_ge(sem("state_sums"), NCH + one)
                tt(SG, SG, banks(1, 2, 4, 256), add)
                dve.drain().then_inc(sem("gl_state"), 1)
                dve.wait_ge(sem("square_sums"), NCH + one)
                ts(RG4, bank(5, 4, L, n=256), 1.0 / 256, 1e-5, mul, add)
                dve.drain()
                dve.reciprocal(RG4, RG4)
                dve.drain().then_inc(sem("variance"), 1)
                dve.wait_ge(sem("rstd"), NCH + one)
                o4 = O8.rearrange("p (h i) b -> p h i b", i=2)
                for i in range(2):
                    tt(o4[:, :, i], o4[:, :, i], RG4, mul)
                dve.drain()
                for i in range(2):
                    ts(o4[:, :, i], o4[:, :, i], VEC[:, V_GNG + i:V_GNG + i + 1], None, mul)
                dve.drain()
                tt(OT[:, 8:16, bass.ds(c * L, L)], O8, RR, mul)
                dve.drain().then_inc(sem("gl_out"), 1)

            with dve.Fori(0, NPC) as c:
                gla(c)
            gla(NPC)
            dve.wait_ge(sem("state_out"), 96)
            meet(dve, 4)

            nc.vector.sem_inc(sem("wo_free"), 2)
            dve.wait_ge(sem("gates_ready"), 2)

            def merge(d, p):
                dve.wait_ge(sem("tile_done"), d * 4 + (NT + 4))
                b = [PS[:, 3 * p + k, 0:NTOK] for k in range(3)]
                tt(MG[:, d, :], b[0], GTF[:, d + 8, :], mul)
                tt(MTMP[:, 0], b[1], GTF[:, d, :], mul)
                tt(MTMP[:, 1], b[2], GTF[:, d + 16, :], mul)
                dve.drain()
                nc.vector.sem_inc(sem("wo_free"), 1)
                tt(MG[:, d, :], MG[:, d, :], MTMP[:, 0], add)
                dve.drain()
                tt(MG[:, d, :], MG[:, d, :], MTMP[:, 1], add)
                dve.drain().then_inc(sem("merged"), 1)

            with dve.Fori(0, 4) as d2:
                for p in range(2):
                    merge(d2 * 2 + p, p)
            dve.wait_ge(sem("ln_in"), 64)
            for t in range(TT3):
                w = 128 if t < 2 else 64
                dve.wait_ge(sem("w_out_done"), t + 1)
                stt(H0[0:w, t, :], H0[0:w, t, :], ALPHA, banks(2 * t, 2, D)[0:w], mul, add)
                dve.drain()
                layer_norm(H0, t, LN1[:, 0, :], LN1[:, 1, :], TT3 + t + 1, BN1, MV1, RS1).then_inc(sem("h1_ready"), 1)
            meet(dve, 5)

            dve.memset(SCO, 0.0)
            dve.memset(CHO, 0.0)
            dve.memset(PLACE, 0.0)
            dve.drain()
            nc.vector.sem_inc(sem("score_room"), 1)
            dve.wait_ge(sem("scores"), 1)

            def choose(out, x, th, k, n):
                ts(out, x, th, None, ALU.is_gt)
                ts(TIE[:, 0:n], x, th, None, ALU.is_equal)
                dve.drain()
                dve.tensor_reduce(CNT, out, AX.X, add)
                dve.tensor_tensor_scan(TRK[:, 0:n], TIE[:, 0:n], CON[:, C_ONE:C_ONE + n], 0.0, add, mul)
                dve.drain()
                tt(TRK[:, 0:n], TRK[:, 0:n], CNT.to_broadcast([128, n]), add)
                dve.drain()
                ts(TRK[:, 0:n], TRK[:, 0:n], float(k), None, ALU.is_le)
                dve.drain()
                tt(TIE[:, 0:n], TIE[:, 0:n], TRK[:, 0:n], mul)
                dve.drain()
                tt(out, out, TIE[:, 0:n], add)
                dve.drain()

            for t in range(TT3):
                w = 128 if t < 2 else 64
                tt(SBI, SCO[:, t, :], RB, add)
                dve.drain()
                for g in range(NG):
                    dve.max(TOP[:, g, :], SBI[:, 8 * g:8 * g + 8])
                dve.drain()
                tt(GSC, TOP[:, :, 0], TOP[:, :, 1], add)
                dve.drain()
                dve.max(TOP[:, 0, :], GSC)
                dve.drain()
                choose(GM, GSC, TOP[:, 0, 3:4], 4, NG)
                ts(GM, GM, -1.0, 1e30, add, mul)
                dve.drain()
                s3 = SBI.rearrange("p (g k) -> p g k", k=8)
                tt(s3, s3, GM.unsqueeze(2).to_broadcast([128, NG, 8]), add)
                dve.drain()
                dve.max(TOP[:, 0, :], SBI)
                dve.drain()
                choose(TIE2, SBI, TOP[:, 0, 7:8], TOPK, NE)
                dve.tensor_copy(CHO[0:w, t, :], TIE2[0:w])
                dve.drain()
                tt(GTE, SCO[:, t, :], CHO[:, t, :], mul)
                dve.drain()
                dve.tensor_reduce(CNT, GTE, AX.X, add)
                dve.drain()
                ts(CNT, CNT, 1e-30, None, mx)
                dve.drain()
                dve.reciprocal(CNT, CNT)
                dve.drain()
                ts(INFO[:, t, :, 0], GTE, CNT, 2.5, mul, mul)
                dve.tensor_tensor_scan(TRK, CHO[:, t, :], CON[:, C_ONE:C_ONE + NE], 0.0, add, mul)
                dve.drain()
                ts(TRK, TRK, VEC[:, V_TOK8 + t:V_TOK8 + t + 1], -1.0 - SKIP, add, add)
                dve.drain()
                dve.tensor_copy(INFO[:, t, :, 1], TRK)
                dve.drain()
            dve.drain().then_inc(sem("chosen"), 1)
            dve.wait_ge(sem("shared_silu"), 1)
            tt(SHID, SHID, PS[:, 6:8, 0:NTOK], mul)
            dve.drain().then_inc(sem("shared_act"), 1)
            nc.vector.sem_inc(sem("shared_free"), 2)
            dve.wait_ge(sem("places"), 1)
            ts(PLACE, bank(3, 8, NE)[:, 0:3], 1.0, None, mul)
            dve.tensor_copy(CTOT, PS[:, 3, 192:192 + NE])
            ts(TIE3, CHO, -1e4, 1e4, mul, add)
            dve.drain()
            tt(PLACE, PLACE, TIE3, add)
            dve.tensor_reduce(CNT, CTOT, AX.X, mx)
            dve.drain()
            ts(CNT, CNT, float(CAP), None, ALU.is_gt)
            dve.drain()
            dve.tensor_copy(FLAG[:, :], CNT)
            dve.drain().then_inc(sem("flag"), 1)
            for t in range(TT3):
                w = 128 if t < 2 else 64
                dve.wait_ge(sem("shared_out"), t + 1)
                stt(ACC[0:w, t, :], H0[0:w, t, :], ALPHA, banks(4 + 2 * (t % 2), 2, D)[0:w], mul, add)
                dve.drain()
                nc.vector.sem_inc(sem("shared_free"), 1)
            nc.vector.sem_inc(sem("hid_moved"), 2)
            nc.vector.sem_inc(sem("y_left"), 2)
            nc.vector.sem_inc(sem("y_right"), 2)
            nc.vector.sem_inc(sem("rows_out"), YRING)

            def onehot(e, p, b):
                for t in range(TT3):
                    ts(OH[:, p, t, :], CON[:, C_IOTA + CAP * b:C_IOTA + CAP * b + CAP], PLACE[:, t, bass.ds(e, 1)], None,
                       ALU.is_equal)
                dve.drain().then_inc(sem("onehot"), 1)

            def hid_step(n, p, s):
                dve.wait_ge(sem("silu_ready"), n + 1)
                dve.wait_ge(sem("rows_out"), n + 1)
                hb = bank(2 + p, 8, CAP)
                tt(HID[:, p], SIL[:, p], hb[:, 2:4], mul)
                dve.tensor_copy(GA[0:CAP, s:s + 1], PS[0:CAP, 2 + p, 256:257])
                ts(IDX[0:CAP, s:s + 1], PS[0:CAP, 2 + p, 257:258], float(SKIP), None, add)
                dve.drain().then_inc(sem("hid_ready"), 1)
                nc.vector.sem_inc(sem("hid_moved"), 1)

            def y_step(n, p, s):
                dve.wait_ge(sem("expert_done"), n + 1)
                ts(Y[0:CAP, s, 0:512], PS[0:CAP, 4 + 2 * p, :], GA[0:CAP, s:s + 1], None, mul)
                dve.drain().then_inc(sem("y_left"), 1)

            onehot(0, 0, 0)
            onehot(1, 1, 0)
            hid_step(0, 0, 0)
            onehot(2, 0, 0)

            def steady(m, i, more=True):
                hid_step(m * MRING + i, i % 2, i % YRING)
                if more:
                    onehot(m * MRING + (i + 2), i % 2, 0)
                y_step(m * MRING + (i - 1), (i - 1) % 2, (i - 1) % YRING)

            with dve.Fori(0, NE // MRING - 1) as m:
                for i in range(1, MRING + 1):
                    steady(m, i)
            for e in range(NE - 3, NE):
                steady(e // MRING, e % MRING, e + 2 < NE)
            y_step(NE - 1, 1, 3)
            with overflow(dve):
                with dve.Fori(0, NE) as e:
                    for b in range(NBLK - 1):
                        n = e * (NBLK - 1) + (NE + b)
                        onehot(e, b % 2, b + 1)
                        hid_step(n, b % 2, b % YRING)
                        y_step(n, b % 2, b % YRING)
            dve.wait_ge(sem("ln_in"), 96)
            for t in range(TT3):
                w = 128 if t < 2 else 64
                dve.wait_ge(sem(f"slots_in{t % 2}"), 16 * (t // 2 + 1))
                rw = ROWS[0:w, t % 2]
                for k in (4, 2, 1):
                    tt(rw[:, 0:k], rw[:, 0:k], rw[:, k:2 * k], add)
                    dve.drain()
                tt(ACC[0:w, t, :], ACC[0:w, t, :], rw[:, 0], add)
                dve.drain().then_inc(sem("rows_summed"), 1)
                layer_norm(ACC, t, LN2[:, 0, :], LN2[:, 1, :], 2 * TT3 + t + 1, BN2, MV2, RS2, w).then_inc(sem("y_ready"), 1)

        @block.gpsimd
        def _(pool):
            meet(pool, 1)
            meet(pool, 2)
            for x in (XTBD, XDBD, XEBD):
                pool.memset(x, 0.0)
            pool.drain().then_inc(sem("zeroed"), 1)
            nc.gpsimd.sem_inc(sem("ss_free_pool"), 1)

            def ssm(c):
                one = c + 1
                pool.wait_ge(sem("ss_bcs"), one)
                pool.wait_ge(sem("rows_in"), one * 32)
                x = XC[:, 16:24]
                def w(k):
                    return VEC[:, V_CW + 24 * k + 16:V_CW + 24 * k + 24].unsqueeze(2).to_broadcast([128, 8, L])
                pool.tensor_tensor(x, UX[:, 16:24, 0:L], w(0), ALU.mult)
                for k in range(1, 4):
                    pool.tensor_tensor(TMP2, UX[:, 16:24, k:k + L], w(k), ALU.mult)
                    pool.drain()
                    pool.tensor_tensor(x, x, TMP2, ALU.add)
                    pool.drain()
                pool.tensor_tensor(x, x, vec(V_CB + 16, 8, L), ALU.add)
                pool.drain().then_inc(sem("ss_cbc"), 1)
                nc.gpsimd.sem_inc(sem("ss_free_pool"), 1)
                pool.wait_ge(sem("ss_xs"), one)
                pool.tensor_tensor(XD, XS_, vec(V_DSK, 16, L), ALU.mult)
                pool.drain().then_inc(sem("ss_xd"), 1)

            with pool.Fori(0, NCH) as c:
                ssm(c)
            meet(pool, 3)
            for x in (VT, SCT, KET):
                pool.memset(x, 0.0)
            pool.drain().then_inc(sem("zeroed"), 1)
            meet(pool, 4)
            meet(pool, 5)

            last_slot = pool.to_reg(SLOTS - 1)

            def scatter(m):
                def sent(i):
                    pool.wait_ge(sem(f"rows_sent{i % 2}"), m * 32 + 16 * (i // 2 + 1))
                    nc.gpsimd.sem_inc(sem("rows_out"), 1)

                for i in range(YRING):
                    pool.wait_ge(sem("y_left"), m * YRING + (i + 3))
                    pool.wait_ge(sem("y_right"), m * YRING + (i + 3))
                    if i >= 2:
                        sent(i - 2)
                    nc.gpsimd.sem_inc(sem("rows_taken"), 1)
                    pool.indirect_dma_start(slots[:, :], bass.IndirectOffsetOnAxis(ap=IDX[0:CAP, i:i + 1], axis=0),
                                            Y[0:CAP, i, :], None, bounds_check=last_slot, oob_is_err=False
                                            ).then_inc(sem(f"rows_sent{i % 2}"), 16)
                sent(2)
                sent(3)

            with pool.Fori(0, NE // YRING) as m:
                scatter(m)
            with overflow(pool):
                with pool.Fori(NE // YRING, NE // YRING * NBLK) as m:
                    scatter(m)
            pool.drain().then_inc(sem("rows_over"), 1)


def _tiles(w, ncol):
    import numpy as np
    k, n = w.shape
    return w.reshape(k // 128, 128, n // ncol, ncol).transpose(2, 1, 0, 3)


def _cols(v):
    return v.reshape(-1, 128).T


def _constants():
    import numpy as np
    c = np.zeros((128, NC), np.float32)
    p = np.arange(128)
    s = p % 64
    t = np.arange(64)
    c[:, C_ID:C_ID + 128] = np.eye(128)
    c[:, C_ONE:C_ONE + 128] = 1.0
    c[:, C_BLK:C_BLK + 128] = (p[:, None] // 64) == (p[None] // 64)
    c[:, C_M2:C_M2 + 64] = t[None] > s[:, None]
    c[:, C_M2 + 64:C_M2 + 128] = t[None] >= s[:, None]
    c[:, C_ML:C_ML + 64] = t[None] < s[:, None]
    c[:, C_E:C_E + 64] = t[None] == s[:, None]
    c[:, C_RST:C_RST + 512] = np.arange(512) % 64 != 0
    h = np.arange(32)
    c[32:64, C_LH:C_LH + 128] = (h[:, None] % 2) == (p[None] // 64)
    c[32:64, C_PM:C_PM + 16] = (h[:, None] // 2) == np.arange(16)[None]
    c[32:64, C_SEL:C_SEL + 32] = np.eye(32)
    c[:, C_TRI:C_TRI + 128] = p[:, None] < p[None]
    c[:, C_IOTA:C_IOTA + NTOK] = np.arange(NTOK)
    return c


def _layout(i):
    import numpy as np
    f = np.float32
    g = {k: np.asarray(v)[0] if k not in ('x_prompt', 'x_sample', 'ln_in_g', 'ln_in_b') else np.asarray(v)
         for k, v in i.items()}
    a = {}
    x = np.zeros((384, D), f)
    x[:256] = g['x_prompt'][0]
    x[256:320] = g['x_sample'][0]
    a['x'] = x.reshape(3, 128, D)
    w = g['w_in']
    wp = np.zeros((D, NT * 128), f)
    place = [(T_RW, 6160, 3328), (T_XBC, 11536, 3072), (T_Z, 9488, 2048), (T_GLA, 3072, 3072), (T_GATE, 0, 3072)]
    for tile, col, n in place:
        wp[:, tile * 128:tile * 128 + n] = w[:, col:col + n]
    wp[:, T_MISC * 128:T_MISC * 128 + 16] = w[:, 6144:6160]
    wp[:, T_MISC * 128 + 32:T_MISC * 128 + 64] = w[:, 14608:14640]
    a['w_in'] = np.ascontiguousarray(_tiles(wp, 128))
    hist = np.zeros((128, NT, 2, HIST), f)
    hist[:, T_RW:T_RW + 26, 1, 2] = _cols(g['state_rwkv_shift'][0, 0])
    for k in range(3):
        hist[:, T_XBC:T_XBC + 24, 1, k] = _cols(g['state_ssm_conv'][0, k])
    a['hist'] = hist
    v = np.zeros((128, NV), f)
    for at, name in ((V_MU, 'rwkv_mu'), (V_W0, 'rwkv_w0'), (V_A0, 'rwkv_a0'), (V_KK, 'rwkv_k_k'), (V_KA, 'rwkv_k_a'),
                     (V_RK, 'rwkv_r_k'), (V_LNG, 'rwkv_ln_g'), (V_LNB, 'rwkv_ln_b'), (V_BA, 'gla_ba'),
                     (V_GNG, 'gla_norm_g'), (V_CB, 'ssm_conv_b'), (V_SNG, 'ssm_norm_g')):
        c = _cols(g[name])
        v[:, at:at + c.shape[1]] = c
    for k in range(4):
        v[:, V_CW + 24 * k:V_CW + 24 * k + 24] = _cols(g['ssm_conv_w'][k])
    d = g['ssm_d'].reshape(16, 2).T
    v[0:64, V_DSK:V_DSK + 16] = d[0]
    v[64:128, V_DSK:V_DSK + 16] = d[1]
    v[32:64, V_DTB] = g['ssm_dt_bias']
    v[32:64, V_ALOG] = g['ssm_a_log']
    for k in range(3):
        v[:, V_TOK8 + k] = 8.0 * (np.arange(128) + 128 * k)
    a['vecs'] = v
    a['consts'] = _constants()
    sm = np.zeros((128, 3 * D + 512), f)
    sm[0:64, 0:D] = g['rwkv_w2']
    sm[64:128, D:2 * D] = g['rwkv_a2']
    sm[:, 2 * D:3 * D] = g['rwkv_g2']
    sm[0:16, 3 * D:] = g['gla_wa2']
    a['small_w'] = sm
    wo = np.zeros((8, 4, 128, 8, 128), f)
    wo[:, 0] = _tiles(g['rwkv_wo'], 128)
    wo[:, 1] = _tiles(g['gla_wo'], 128)
    wo[:, 2] = _tiles(g['ssm_wo'][:D], 128)
    wo[:, 3] = _tiles(g['ssm_wo'][D:], 128)
    a['wo'] = wo
    a['w_out'] = np.ascontiguousarray(_tiles(g['w_out'], D)[0])
    a['lnv'] = np.stack([g[k] for k in ('ln_in_g', 'ln_in_b', 'ln1_g', 'ln1_b', 'ln2_g', 'ln2_b')])
    a['w_router'] = np.ascontiguousarray(_tiles(g['w_router'], NE)[0])
    a['router_bias'] = g['router_bias'].reshape(1, NE)

    def expert(w1, w3, w2):
        e = np.empty((128, 6144), f)
        b = e[:, 0:4096].reshape(128, KT, 512)
        b[:, :, 0:256] = _tiles(w1, 256)[0]
        b[:, :, 256:512] = _tiles(w3, 256)[0]
        e[:, 4096:] = _tiles(w2, D)[0].reshape(128, 2 * D)
        return e

    m = np.empty((NE + 1, 128, 6144), f)
    for e in range(NE):
        m[e] = expert(g['exp_w1'][e], g['exp_w3'][e], g['exp_w2'][e])
    m[NE] = expert(g['sh_w1'], g['sh_w3'], g['sh_w2'])
    a['moe_w'] = m
    s = g['state_rwkv'][0].reshape(8, 2, 64, 64)
    a['st_rwkv'] = np.ascontiguousarray(s.transpose(1, 3, 0, 2).reshape(128, 8, 64))
    a['st_gla'] = np.ascontiguousarray(g['state_gla'][0].transpose(1, 0, 2))
    a['st_ssm'] = np.ascontiguousarray(g['state_ssm'][0].transpose(2, 0, 1)).reshape(128, 2048)
    return {k: np.ascontiguousarray(z, dtype=f) for k, z in a.items()}


_OUTS = [('y', (3, 128, D)), ('gla', (2, 128, 4, 256)), ('rwkv', (2, 128, 8, 64)), ('shift', (2, 128, 26)),
         ('ssm', (2, 128, 2048)), ('conv', (2, 128, 24, 3))]


def kernel(**inputs):
    import numpy as _np
    import concourse.bacc as _bacc
    from concourse import mybir as _mybir
    from concourse.bass_utils import run_bass_kernel_spmd as _run

    nc = _bacc.Bacc("TRN2", target_bir_lowering=False, num_devices=1)
    a = _layout(inputs)
    io = {k: nc.dram_tensor(k, v.shape, _mybir.dt.from_np(v.dtype), kind="ExternalInput").ap() for k, v in a.items()}
    for n, s in _OUTS:
        io['out_' + n] = nc.dram_tensor('out_' + n, s, _mybir.dt.float32, kind="ExternalOutput").ap()
    hybrid_layer(nc, io)
    r = _run(nc, [a], core_ids=[0]).results[0]
    y = r['out_y'].reshape(384, D)
    gla = r['out_gla'].transpose(0, 2, 1, 3)
    rw = r['out_rwkv'].reshape(2, 2, 64, 8, 64).transpose(0, 3, 1, 4, 2).reshape(2, 16, 64, 64)
    sh = r['out_shift'].transpose(0, 2, 1).reshape(2, 3328)
    ss = r['out_ssm'].reshape(2, 128, 32, 64).transpose(0, 2, 3, 1)
    cv = r['out_conv'].transpose(0, 3, 2, 1).reshape(2, 3, 3072)
    c = _np.ascontiguousarray

    def states(s):
        return (c(gla[s])[None, None], c(rw[s])[None, None], c(sh[s])[None, None, None], c(ss[s])[None, None],
                c(cv[s])[None, None])

    return (c(y[:256])[None], c(y[256:320])[None]) + states(0) + states(1)
```

```python
import concourse.bass as bass
from concourse import mybir
from contextlib import ExitStack, contextmanager

FP32 = mybir.dt.float32
I32 = mybir.dt.int32
ALU = mybir.AluOpType
ACT = mybir.ActivationFunctionType
AX = mybir.AxisListType

D = 1024
KT = D // 128
NTOK = 320
TT3 = 3
L = 64
NCH = NTOK // L
NPC = NCH - 1
HIST = 3
CW = HIST + L

T_RW = 0
T_MISC = 26
T_XBC = 27
T_Z = 51
T_GLA = 67
T_GATE = 91
NT = 115
RING = 4
PRE = 28
FILL = 8
PB = NT - PRE - 2 * NCH * FILL

V_MU, V_W0, V_A0, V_KK, V_KA, V_RK, V_LNG, V_LNB = 0, 26, 34, 42, 50, 58, 66, 74
V_BA, V_GNG, V_CW, V_CB, V_SNG, V_DSK, V_DTB, V_ALOG, V_TOK8 = 82, 86, 88, 184, 208, 224, 240, 241, 242
NV = 245

C_ID, C_ONE, C_BLK, C_M2, C_ML, C_E, C_RST, C_LH, C_PM, C_SEL, C_TRI, C_IOTA = (
    0, 128, 256, 384, 512, 576, 640, 1152, 1280, 1296, 1328, 1456)
NC = 1456 + NTOK

DECAY = 0.6065306597126334
GLA_SCALE = 128 ** -0.5
ALPHA = 2.0 ** 0.25
NE, TOPK, NG, DE = 64, 8, 8, 256
CAP = 64
NBLK = NTOK // CAP
SLOTS = NTOK * TOPK
RW_IN, SSM_IN, GLA_IN = 26, 24, 24


def hybrid_layer(nc, io):
    ctx = ExitStack()
    with ctx:
        sems = {}

        def sem(name):
            if name not in sems:
                sems[name] = ctx.enter_context(nc.semaphore(name))
            return sems[name]

        ut = nc.dram_tensor("projected", (NT, 128, NCH, CW), FP32, kind="Internal").ap()
        slots = nc.dram_tensor("expert_rows", (SLOTS, D), FP32, kind="Internal").ap()
        PS = ctx.enter_context(nc.psum_tensor("PS", [128, 8, 512], FP32))

        def sb(name, *shape):
            return ctx.enter_context(nc.sbuf_tensor(name, [128, *shape], FP32))

        CON = sb("constants", NC)
        VEC = sb("feature_vectors", NV)
        HISTS = sb("history", NT, 2, HIST)
        H0 = sb("h0", TT3, D)
        H0T = sb("h0T", KT, NTOK)
        REGION = sb("region", 53100 - (NC + NV + NT * 6 + TT3 * D + KT * NTOK))
        ID, ONE, BLK = (CON[:, c:c + 128] for c in (C_ID, C_ONE, C_BLK))
        M2, ML, E = CON[:, C_M2:C_M2 + 128], CON[:, C_ML:C_ML + 64], CON[:, C_E:C_E + 64]
        LH, PM, SEL, TRI = (CON[:, a:a + n] for a, n in ((C_LH, 128), (C_PM, 16), (C_SEL, 32), (C_TRI, 128)))
        at = [0]

        def size(shape):
            n = 1
            for k in shape:
                n *= k
            return n

        def take(*shape):
            n = size(shape)
            v = REGION[:, at[0]:at[0] + n]
            at[0] += n
            return shaped(v, *shape)

        def shaped(v, *shape):
            names = "abcd"[:len(shape)]
            if len(shape) <= 1:
                return v
            return v.rearrange(f"p ({' '.join(names)}) -> p {' '.join(names)}",
                               **{k: s for k, s in zip(names[1:], shape[1:])})

        def vec(a, n, w):
            return VEC[:, a:a + n].unsqueeze(2).to_broadcast([128, n, w])

        def over(ap, n, m, w):
            return ap.unsqueeze(1).to_broadcast([128, n, w])

        def half(ap, h):
            return ap[64 * h:64 * h + 64, :, 64 * h:64 * h + 64]

        def bank(b, *shape, n=512):
            return shaped(PS[:, b, 0:n], *shape)

        def banks(b, k, *shape):
            v = PS[:, b:b + k, :].rearrange("p b n -> p (b n)")
            return shaped(v, *shape)

        WR = take(RING, KT, 128)
        STG = take(RING, NCH, CW)
        OT = take(32, NTOK)
        mixer_base = at[0]

        UR, US = take(26, L + 1), take(26, L)
        LOW, GS = take(L), take(L)
        (WS, AS, CS, GP, G, GI, KK, SQ, K2, KA, TA, BQ, BV, YS) = (take(8, L) for _ in range(14))
        AR = take(8, 2, L)
        ABD, BBD, KBD, VBD, PBD, PTBD, AKBD, SBD, SABD = (take(8, 128) for _ in range(9))
        VS, PSK, XS, SAS, SS = (take(8, L) for _ in range(5))
        SB, SK = take(8, 2, L), take(8, 2, L)
        PTT = take(8, 2, L)
        SHO, GLAST = take(26), take(8)
        GATE, BVL = take(8, L), take(8, L)
        assert at[0] <= REGION.shape[1], at[0]
        W2P, A2P, G2 = (OT[:, 16:].rearrange("p a b -> p (a b)")[:, k * D:k * D + D] for k in range(3))

        at[0] = mixer_base
        UX, UZ, UM = take(24, CW), take(16, L), take(L)
        XC, TMP, TMP2, XS_, XD = take(24, L), take(16, L), take(8, L), take(16, L), take(16, L)
        XTBD, XDBD, XEBD = take(16, 128), take(16, 128), take(16, 128)
        BT2, CT, BTM, CBM = take(4, 2, L), take(4, L), take(4, 128), take(4, L)
        T1, AB, LB, DT2, AC2, SELL = take(L), take(L), take(L), take(2, L), take(2, L), take(32)
        DTS, ACS, ALS, EL, NA = take(16), take(16), take(16), take(32), take(1)
        RD, SEG, EBC, YO, YC, SN = take(16, L), take(16, L), take(16, L), take(16, L), take(16, L), take(2048)
        RG, CVO = take(4, L), take(24, HIST)
        assert at[0] <= REGION.shape[1], at[0]

        at[0] = mixer_base
        UG, UA, WA2 = take(24, L), take(L), take(512)
        T4, AB4, LB4, CS4, EG, EI, EE, QD, KI, KE, SCT, RG4 = (take(4, L) for _ in range(12))
        VT, KET, SG, O8, SQO, RR = take(8, 128), take(4, 128), take(4, 256), take(8, L), take(8, L), take(8, L)

        at[0] = mixer_base
        GT, MG, MTMP, WOUT = take(24, NCH, L), take(8, NTOK), take(2, NTOK), take(KT, D)
        GTF = GT.rearrange("p t c w -> p t (c w)")
        LN1, BN1, MV1, RS1 = take(2, D), take(3, 2, 6), take(3, 2), take(3)
        assert at[0] <= REGION.shape[1], at[0]

        at[0] = 0
        W13, W2 = take(2, 2, 4096), take(2, 2, 2048)
        WRT, RB, SCO, CHO, PLACE, TIE3 = take(KT, NE), take(NE), take(3, NE), take(3, NE), take(3, NE), take(3, NE)
        SBI, TIE, TIE2, TRK, GTE, CTOT = (take(NE) for _ in range(6))
        TOP, GSC, GM, CNT, FLAGW = take(NG, 8), take(8), take(8), take(1), take(1)
        INFO, OH, XE = take(3, 2 * NE), take(2, 3, 128), take(KT, 128)
        SIL, HID, HIDT, SHID, Y = take(256), take(256), take(2, 128), take(2, NTOK), take(2, D)
        ACC, GA, LN2, BN2, MV2, RS2 = take(3, D), take(2), take(2, D), take(3, 2, 6), take(3, 2), take(3)
        assert at[0] <= REGION.shape[1], at[0]
        IDX = ctx.enter_context(nc.sbuf_tensor("row_index", [128, 2], I32))
        FLAG = ctx.enter_context(nc.sbuf_tensor("overflow", [128, 1], I32))
        ROWS = shaped(REGION[:, 0:16384], 2, TOPK, D)
        SKIP = 4096

        @contextmanager
        def overflow(e):
            e.wait_ge(sem("flag"), 1)
            more = e.value_load(FLAG[0:1, 0:1], min_val=0, max_val=1)
            with e.If(more > 0):
                yield

        LNB = shaped(REGION[:, mixer_base:mixer_base + 2 * D], 2, D)
        BN = shaped(REGION[:, mixer_base + 2 * D:mixer_base + 2 * D + 36], 3, 2, 6)
        MV = shaped(REGION[:, mixer_base + 2 * D + 36:mixer_base + 2 * D + 42], 3, 2)
        RS = REGION[:, mixer_base + 2 * D + 42:mixer_base + 2 * D + 45]
        MIX = REGION[:, mixer_base:]

        block = ctx.enter_context(nc.Block())
        ENG = 4

        def meet(e, k):
            e.drain().then_inc(sem("phase_over"), 1)
            e.wait_ge(sem("phase_over"), ENG * k)

        @block.sync
        def _(sp):
            sp.dma_start(H0[:, :, :], io['x'].rearrange("t p d -> p t d")).then_inc(sem("consts_in"), 16)
            sp.dma_start(CON[:, :], io['consts']).then_inc(sem("consts_in"), 16)
            for k in range(2):
                sp.dma_start(LNB[:, k, :], io['lnv'][k:k + 1, :].to_broadcast([128, D])).then_inc(sem("ln_in"), 16)
            sp.dma_start(VEC[:, :], io['vecs']).then_inc(sem("consts_in"), 16)
            sp.dma_start(HISTS[:, :, :, :], io['hist']).then_inc(sem("consts_in"), 16)
            sw = io['small_w']
            for k, t in enumerate((W2P, A2P, G2)):
                sp.dma_start(t, sw[:, k * D:k * D + D]).then_inc(sem("small_w_in"), 16)

            def weights(m, i, first=False):
                n = m * RING + i
                if not first:
                    sp.wait_ge(sem("tile_done"), n - RING + 1)
                sp.dma_start(WR[:, i, :, :], io['w_in'][n, :, :, :]).then_inc(sem(f"weights_in{i}"), 16)

            for i in range(RING):
                weights(0, i, first=True)
            with sp.Fori(1, PRE // RING) as m:
                for i in range(RING):
                    weights(m, i)

            for i in range(RING):
                sp.wait_ge(sem(f"store_done{i}"), 16 * (PRE // RING + 1))

            def chunk_rows(c):
                sp.wait_ge(sem("rw_ur_free"), c + 1)
                sp.dma_start(UR, ut[0:26, :, c, 2:CW].rearrange("t p w -> p t w")).then_inc(sem("rw_ur_in"), 16)

            def fill_weights(c, fs):
                for f in fs:
                    weights(c * (FILL // RING) + (PRE // RING + f // RING), f % RING)

            def state_out(s):
                sp.wait_ge(sem("rw_state"), NPC + 1 + s)
                sp.dma_start(io['out_rwkv'][s], SS).then_inc(sem("state_out"), 16)
                sp.wait_ge(sem("state_out"), 16 * (s + 1))

            def shift_out(s):
                sp.wait_ge(sem("last_rows"), 1 + s)
                sp.dma_start(io['out_shift'][s], SHO).then_inc(sem("last_rows_out"), 16)

            chunk_rows(0)
            with sp.Fori(0, NPC - 1) as c:
                chunk_rows(c + 1)
                fill_weights(c, range(FILL))
            shift_out(0)
            chunk_rows(NPC)
            fill_weights(NPC - 1, range(FILL))
            fill_weights(NPC, range(RING))
            state_out(0)
            sp.dma_start(SS, io['st_rwkv']).then_inc(sem("state_in"), 16)
            fill_weights(NPC, range(RING, FILL))
            state_out(1)
            shift_out(1)
            sp.wait_ge(sem("last_rows_out"), 32)
            for i in range(RING):
                sp.wait_ge(sem(f"store_done{i}"), 16 * ((PRE + NCH * FILL) // RING + 1))

            def ssm(c):
                sp.wait_ge(sem("rows_free"), c + 1)
                sp.wait_ge(sem("ss_free_pool"), c + 1)
                sp.dma_start(UM, ut[T_MISC, :, c, HIST:CW]).then_inc(sem("rows_in"), 16)
                sp.dma_start(UX, ut[T_XBC:T_XBC + 24, :, c, :].rearrange("t p w -> p t w")).then_inc(sem("rows_in"), 16)
                sp.wait_ge(sem("ss_z_free"), c + 1)
                sp.dma_start(UZ, ut[T_Z:T_Z + 16, :, c, HIST:CW].rearrange("t p w -> p t w")).then_inc(sem("ss_z_in"), 16)
                for f in range(FILL):
                    weights(c * 2 + (PRE // RING + NCH * FILL // RING + f // RING), f % RING)

            def ssm_out(s):
                sp.wait_ge(sem("ss_state"), (NPC if s == 0 else NCH) + 1)
                sp.dma_start(io['out_ssm'][s], SN).then_inc(sem("state_out"), 16)
                sp.wait_ge(sem("last_rows"), 3 + s)
                sp.dma_start(io['out_conv'][s], CVO).then_inc(sem("last_rows_out"), 16)
                sp.wait_ge(sem("state_out"), 32 + 16 * (s + 1))
                sp.wait_ge(sem("last_rows_out"), 32 + 16 * (s + 1))

            with sp.Fori(0, NPC) as c:
                ssm(c)
            ssm_out(0)
            sp.dma_start(SN, io['st_ssm']).then_inc(sem("state_in"), 16)
            ssm(NPC)
            ssm_out(1)
            for n in range(NT - PB, NT):
                weights(n // RING, n % RING)

            sp.wait_ge(sem("phase_over"), ENG * 3)
            sp.dma_start(WA2, io['small_w'][:, 3 * D:3 * D + 512]).then_inc(sem("small_w_in"), 16)
            for i in range(RING):
                sp.wait_ge(sem(f"store_done{i}"), 16 * ((NT + RING - 1 - i) // RING + 1))

            def gla(c):
                sp.wait_ge(sem("rows_free"), c + (NCH + 2))
                sp.dma_start(UA, ut[T_MISC, :, c, HIST:CW]).then_inc(sem("rows_in"), 16)
                sp.dma_start(UG, ut[T_GLA:T_GLA + 24, :, c, HIST:CW].rearrange("t p w -> p t w")).then_inc(sem("rows_in"), 16)

            def gla_out(s):
                sp.wait_ge(sem("gl_state"), (NPC if s == 0 else NCH) + 1)
                sp.dma_start(io['out_gla'][s], SG).then_inc(sem("state_out"), 16)
                sp.wait_ge(sem("state_out"), 64 + 16 * (s + 1))

            with sp.Fori(0, NPC) as c:
                gla(c)
            gla_out(0)
            sp.dma_start(SG, io['st_gla']).then_inc(sem("state_in"), 16)
            gla(NPC)
            gla_out(1)

            sp.wait_ge(sem("phase_over"), ENG * 4)
            for c in range(NCH):
                sp.dma_start(GT[:, :, c, :], ut[T_GATE:T_GATE + 24, :, c, HIST:CW].rearrange("t p w -> p t w")
                             ).then_inc(sem("gates_in"), 16)
            for q in range(4):
                sp.dma_start(WR[:, q, :, :], io['wo'][0, q, :, :, :]).then_inc(sem(f"weights_in{q}"), 16)
            sp.dma_start(WOUT, io['w_out']).then_inc(sem("w_out_in"), 16)
            with sp.Fori(1, 8) as d:
                for q in range(4):
                    sp.wait_ge(sem("tile_done"), d * 4 + (NT - 3 + q))
                    sp.dma_start(WR[:, q, :, :], io['wo'][d, q, :, :, :]).then_inc(sem(f"weights_in{q}"), 16)
            for k in range(2):
                sp.dma_start(LN1[:, k, :], io['lnv'][2 + k:3 + k, :].to_broadcast([128, D])).then_inc(sem("ln_in"), 16)

            sp.wait_ge(sem("phase_over"), ENG * 5)
            sp.dma_start(WRT, io['w_router']).then_inc(sem("router_in"), 16)
            sp.dma_start(RB, io['router_bias'].to_broadcast([128, NE])).then_inc(sem("router_in"), 16)
            for k in range(2):
                sp.dma_start(LN2[:, k, :], io['lnv'][4 + k:5 + k, :].to_broadcast([128, D])).then_inc(sem("ln_in"), 16)
            sp.dma_start(W13[:, 1, 1, :], io['moe_w'][NE, :, 0:4096]).then_inc(sem("shared_in"), 16)
            sp.dma_start(W2[:, 1, 1, :], io['moe_w'][NE, :, 4096:6144]).then_inc(sem("shared_in"), 16)

            def up_weights(e, p, i):
                sp.dma_start(W13[:, p, i, :], io['moe_w'][e, :, 0:4096]).then_inc(sem(f"w13_in{p}"), 16)

            def down_weights(e, p, i):
                sp.dma_start(W2[:, p, i, :], io['moe_w'][e, :, 4096:6144]).then_inc(sem(f"w2_in{p}"), 16)

            for e in range(4):
                if e == 3:
                    sp.wait_ge(sem("shared_used"), 1)
                up_weights(e, e // 2, e % 2)
                down_weights(e, e // 2, e % 2)
            with sp.Fori(1, NE // 4) as m:
                for p in range(2):
                    sp.wait_ge(sem("hid_done"), m * 2 + (p - 1))
                    for i in range(2):
                        up_weights(m * 4 + (2 * p + i), p, i)
                    sp.wait_ge(sem("pair_done"), m * 2 + (p - 1))
                    for i in range(2):
                        down_weights(m * 4 + (2 * p + i), p, i)
            sp.wait_ge(sem("pair_done"), NE // 2)
            with overflow(sp):
                with sp.Fori(0, NE // 2) as m:
                    sp.wait_ge(sem("pair_done"), m * (NBLK - 1) + NE // 2)
                    for i in range(2):
                        up_weights(m * 2 + i, 0, i)
                        down_weights(m * 2 + i, 0, i)
            sp.wait_ge(sem("rows_over"), 1)
            for t in range(TT3):
                w = 128 if t < 2 else 64
                sp.dma_start(ROWS[0:w, t % 2, :, :], slots[t * 1024:t * 1024 + w * 8, :].rearrange("(p k) d -> p k d", k=8)
                             ).then_inc(sem(f"slots_in{t % 2}"), 16)
                if t == 1:
                    sp.wait_ge(sem("rows_summed"), 1)
            for t in range(TT3):
                sp.wait_ge(sem("y_ready"), t + 1)
                w = 128 if t < 2 else 64
                sp.dma_start(io['out_y'][t, 0:w], ACC[0:w, t, :]).then_inc(sem("y_out"), 16)
            sp.wait_ge(sem("y_out"), 16 * TT3)

        @block.tensor
        def _(pe):
            mm = nc.tensor.matmul

            def project(m, i):
                n = m * RING + i
                pe.wait_ge(sem(f"weights_in{i}"), (m + 1) * 16)
                pe.wait_ge(sem("tile_moved"), n + 1)
                for k in range(KT):
                    last = mm(PS[:, 6 + i % 2, 0:NTOK], WR[:, i, k, :], H0T[:, k, :], start=(k == 0), stop=(k == KT - 1))
                last.then_inc(sem("tile_done"), 1)

            pe.wait_ge(sem("consts_in"), 64)
            for t in range(TT3):
                w = 128 if t < 2 else 64
                pe.wait_ge(sem("h_ready"), t + 1)
                for k in range(KT):
                    last = mm(PS[:, 2 * t + k // 4, (k % 4) * 128:(k % 4) * 128 + w], H0[:, t, k * 128:k * 128 + 128],
                              ID[:, 0:w], start=True, stop=True)
                last.then_inc(sem("h_turned"), 1)
            pe.wait_ge(sem("h0T_ready"), TT3)
            with pe.Fori(0, PRE // RING) as m:
                for i in range(RING):
                    project(m, i)
            meet(pe, 1)
            pe.wait_ge(sem("small_w_in"), 48)

            def pairs(out, lhs, rhs, **kw):
                for j in range(8):
                    last = mm(out(j), lhs(j), rhs(j), **kw)
                return last

            full = dict(start=True, stop=True)

            b = [bank(k, 8, L) for k in range(6)]

            def front_lora(c):
                pe.wait_ge(sem("rw_low"), c + 1)
                pairs(lambda j: b[2][:, j], lambda j: W2P[:, j * 128:j * 128 + 128], lambda j: LOW, **full)
                pairs(lambda j: b[3][:, j], lambda j: A2P[:, j * 128:j * 128 + 128], lambda j: LOW,
                      **full).then_inc(sem("rw_pre"), 1)
                pe.wait_ge(sem("rw_sq"), c + 1)
                mm(bank(5), BLK, SQ.rearrange("p a b -> p (a b)"), **full).then_inc(sem("rw_ss"), 1)

            def front_bonus(c):
                pe.wait_ge(sem("rw_bq"), c + 1)
                mm(bank(3), BLK, BQ.rearrange("p a b -> p (a b)"), **full).then_inc(sem("rw_bonus"), 1)

            def rwkv(c, ahead):
                def fill(f):
                    project(c * (FILL // RING) + (PRE // RING + f // RING), f % RING)

                one = c + 1
                pe.wait_ge(sem("rw_vbd"), one)
                pairs(lambda j: b[5][:, j], lambda j: VBD[:, j], lambda j: E, **full).then_inc(sem("rw_vtok"), 1)
                fill(0)
                pe.wait_ge(sem("rw_ops"), one)
                for o, lhs in ((0, BBD), (2, KBD)):
                    w = banks(o, 2, 8, 2, L)
                    pairs(lambda j: w[:, j], lambda j: lhs[:, j], lambda j: AR[:, j], **full).then_inc(sem("rw_scores"), 1)
                fill(1)
                pe.wait_ge(sem("rw_lva"), c * 5 + 1)
                pairs(lambda j: b[4][:, j], lambda j: PTBD[:, j], lambda j: E, **full).then_inc(sem("rw_p0"), 1)
                pe.wait_ge(sem("rw_masked"), c * 2 + 2)
                pairs(lambda j: b[2][:, j], lambda j: BBD[:, j], lambda j: E, **full)
                pairs(lambda j: b[3][:, j], lambda j: KBD[:, j], lambda j: E, **full).then_inc(sem("rw_bktok"), 1)
                for r in range(6):
                    pe.wait_ge(sem("rw_lv"), c * 6 + (r + 1))
                    if r < 5:
                        pe.wait_ge(sem("rw_lva"), c * 5 + (r + 1))
                        pairs(lambda j: b[4][:, j], lambda j: PTBD[:, j], lambda j: PSK[:, j], **full)
                    if r < 4:
                        pairs(lambda j: b[0][:, j], lambda j: PBD[:, j], lambda j: PTT[:, j, 0], **full)
                    if r:
                        pairs(lambda j: b[1][:, j], lambda j: PBD[:, j], lambda j: PTT[:, j, 1], **full)
                    pe.drain().then_inc(sem("rw_round"), 1)
                    if r < 3:
                        fill(2 + r)
                    if r == 3:
                        pe.wait_ge(sem("rw_sbd"), one)
                        pairs(lambda j: b[5][:, j], lambda j: G2[:, j * 128:j * 128 + 128], lambda j: GS,
                              **full).then_inc(sem("rw_gate"), 1)
                        fill(5)
                        if ahead:
                            front_lora(c + 1)
                if ahead:
                    pe.wait_ge(sem("rw_ssc"), c + 2)
                else:
                    pe.wait_ge(sem("rw_gated"), one)
                for j in range(8):
                    mm(b[5][:, j], AKBD[:, j], VS[:, j], start=True, stop=False)
                    last = mm(b[5][:, j], ABD[:, j], SS[:, j], start=False, stop=True)
                last.then_inc(sem("rw_x"), 1)
                fill(6)
                pe.wait_ge(sem("rw_xs"), one)
                pairs(lambda j: b[4][:, j], lambda j: PTBD[:, j], lambda j: XS[:, j], **full).then_inc(sem("rw_sa"), 1)
                if ahead:
                    front_bonus(c + 1)
                pe.wait_ge(sem("rw_sas"), one)
                for j in range(8):
                    mm(b[2][:, j], BBD[:, j], SAS[:, j], start=True, stop=False)
                    last = mm(b[2][:, j], KBD[:, j], VS[:, j], start=False, stop=True)
                last.then_inc(sem("rw_st"), 1)
                pe.wait_ge(sem("rw_sabd"), one)
                for j in range(8):
                    mm(b[0][:, j], SBD[:, j], AR[:, j, 1], start=True, stop=False)
                    mm(b[0][:, j], VBD[:, j], SK[:, j, 1], start=False, stop=False)
                    last = mm(b[0][:, j], SABD[:, j], SB[:, j, 1], start=False, stop=True)
                last.then_inc(sem("rw_y"), 1)
                fill(7)
                for f in range(8, FILL):
                    fill(f)
                pe.wait_ge(sem("rw_ys"), one)
                mm(bank(3), BLK, YS.rearrange("p a b -> p (a b)"), **full).then_inc(sem("rw_mean"), 1)
                pe.wait_ge(sem("rw_ysq"), one)
                mm(bank(4), BLK, SQ.rearrange("p a b -> p (a b)"), **full).then_inc(sem("rw_var"), 1)

            front_lora(0)
            front_bonus(0)
            with pe.Fori(0, NPC) as c:
                rwkv(c, True)
            rwkv(NPC, False)
            meet(pe, 2)
            def ssm(c):
                def fill(f):
                    project(c * 2 + (PRE // RING + NCH * FILL // RING + f // RING), f % RING)

                one = c + 1
                pe.wait_ge(sem("ss_ac"), one)
                mm(PS[:, 2, 0:32], DT2, SEL, **full)
                mm(PS[:, 2, 32:64], AC2, SEL, **full)
                mm(PS[:, 2, 64:96], ONE, SELL, **full)
                for k in range(2):
                    last = mm(bank(3 + k, 8, L), LH, RD[:, 8 * k:8 * k + 8, :], **full)
                last.then_inc(sem("ss_bc"), 1)
                fill(0)
                pe.wait_ge(sem("ss_xs"), one)
                w = banks(0, 2, 16, L)
                for j in range(16):
                    last = mm(w[:, j], XTBD[:, j], E, **full)
                last.then_inc(sem("ss_xtok"), 1)
                fill(1)
                pe.wait_ge(sem("ss_bcs"), one + 1)
                w = bank(5, 4, L, n=256)
                for g in range(4):
                    last = mm(w[:, g], BT2[:, g], CT[:, g], **full)
                pe.wait_ge(sem("ss_seg"), one)
                w = bank(2, 4, 128)
                for g in range(4):
                    last = mm(w[:, g], BT2[:, g], ID, **full)
                last.then_inc(sem("ss_cb"), 1)
                fill(2)
                fill(3)
                pe.wait_ge(sem("decays"), one)
                pe.wait_ge(sem("ss_state"), one)
                if c is NPC:
                    pe.wait_ge(sem("state_in"), 32)
                w = banks(3, 2, 16, L)
                for j in range(16):
                    last = mm(w[:, j], SN[:, j * 128:j * 128 + 128], CT[:, j // 4], **full)
                pe.wait_ge(sem("ss_mt"), one)
                w = banks(0, 2, 16, L)
                for j in range(16):
                    last = mm(w[:, j], XDBD[:, j], SEG[:, j], **full)
                last.then_inc(sem("mixed"), 1)
                fill(4)
                pe.wait_ge(sem("ss_yr"), one)
                pe.wait_ge(sem("ss_btm"), one)
                w = banks(0, 4, 16, 128)
                for j in range(16):
                    last = mm(w[:, j], BTM[:, j // 4], XEBD[:, j], **full)
                last.then_inc(sem("state_sums"), 1)
                fill(5)
                pe.wait_ge(sem("squares"), one)
                w = bank(5, 4, L, n=256)
                for k in range(4):
                    last = mm(w, ONE, YO.rearrange("p (g i) b -> p g i b", i=4)[:, :, k, :], start=(k == 0), stop=(k == 3))
                last.then_inc(sem("square_sums"), 1)
                fill(6)
                fill(7)

            with pe.Fori(0, NPC) as c:
                ssm(c)
            ssm(NPC)
            for n in range(NT - PB, NT):
                project(n // RING, n % RING)
            meet(pe, 3)

            def gla(c):
                one = c + 1
                if c is NPC:
                    pe.wait_ge(sem("state_in"), 48)
                pe.wait_ge(sem("rows_in"), one * 32 + 32 * NCH)
                pe.wait_ge(sem("gl_state"), one)
                for j in range(4):
                    last = mm(bank(0, 4, L, n=256)[:, j], WA2[:, j * 128:j * 128 + 128], UA, **full)
                last.then_inc(sem("gl_pre"), 1)
                w = banks(1, 2, 8, 128)
                for j in range(8):
                    last = mm(w[0:64, j], UG[:, 8 + j], ID, **full)
                last.then_inc(sem("gl_v"), 1)
                pe.wait_ge(sem("gl_ops"), one)
                for h in range(4):
                    last = mm(bank(0, 4, L, n=256)[0:64, h], KI[:, h], QD[:, h], **full)
                for h in range(4):
                    last = mm(bank(3, 4, 128)[0:64, h], KE[:, h], ID, **full)
                last.then_inc(sem("gl_sc"), 1)
                pe.wait_ge(sem("gl_scm"), one)
                pe.wait_ge(sem("gl_vt"), one)
                for j in range(8):
                    mm(bank(4, 8, L)[:, j], VT[:, j], SCT[:, j // 2], start=True, stop=False)
                    last = mm(bank(4, 8, L)[:, j], SG[:, j // 2, (j % 2) * 128:(j % 2) * 128 + 128], QD[:, j // 2],
                              start=False, stop=True)
                last.then_inc(sem("mixed"), 1)
                w = banks(1, 2, 4, 256)
                for h in range(4):
                    last = mm(w[:, h], KET[:, h], VT[:, 2 * h:2 * h + 2], **full)
                last.then_inc(sem("state_sums"), 1)
                pe.wait_ge(sem("squares"), NCH + one)
                for k in range(2):
                    last = mm(bank(5, 4, L, n=256), ONE, SQO.rearrange("p (g i) b -> p g i b", i=2)[:, :, k, :],
                              start=(k == 0), stop=(k == 1))
                last.then_inc(sem("square_sums"), 1)

            pe.wait_ge(sem("small_w_in"), 64)
            with pe.Fori(0, NPC) as c:
                gla(c)
            gla(NPC)
            meet(pe, 4)

            def outproj(d, p):
                pe.wait_ge(sem("wo_free"), d + 1)
                for q, (b, k0) in enumerate(((0, 0), (1, 8), (2, 16), (2, 24))):
                    pe.wait_ge(sem(f"weights_in{q}"), d * 16 + 16 * ((NT + RING - 1 - q) // RING + 1))
                    for k in range(KT):
                        last = mm(PS[:, 3 * p + b, 0:NTOK], WR[:, q, k, :], OT[:, k0 + k, :],
                                  start=(k == 0 and q < 3), stop=(k == KT - 1 and q != 2))
                    last.then_inc(sem("tile_done"), 1)

            with pe.Fori(0, 4) as d2:
                for p in range(2):
                    outproj(d2 * 2 + p, p)
            pe.wait_ge(sem("merged"), 8)
            pe.wait_ge(sem("w_out_in"), 16)
            for t in range(TT3):
                w = 128 if t < 2 else 64
                for h in range(2):
                    for k in range(KT):
                        last = mm(PS[0:w, 2 * t + h, :], MG[:, k, t * 128:t * 128 + w], WOUT[:, k, h * 512:h * 512 + 512],
                                  start=(k == 0), stop=(k == KT - 1))
                last.then_inc(sem("w_out_done"), 1)
            for t in range(TT3):
                w = 128 if t < 2 else 64
                pe.wait_ge(sem("h_ready"), TT3 + t + 1)
                for k in range(KT):
                    last = mm(PS[:, 2 * t + k // 4, (k % 4) * 128:(k % 4) * 128 + w], H0[:, t, k * 128:k * 128 + 128],
                              ID[:, 0:w], **full)
                last.then_inc(sem("h_turned"), 1)
            meet(pe, 5)

            pe.wait_ge(sem("router_in"), 32)
            for t in range(TT3):
                w = 128 if t < 2 else 64
                for k in range(KT):
                    last = mm(PS[0:w, t, 0:NE], H0T[:, k, t * 128:t * 128 + w], WRT[:, k, :], start=(k == 0), stop=(k == KT - 1))
            last.then_inc(sem("logits"), 1)
            pe.wait_ge(sem("shared_in"), 32)
            w13 = shaped(W13[:, 1, 1, :], KT, 512)
            for f in range(4):
                for k in range(KT):
                    last = mm(PS[:, 4 + f, 0:NTOK], w13[:, k, f * 128:f * 128 + 128], H0T[:, k, :],
                              start=(k == 0), stop=(k == KT - 1))
            last.then_inc(sem("shared_hid"), 1)
            pe.wait_ge(sem("chosen"), 1)
            for t in range(TT3):
                for u in range(t + 1):
                    last = mm(PS[:, 3, t * NE:t * NE + NE], TRI if u == t else ONE, CHO[:, u, :], start=(u == 0), stop=(u == t))
            for u in range(TT3):
                last = mm(PS[:, 3, 192:192 + NE], ONE, CHO[:, u, :], start=(u == 0), stop=(u == TT3 - 1))
            last.then_inc(sem("places"), 1)
            pe.wait_ge(sem("shared_act"), 1)
            w2 = shaped(W2[:, 1, 1, :], 2, D)
            for t in range(TT3):
                w = 128 if t < 2 else 64
                pe.wait_ge(sem("shared_free"), t + 1)
                for h in range(2):
                    for f in range(2):
                        last = mm(PS[0:w, 4 + 2 * (t % 2) + h, :], SHID[:, f, t * 128:t * 128 + w],
                                  w2[:, f, h * 512:h * 512 + 512], start=(f == 0), stop=(f == 1))
                last.then_inc(sem("shared_out"), 1)
            pe.drain().then_inc(sem("shared_used"), 1)
            pe.wait_ge(sem("shared_free"), TT3 + 2)

            def tiles(i):
                return slice(64 * i, 64 * i + 64)

            def gather(n, m, p, h):
                if h == 0:
                    pe.wait_ge(sem("onehot"), n + 1)
                    pe.wait_ge(sem("x_left"), n + 1)
                for k in range(4):
                    for t in range(TT3):
                        last = mm(bank(h, 4, 128)[:, k], H0[:, t, (4 * h + k) * 128:(4 * h + k) * 128 + 128], OH[:, p, t, :],
                                  start=(t == 0), stop=(t == TT3 - 1))
                if h == 0:
                    last.then_inc(sem("x_half"), 1)
                else:
                    for t in range(TT3):
                        last = mm(PS[:, 4, 0:4], OH[:, p, t, :], INFO[:, t, bass.ds(m * 4, 4)], start=(t == 0), stop=(t == TT3 - 1))
                    last.then_inc(sem("x_done"), 1)

            def hidden(n, p, loads):
                pe.wait_ge(sem("x_left"), n + 2)
                pe.wait_ge(sem("x_right"), n + 1)
                pe.wait_ge(sem(f"w13_in{p}"), loads * 32)
                for k in range(KT):
                    for i in range(2):
                        last = mm(PS[tiles(i), 2, :], XE[:, k, tiles(i)], W13[:, p, i, k * 512:k * 512 + 512],
                                  start=(k == 0), stop=(k == KT - 1))
                last.then_inc(sem("hid_done"), 1)

            def turn(n):
                pe.wait_ge(sem("hid_ready"), n + 1)
                for f in range(2):
                    last = mm(PS[:, 3, f * 128:f * 128 + 128], HID[:, f * 128:f * 128 + 128], ID, **full)
                last.then_inc(sem("hid_turned"), 1)

            def down(n, p, loads):
                pe.wait_ge(sem("hidt_ready"), n + 1)
                pe.wait_ge(sem(f"w2_in{p}"), loads * 32)
                pe.wait_ge(sem("y_left"), n + 1)
                pe.wait_ge(sem("y_right"), n + 1)
                for h in range(2):
                    for f in range(2):
                        for i in range(2):
                            last = mm(PS[tiles(i), 5 + h, :], HIDT[:, f, tiles(i)],
                                      W2[:, p, i, f * D + h * 512:f * D + h * 512 + 512], start=(f == 0), stop=(f == 1))
                last.then_inc(sem("pair_done"), 1)

            for h in range(2):
                gather(0, 0, 0, h)

            def steady(m, p):
                n = m * 2 + p
                hidden(n, p, m + 1)
                gather(n + 1, n + 1, 1 - p, 0)
                turn(n)
                gather(n + 1, n + 1, 1 - p, 1)
                down(n, p, m + 1)

            with pe.Fori(0, NE // 4 - 1) as m:
                for p in range(2):
                    steady(m, p)
            steady(NE // 4 - 1, 0)
            hidden(NE // 2 - 1, 1, NE // 4)
            turn(NE // 2 - 1)
            down(NE // 2 - 1, 1, NE // 4)
            with overflow(pe):
                with pe.Fori(0, NE // 2) as m:
                    for b in range(NBLK - 1):
                        n = m * (NBLK - 1) + (NE // 2 + b)
                        for h in range(2):
                            gather(n, m, b % 2, h)
                        hidden(n, 0, m + (NE // 4 + 1))
                        turn(n)
                        down(n, 0, m + (NE // 4 + 1))

        @block.scalar
        def _(act):
            def a_(out, in_, f, **kw):
                return nc.scalar.activation(out, in_, f, **kw)

            def root(x, asked, n, done):
                act.wait_ge(sem(asked), n)
                a_(x, x, ACT.Sqrt)
                act.drain().then_inc(sem(done), 1)

            for t in range(TT3):
                w = 128 if t < 2 else 64
                root(RS[:, t:t + 1], "ln_var", t + 1, "ln_rstd")
                act.wait_ge(sem("h_turned"), t + 1)
                src = banks(2 * t, 2, KT, 128)
                a_(H0T[:, :, t * 128:t * 128 + w], src[:, :, 0:w], ACT.Copy).then_inc(sem("h0T_ready"), 1)
            act.wait_ge(sem("consts_in"), 64)
            act.wait_ge(sem("stage_zero"), 1)
            for i in range(RING):
                nc.scalar.sem_inc(sem(f"store_done{i}"), 16)
            nc.scalar.sem_inc(sem("tile_moved"), 2)

            def move(m, i):
                n = m * RING + i
                act.wait_ge(sem("tile_done"), n + 1)
                act.wait_ge(sem(f"store_done{i}"), (m + 1) * 16)
                src = bank(6 + i % 2, NCH, L, n=NTOK)
                a_(STG[:, i, 1:NPC, 0:HIST], src[:, 0:NPC - 1, L - HIST:L], ACT.Copy)
                a_(STG[:, i, 0:NCH:NPC, 0:HIST], HISTS[:, n, :, :], ACT.Copy)
                a_(STG[:, i, :, HIST:CW], src, ACT.Copy)
                act.drain().then_inc(sem("tile_moved"), 1)
                act.wait_ge(sem("tile_moved"), n + 3)
                act.dma_start(ut[n, :, :, :], STG[:, i, :, :]).then_inc(sem(f"store_done{i}"), 16)

            with act.Fori(0, PRE // RING) as m:
                for i in range(RING):
                    move(m, i)
            meet(act, 1)

            def diag(out, src, func=ACT.Copy):
                for h in range(2):
                    last = a_(half(out, h), src[64 * h:64 * h + 64, :, :], func)
                return last

            b = [bank(k, 8, L) for k in range(6)]

            def front_low(c):
                act.wait_ge(sem("rw_us"), c + 1)
                a_(LOW[0:64, :], US[0:64, 24, :], ACT.Tanh)
                a_(LOW[64:128, :], US[64:128, 24, :], ACT.Copy)
                a_(GS, US[:, 25, :], ACT.Sigmoid)
                act.drain().then_inc(sem("rw_low"), 1)

            def front_decay(c):
                act.wait_ge(sem("rw_wa"), c + 1)
                a_(WS, WS, ACT.Sigmoid)
                a_(AS, AS, ACT.Sigmoid)
                act.drain().then_inc(sem("rw_sig"), 1)
                root(TA, "rw_ssc", c + 1, "rw_rn")
                act.wait_ge(sem("rw_cs"), c + 1)
                a_(G, CS, ACT.Exp, scale=-DECAY)
                a_(GI, CS, ACT.Exp, scale=DECAY)
                a_(GP, GP, ACT.Exp, scale=-DECAY)
                act.drain().then_inc(sem("rw_exp"), 1)

            def rwkv(c, late, ahead):
                def fill(f):
                    move(c * (FILL // RING) + (PRE // RING + f // RING), f % RING)

                one = c + 1
                diag(VBD, US[:, 16:24, :])
                act.drain().then_inc(sem("rw_vbd"), 1)
                act.wait_ge(sem("rw_vtok"), one)
                a_(VS, b[5], ACT.Copy)
                diag(VBD, b[5])
                act.wait_ge(sem("rw_ar"), one)
                diag(ABD, AR[:, :, 0, :])
                fill(0)
                act.wait_ge(sem("rw_masked"), c * 2 + 1)
                diag(PTBD, SB[:, :, 0, :])
                act.drain().then_inc(sem("rw_lva"), 1)
                fill(1)
                act.wait_ge(sem("rw_masked"), c * 2 + 2)
                diag(AKBD, SK[:, :, 0, :])
                act.wait_ge(sem("rw_bktok"), one)
                diag(BBD, b[2])
                diag(KBD, b[3])
                act.drain()
                act.wait_ge(sem("rw_state"), one)
                if c is NPC:
                    act.wait_ge(sem("state_in"), 16)
                diag(SBD, SS)
                act.drain().then_inc(sem("rw_sbd"), 1)
                for r in range(4):
                    act.wait_ge(sem("rw_round"), c * 6 + (r + 1))
                    diag(PTBD, b[0])
                    a_(PTT[:, :, 0, :], b[0], ACT.Copy)
                    act.drain().then_inc(sem("rw_lva"), 1)
                    if r < 3:
                        fill(2 + r)
                    if r == 0 and late:
                        root(TA, "rw_varc", c, "rw_rstd")
                act.wait_ge(sem("rw_late"), one)
                act.wait_ge(sem("rw_gate"), one)
                a_(GATE, b[5], ACT.Copy)
                act.drain().then_inc(sem("rw_gated"), 1)
                if ahead:
                    front_low(c + 1)
                fill(5)
                if ahead:
                    front_decay(c + 1)
                fill(6)
                act.wait_ge(sem("rw_sas"), one)
                diag(SABD, SAS)
                act.drain().then_inc(sem("rw_sabd"), 1)
                for f in range(7, FILL):
                    fill(f)

            front_low(0)
            front_decay(0)
            rwkv(0, False, True)
            with act.Fori(1, NPC) as c:
                rwkv(c, True, True)
            rwkv(NPC, True, False)
            root(TA, "rw_varc", NCH, "rw_rstd")
            meet(act, 2)
            a_(NA, VEC[:, V_ALOG:V_ALOG + 1], ACT.Exp)
            act.drain().then_inc(sem("gates_ready"), 1)
            nc.scalar.sem_inc(sem("ss_bcs"), 1)

            def ssm(c):
                def fill(f):
                    move(c * 2 + (PRE // RING + NCH * FILL // RING + f // RING), f % RING)

                one = c + 1
                act.wait_ge(sem("softplus_in"), one)
                a_(LB, AB, ACT.Exp, scale=-1.0)
                act.drain()
                a_(LB, LB, ACT.Ln, bias=1.0)
                act.drain().then_inc(sem("softplus_out"), 1)
                act.wait_ge(sem("ss_cx"), one)
                a_(XS_, XC[:, 0:16], ACT.Silu)
                diag(XTBD, XC[:, 0:16], ACT.Silu)
                act.drain().then_inc(sem("ss_xs"), 1)
                act.wait_ge(sem("ss_cbc"), one)
                for k in range(2):
                    a_(BT2[:, :, k, :], XC[:, 16:20], ACT.Silu)
                a_(CT, XC[:, 20:24], ACT.Silu)
                act.drain().then_inc(sem("ss_bcs"), 1)
                fill(0)
                act.wait_ge(sem("ss_z_in"), one * 16)
                a_(UZ, UZ, ACT.Silu)
                act.drain().then_inc(sem("ss_z"), 1)
                fill(1)
                act.wait_ge(sem("ss_seg"), one)
                a_(EBC, banks(3, 2, 16, L), ACT.Exp)
                a_(SEG, SEG, ACT.Exp)
                a_(EL, EL, ACT.Exp)
                a_(ALS, ALS, ACT.Exp)
                act.drain().then_inc(sem("decays"), 1)
                fill(2)
                act.wait_ge(sem("ss_cb"), one)
                a_(BTM, bank(2, 4, 128), ACT.Copy)
                act.drain().then_inc(sem("ss_btm"), 1)
                fill(3)
                fill(4)
                act.wait_ge(sem("ss_yz"), one)
                a_(YO, YC, ACT.Square)
                act.drain().then_inc(sem("squares"), 1)
                fill(5)
                root(RG, "variance", one, "rstd")
                fill(6)
                fill(7)

            with act.Fori(0, NPC) as c:
                ssm(c)
            ssm(NPC)
            for n in range(NT - PB, NT):
                move(n // RING, n % RING)
            meet(act, 3)
            act.wait_ge(sem("zeroed"), 2)

            def gla(c):
                one = c + 1
                act.wait_ge(sem("rows_in"), one * 32 + 32 * NCH)
                act.wait_ge(sem("gl_out"), one)
                a_(RR, UG[:, 16:24, :], ACT.Silu)
                act.wait_ge(sem("gl_v"), one)
                a_(VT[0:64], banks(1, 2, 8, 128)[0:64], ACT.Copy)
                act.drain().then_inc(sem("gl_vt"), 1)
                act.wait_ge(sem("softplus_in"), NCH + one)
                a_(LB4, AB4, ACT.Exp, scale=-1.0)
                act.drain()
                a_(LB4, LB4, ACT.Ln, bias=1.0)
                act.drain().then_inc(sem("softplus_out"), 1)
                act.wait_ge(sem("gl_cs"), one)
                a_(EG, CS4, ACT.Exp, scale=1.0 / 16)
                a_(EI, CS4, ACT.Exp, scale=-1.0 / 16)
                a_(EE, EE, ACT.Exp, scale=1.0 / 16)
                act.drain().then_inc(sem("decays"), 1)
                root(RG4, "variance", NCH + one, "rstd")

            with act.Fori(0, NPC) as c:
                gla(c)
            gla(NPC)
            meet(act, 4)

            act.wait_ge(sem("gates_in"), 16 * NCH)
            for g in range(3):
                a_(GT[:, 8 * g:8 * g + 8], GT[:, 8 * g:8 * g + 8], ACT.Sigmoid)
            act.drain().then_inc(sem("gates_ready"), 1)
            for t in range(TT3):
                root(RS1[:, t:t + 1], "ln_var", TT3 + t + 1, "ln_rstd")
            for t in range(TT3):
                w = 128 if t < 2 else 64
                act.wait_ge(sem("h_turned"), TT3 + t + 1)
                a_(H0T[:, :, t * 128:t * 128 + w], banks(2 * t, 2, KT, 128)[:, :, 0:w], ACT.Copy)
            meet(act, 5)

            act.wait_ge(sem("logits"), 1)
            act.wait_ge(sem("score_room"), 1)
            for t in range(TT3):
                w = 128 if t < 2 else 64
                a_(SCO[0:w, t, :], PS[0:w, t, 0:NE], ACT.Sigmoid)
            act.drain().then_inc(sem("scores"), 1)
            act.wait_ge(sem("shared_hid"), 1)
            a_(SHID, PS[:, 4:6, 0:NTOK], ACT.Silu)
            act.drain().then_inc(sem("shared_silu"), 1)
            nc.scalar.sem_inc(sem("x_left"), 1)

            def x_step(n):
                act.wait_ge(sem("x_half"), n + 1)
                a_(XE[:, 0:4], bank(0, 4, 128), ACT.Copy)
                act.drain().then_inc(sem("x_left"), 1)

            def silu_step(n):
                act.wait_ge(sem("hid_done"), n + 1)
                a_(SIL, PS[:, 2, 0:256], ACT.Silu)
                act.drain().then_inc(sem("silu_ready"), 1)

            def turn_step(n):
                act.wait_ge(sem("hid_turned"), n + 1)
                a_(HIDT, bank(3, 2, 128, n=256), ACT.Copy)
                act.drain().then_inc(sem("hidt_ready"), 1)

            def y_step(n, p):
                act.wait_ge(sem("pair_done"), n + 1)
                act.wait_ge(sem("rows_out"), n + 1)
                a_(Y[:, p, 512:D], PS[:, 6, :], ACT.Copy, scale=GA[:, p:p + 1])
                act.drain().then_inc(sem("y_right"), 1)

            def steady(n, p, more=True):
                silu_step(n)
                if more:
                    x_step(n + 1)
                turn_step(n)
                y_step(n, p)

            x_step(0)
            with act.Fori(0, NE // 4 - 1) as m:
                for p in range(2):
                    steady(m * 2 + p, p)
            steady(NE // 2 - 2, 0)
            steady(NE // 2 - 1, 1, False)
            with overflow(act):
                with act.Fori(0, NE // 2) as m:
                    for b in range(NBLK - 1):
                        n = m * (NBLK - 1) + (NE // 2 + b)
                        x_step(n)
                        steady(n, b % 2, False)
            for t in range(TT3):
                w = 128 if t < 2 else 64
                root(RS2[0:w, t:t + 1], "ln_var", 2 * TT3 + t + 1, "ln_rstd")

        @block.vector
        def _(dve):
            def tt(out, a, b, op):
                return dve.tensor_tensor(out, a, b, op)

            def ts(out, a, s1, s2, op0, op1=None):
                return dve.tensor_scalar(out, a, s1, s2, op0, op1) if op1 is not None else \
                    dve.tensor_scalar(out, a, s1, s2, op0)

            def stt(out, a, s, b, op0, op1):
                return dve.scalar_tensor_tensor(out=out, in0=a, scalar=s, in1=b, op0=op0, op1=op1)

            mul, add, sub, mx = ALU.mult, ALU.add, ALU.subtract, ALU.max

            def layer_norm(X, t, g, b, n_ln, BN=BN, MV=MV, RS=RS, w=128, eps=1e-5):
                X, BN, MV, RS, g, b = X[0:w], BN[0:w], MV[0:w], RS[0:w], g[0:w], b[0:w]
                for k in range(2):
                    dve.bn_stats(BN[:, t, k, :], X[:, t, k * 512:k * 512 + 512])
                dve.drain()
                dve.bn_aggr(MV[:, t, :], BN[:, t, :, :].rearrange("p a b -> p (a b)"))
                dve.drain()
                ts(RS[:, t:t + 1], MV[:, t, 1:2], eps, None, add)
                dve.drain()
                dve.reciprocal(RS[:, t:t + 1], RS[:, t:t + 1])
                dve.drain().then_inc(sem("ln_var"), 1)
                dve.wait_ge(sem("ln_rstd"), n_ln)
                ts(X[:, t, :], X[:, t, :], MV[:, t, 0:1], RS[:, t:t + 1], sub, mul)
                dve.drain()
                tt(X[:, t, :], X[:, t, :], g, mul)
                dve.drain()
                tt(X[:, t, :], X[:, t, :], b, add)
                return dve.drain()

            dve.memset(STG, 0.0)
            dve.drain().then_inc(sem("stage_zero"), 1)
            dve.wait_ge(sem("consts_in"), 64)
            dve.wait_ge(sem("ln_in"), 32)
            for t in range(TT3):
                layer_norm(H0, t, LNB[:, 0, :], LNB[:, 1, :], t + 1).then_inc(sem("h_ready"), 1)
            dve.memset(MIX, 0.0)
            dve.wait_ge(sem("consts_in"), 64)
            dve.drain().then_inc(sem("rw_ur_free"), 1)
            meet(dve, 1)
            nc.vector.sem_inc(sem("rw_state"), 1)
            dve.wait_ge(sem("consts_in"), 64)

            b = [bank(k, 8, L) for k in range(6)]
            r, k, v = US[:, 0:8, :], US[:, 8:16, :], US[:, 16:24, :]

            def front_shift(c, sample):
                dve.wait_ge(sem("rw_ur_in"), c * 16 + 16)
                if sample is not None:
                    dve.wait_ge(sem("rw_vbd"), c)
                tt(US, UR[:, :, 0:L], UR[:, :, 1:L + 1], sub)
                dve.drain()
                tt(US, US, vec(V_MU, 26, L), mul)
                dve.drain()
                tt(US, US, UR[:, :, 1:L + 1], add)
                if sample:
                    dve.wait_ge(sem("last_rows_out"), 16)
                dve.tensor_copy(SHO, UR[:, :, L])
                dve.drain().then_inc(sem("rw_us"), 1)
                nc.vector.sem_inc(sem("rw_ur_free"), 1)
                tt(KK, k, vec(V_KK, 8, L), mul)
                dve.drain()
                tt(SQ, KK, KK, mul)
                dve.drain().then_inc(sem("rw_sq"), 1)

            def front_rates(c):
                dve.wait_ge(sem("rw_pre"), c + 1)
                tt(WS, b[2], vec(V_W0, 8, L), add)
                tt(AS, b[3], vec(V_A0, 8, L), add)
                dve.drain().then_inc(sem("rw_wa"), 1)
                dve.wait_ge(sem("rw_ss"), c + 1)
                ts(TA, b[5], 1e-24, None, mx)
                dve.drain()
                dve.reciprocal(TA, TA)
                dve.drain().then_inc(sem("rw_ssc"), 1)

            def front_keys(c):
                dve.wait_ge(sem("rw_sig"), c + 1)
                dve.tensor_tensor_scan(CS.rearrange("p a b -> p (a b)"), CON[:, C_RST:C_RST + 512],
                                       WS.rearrange("p a b -> p (a b)"), 0.0, mul, add)
                dve.drain()
                tt(GP, CS, WS, sub)
                dve.drain().then_inc(sem("rw_cs"), 1)
                dve.wait_ge(sem("rw_rn"), c + 1)
                tt(KK, KK, TA, mul)
                dve.drain()
                tt(KA, KK, AS, mul)
                stt(TA, AS, -1.0, vec(V_KA, 8, L), add, mul)
                dve.drain()
                stt(K2, TA, 1.0, k, add, mul)
                dve.drain()
                tt(BQ, r, K2, mul)
                dve.drain()
                tt(BQ, BQ, vec(V_RK, 8, L), mul)
                dve.drain().then_inc(sem("rw_bq"), 1)

            def front_bonus(c):
                dve.wait_ge(sem("rw_bonus"), c + 1)
                tt(BV, b[3], v, mul)

            def late_root(c):
                dve.reciprocal(TA, TA)
                dve.drain().then_inc(sem("rw_varc"), 1)

            def late_out(c):
                dve.wait_ge(sem("rw_rstd"), c + 1)
                tt(YS, YS, TA, mul)
                dve.drain()
                tt(YS, YS, vec(V_LNG, 8, L), mul)
                dve.drain()
                tt(YS, YS, vec(V_LNB, 8, L), add)
                dve.drain()
                tt(YS, YS, BVL, add)
                dve.drain()
                dve.wait_ge(sem("rw_gated"), c + 1)
                tt(OT[:, 0:8, bass.ds(c * L, L)], YS, GATE, mul)
                dve.drain()

            def rwkv(c, late, ahead, sample=False):
                one = c + 1
                dve.wait_ge(sem("rw_exp"), one)
                stt(AR[:, :, 0, :], KK, -1.0, GP, mul, mul)
                tt(AR[:, :, 1, :], r, G, mul)
                dve.drain().then_inc(sem("rw_ar"), 1)
                for h in range(2):
                    q = slice(64 * h, 64 * h + 64)
                    tt(half(BBD, h), KA[q], GI[q], mul)
                    tt(half(KBD, h), K2[q], GI[q], mul)
                dve.drain().then_inc(sem("rw_ops"), 1)
                dve.tensor_copy(GLAST, G[:, :, L - 1])
                dve.wait_ge(sem("rw_scores"), c * 2 + 1)
                for k2 in range(2):
                    tt(SB[:, 4 * k2:4 * k2 + 4].rearrange("p a b c -> p a (b c)"),
                       bank(k2, 4, 128), over(M2, 4, 0, 128), mul)
                dve.drain().then_inc(sem("rw_masked"), 1)
                dve.wait_ge(sem("rw_scores"), c * 2 + 2)
                for k2 in range(2):
                    tt(SK[:, 4 * k2:4 * k2 + 4].rearrange("p a b c -> p a (b c)"),
                       bank(2 + k2, 4, 128), over(M2, 4, 0, 128), mul)
                dve.drain().then_inc(sem("rw_masked"), 1)
                dve.tensor_copy(PTT[:, :, 0, :], SB[:, :, 0, :])
                tt(PTT[:, :, 1, :], SB[:, :, 0, :], over(E, 8, 0, L), add)
                dve.wait_ge(sem("rw_p0"), one)

                def power():
                    dve.tensor_copy(PSK, b[4])
                    for h in range(2):
                        dve.tensor_copy(half(PBD, h), b[4][64 * h:64 * h + 64])

                power()
                dve.drain().then_inc(sem("rw_lv"), 1)
                for rd in range(5):
                    dve.wait_ge(sem("rw_round"), c * 6 + (rd + 1))
                    if rd:
                        tt(PTT[:, :, 1, :], PTT[:, :, 1, :], b[1], add)
                    power()
                    dve.drain().then_inc(sem("rw_lv"), 1)
                    if rd == 0 and late:
                        late_root(c - 1)
                    if rd == 1:
                        if late:
                            late_out(c - 1)
                        dve.tensor_copy(BVL, BV)
                        dve.drain().then_inc(sem("rw_late"), 1)
                    if rd == 2 and ahead:
                        front_shift(c + 1, sample)
                    if rd == 3 and ahead:
                        front_rates(c + 1)
                    if rd == 4 and ahead:
                        front_keys(c + 1)
                dve.wait_ge(sem("rw_round"), c * 6 + 6)
                for h in range(2):
                    q = slice(64 * h, 64 * h + 64)
                    tt(half(PTBD, h), b[1][q], PTT[q, :, 1, :], add)
                dve.wait_ge(sem("rw_x"), one)
                dve.tensor_copy(XS, b[5])
                dve.drain().then_inc(sem("rw_xs"), 1)
                dve.wait_ge(sem("rw_sa"), one)
                dve.tensor_copy(SAS, b[4])
                dve.drain().then_inc(sem("rw_sas"), 1)
                if ahead:
                    front_bonus(c + 1)
                dve.wait_ge(sem("rw_st"), one)
                tt(SS, SS, b[2], add)
                dve.drain()
                tt(SS, SS, GLAST.unsqueeze(2).to_broadcast([128, 8, L]), mul)
                dve.drain().then_inc(sem("rw_state"), 1)
                dve.wait_ge(sem("rw_y"), one)
                dve.tensor_copy(YS, b[0])
                dve.drain().then_inc(sem("rw_ys"), 1)
                dve.wait_ge(sem("rw_mean"), one)
                stt(YS, b[3], -1.0 / 64, YS, mul, add)
                dve.drain()
                tt(SQ, YS, YS, mul)
                dve.drain().then_inc(sem("rw_ysq"), 1)
                dve.wait_ge(sem("rw_var"), one)
                ts(TA, b[4], 1.0 / 64, 64e-5, mul, add)
                dve.drain()

            front_shift(0, None)
            front_rates(0)
            front_keys(0)
            front_bonus(0)
            rwkv(0, False, True)
            with dve.Fori(1, NPC - 1) as c:
                rwkv(c, True, True)
            nc.vector.sem_inc(sem("last_rows"), 1)
            rwkv(NPC - 1, True, True, True)
            nc.vector.sem_inc(sem("last_rows"), 1)
            dve.wait_ge(sem("state_in"), 16)
            rwkv(NPC, True, False)
            late_root(NPC)
            late_out(NPC)
            dve.wait_ge(sem("state_out"), 32)
            meet(dve, 2)
            def neg_exp_a():
                dve.wait_ge(sem("gates_ready"), 1)
                ts(NA, NA, -1.0, None, mul)

            neg_exp_a()
            dve.memset(SN, 0.0)
            dve.drain().then_inc(sem("ss_state"), 1)
            nc.vector.sem_inc(sem("rows_free"), 1)
            nc.vector.sem_inc(sem("ss_z_free"), 1)
            dve.wait_ge(sem("zeroed"), 1)

            def ssm(c):
                one = c + 1
                dve.wait_ge(sem("rows_in"), one * 32)
                ts(T1, UM, VEC[:, V_DTB:V_DTB + 1], None, add)
                dve.drain()
                stt(AB, T1, -1.0, T1, mul, mx)
                dve.drain().then_inc(sem("softplus_in"), 1)
                x = XC[:, 0:16]
                tt(x, UX[:, 0:16, 0:L], vec(V_CW, 16, L), mul)
                for k in range(1, 4):
                    tt(TMP, UX[:, 0:16, k:k + L], vec(V_CW + 24 * k, 16, L), mul)
                    dve.drain()
                    tt(x, x, TMP, add)
                    dve.drain()
                tt(x, x, vec(V_CB, 16, L), add)
                if c is NPC:
                    dve.wait_ge(sem("last_rows_out"), 48)
                dve.tensor_copy(CVO, UX[:, :, L:CW])
                dve.drain().then_inc(sem("ss_cx"), 1)
                dve.wait_ge(sem("softplus_out"), one)
                for k in range(2):
                    stt(DT2[:, k], T1, 0.0, LB, mx, add)
                dve.drain().then_inc(sem("rows_free"), 1)
                ts(T1, DT2[:, 0], NA, None, mul)
                dve.drain()
                dve.tensor_tensor_scan(AC2[:, 0], CON[:, C_RST:C_RST + L], T1, 0.0, mul, add)
                dve.drain()
                dve.tensor_copy(AC2[:, 1], AC2[:, 0])
                ts(SELL, SEL, AC2[:, 0, L - 1:L], None, mul)
                tt(RD, over(AC2[:, 0], 16, 0, L), PM.unsqueeze(2).to_broadcast([128, 16, L]), mul)
                dve.drain().then_inc(sem("ss_ac"), 1)
                dve.wait_ge(sem("ss_bc"), one)
                for h in range(2):
                    q = slice(64 * h, 64 * h + 64)
                    for out, a in ((DTS, 0), (ACS, 32), (ALS, 64)):
                        dve.tensor_copy(out[q], PS[q, 2, a + h:a + 32:2])
                dve.tensor_copy(EL, PS[:, 2, 64:96])
                dve.drain()
                tt(ALS, ALS, ACS, sub)
                tt(SEG, banks(3, 2, 16, L), ACS.unsqueeze(2).to_broadcast([128, 16, L]), sub)
                dve.drain()
                ts(SEG, SEG, 0.0, None, ALU.min)
                dve.drain().then_inc(sem("ss_seg"), 1)
                dve.wait_ge(sem("ss_xtok"), one)
                for h in range(2):
                    q = slice(64 * h, 64 * h + 64)
                    tt(half(XDBD, h), banks(0, 2, 16, L)[q], DTS[q].unsqueeze(2).to_broadcast([64, 16, L]), mul)
                dve.wait_ge(sem("ss_cb"), one)
                tt(CBM, bank(5, 4, L, n=256), over(M2[:, L:2 * L], 4, 0, L), mul)
                dve.drain()
                dve.wait_ge(sem("decays"), one)
                for g in range(4):
                    tt(SEG[:, 4 * g:4 * g + 4], SEG[:, 4 * g:4 * g + 4], over(CBM[:, g], 4, 0, L), mul)
                dve.drain().then_inc(sem("ss_mt"), 1)
                for h in range(2):
                    q = slice(64 * h, 64 * h + 64)
                    tt(half(XEBD, h), half(XDBD, h), ALS[q].unsqueeze(2).to_broadcast([64, 16, L]), mul)
                dve.wait_ge(sem("mixed"), one)
                tt(YO, banks(3, 2, 16, L), EBC, mul)
                dve.drain()
                tt(YC, banks(0, 2, 16, L), YO, add)
                dve.drain().then_inc(sem("ss_yr"), 1)
                dve.wait_ge(sem("ss_xd"), one)
                tt(YC, YC, XD, add)
                dve.drain()
                dve.wait_ge(sem("ss_z"), one)
                tt(YC, YC, UZ, mul)
                dve.drain().then_inc(sem("ss_yz"), 1)
                nc.vector.sem_inc(sem("ss_z_free"), 1)
                sn = SN.rearrange("p (h v) -> p h v", v=64)
                if c is NPC:
                    dve.wait_ge(sem("state_in"), 32)
                tt(sn, sn, EL.unsqueeze(2).to_broadcast([128, 32, 64]), mul)
                dve.drain()
                dve.wait_ge(sem("state_sums"), one)
                tt(SN, SN, banks(0, 4, 2048), add)
                dve.drain().then_inc(sem("ss_state"), 1)
                dve.wait_ge(sem("square_sums"), one)
                ts(RG, bank(5, 4, L, n=256), 1.0 / 512, 1e-5, mul, add)
                dve.drain()
                dve.reciprocal(RG, RG)
                dve.drain().then_inc(sem("variance"), 1)
                dve.wait_ge(sem("rstd"), one)
                for g in range(4):
                    tt(YC[:, 4 * g:4 * g + 4], YC[:, 4 * g:4 * g + 4], over(RG[:, g], 4, 0, L), mul)
                dve.drain()
                tt(OT[:, 16:32, bass.ds(c * L, L)], YC, vec(V_SNG, 16, L), mul)
                dve.drain()

            with dve.Fori(0, NPC) as c:
                ssm(c)
            nc.vector.sem_inc(sem("last_rows"), 1)
            ssm(NPC)
            nc.vector.sem_inc(sem("last_rows"), 1)
            dve.wait_ge(sem("state_out"), 64)
            dve.wait_ge(sem("last_rows_out"), 64)
            meet(dve, 3)

            dve.memset(SG, 0.0)
            dve.drain().then_inc(sem("gl_state"), 1)
            nc.vector.sem_inc(sem("rows_free"), 1)
            nc.vector.sem_inc(sem("gl_out"), 1)
            dve.wait_ge(sem("zeroed"), 2)

            def gla(c):
                one = c + 1
                dve.wait_ge(sem("gl_pre"), one)
                tt(T4, bank(0, 4, L, n=256), vec(V_BA, 4, L), add)
                dve.drain()
                stt(AB4, T4, -1.0, T4, mul, mx)
                dve.drain().then_inc(sem("softplus_in"), 1)
                dve.wait_ge(sem("softplus_out"), NCH + one)
                stt(T4, T4, 0.0, LB4, ALU.min, sub)
                dve.drain()
                flat = lambda x: x.rearrange("p a b -> p (a b)")
                dve.tensor_tensor_scan(flat(CS4), CON[:, C_RST:C_RST + 4 * L], flat(T4), 0.0, mul, add)
                dve.drain()
                tt(EE, CS4[:, :, L - 1:L].to_broadcast([128, 4, L]), CS4, sub)
                dve.drain().then_inc(sem("gl_cs"), 1)
                dve.wait_ge(sem("decays"), NCH + one)
                stt(QD, UG[:, 0:4], GLA_SCALE, EG, mul, mul)
                tt(KI, UG[:, 4:8], EI, mul)
                tt(KE, UG[:, 4:8], EE, mul)
                dve.drain().then_inc(sem("gl_ops"), 1)
                dve.wait_ge(sem("gl_sc"), one)
                tt(SCT[0:64], bank(0, 4, L, n=256)[0:64], M2[0:64, L:2 * L].unsqueeze(1).to_broadcast([64, 4, L]), mul)
                dve.tensor_copy(KET[0:64], bank(3, 4, 128)[0:64])
                dve.drain().then_inc(sem("gl_scm"), 1)
                nc.vector.sem_inc(sem("rows_free"), 1)
                dve.wait_ge(sem("mixed"), NCH + one)
                dve.tensor_copy(O8, bank(4, 8, L))
                dve.drain()
                tt(SQO, O8, O8, mul)
                dve.drain().then_inc(sem("squares"), 1)
                if c is NPC:
                    dve.wait_ge(sem("state_in"), 48)
                tt(SG, SG, EG[:, :, L - 1:L].to_broadcast([128, 4, 256]), mul)
                dve.drain()
                dve.wait_ge(sem("state_sums"), NCH + one)
                tt(SG, SG, banks(1, 2, 4, 256), add)
                dve.drain().then_inc(sem("gl_state"), 1)
                dve.wait_ge(sem("square_sums"), NCH + one)
                ts(RG4, bank(5, 4, L, n=256), 1.0 / 256, 1e-5, mul, add)
                dve.drain()
                dve.reciprocal(RG4, RG4)
                dve.drain().then_inc(sem("variance"), 1)
                dve.wait_ge(sem("rstd"), NCH + one)
                o4 = O8.rearrange("p (h i) b -> p h i b", i=2)
                for i in range(2):
                    tt(o4[:, :, i], o4[:, :, i], RG4, mul)
                dve.drain()
                for i in range(2):
                    ts(o4[:, :, i], o4[:, :, i], VEC[:, V_GNG + i:V_GNG + i + 1], None, mul)
                dve.drain()
                tt(OT[:, 8:16, bass.ds(c * L, L)], O8, RR, mul)
                dve.drain().then_inc(sem("gl_out"), 1)

            with dve.Fori(0, NPC) as c:
                gla(c)
            gla(NPC)
            dve.wait_ge(sem("state_out"), 96)
            meet(dve, 4)

            nc.vector.sem_inc(sem("wo_free"), 2)
            dve.wait_ge(sem("gates_ready"), 2)

            def merge(d, p):
                dve.wait_ge(sem("tile_done"), d * 4 + (NT + 4))
                b = [PS[:, 3 * p + k, 0:NTOK] for k in range(3)]
                tt(MG[:, d, :], b[0], GTF[:, d + 8, :], mul)
                tt(MTMP[:, 0], b[1], GTF[:, d, :], mul)
                tt(MTMP[:, 1], b[2], GTF[:, d + 16, :], mul)
                dve.drain()
                nc.vector.sem_inc(sem("wo_free"), 1)
                tt(MG[:, d, :], MG[:, d, :], MTMP[:, 0], add)
                dve.drain()
                tt(MG[:, d, :], MG[:, d, :], MTMP[:, 1], add)
                dve.drain().then_inc(sem("merged"), 1)

            with dve.Fori(0, 4) as d2:
                for p in range(2):
                    merge(d2 * 2 + p, p)
            dve.wait_ge(sem("ln_in"), 64)
            for t in range(TT3):
                w = 128 if t < 2 else 64
                dve.wait_ge(sem("w_out_done"), t + 1)
                stt(H0[0:w, t, :], H0[0:w, t, :], ALPHA, banks(2 * t, 2, D)[0:w], mul, add)
                dve.drain()
                layer_norm(H0, t, LN1[:, 0, :], LN1[:, 1, :], TT3 + t + 1, BN1, MV1, RS1).then_inc(sem("h_ready"), 1)
            meet(dve, 5)

            dve.memset(SCO, 0.0)
            dve.memset(CHO, 0.0)
            dve.memset(PLACE, 0.0)
            dve.drain()
            nc.vector.sem_inc(sem("score_room"), 1)
            dve.wait_ge(sem("scores"), 1)

            def choose(out, x, th, k, n):
                ts(out, x, th, None, ALU.is_gt)
                ts(TIE[:, 0:n], x, th, None, ALU.is_equal)
                dve.drain()
                dve.tensor_reduce(CNT, out, AX.X, add)
                dve.tensor_tensor_scan(TRK[:, 0:n], TIE[:, 0:n], CON[:, C_ONE:C_ONE + n], 0.0, add, mul)
                dve.drain()
                tt(TRK[:, 0:n], TRK[:, 0:n], CNT.to_broadcast([128, n]), add)
                dve.drain()
                ts(TRK[:, 0:n], TRK[:, 0:n], float(k), None, ALU.is_le)
                dve.drain()
                tt(TIE[:, 0:n], TIE[:, 0:n], TRK[:, 0:n], mul)
                dve.drain()
                tt(out, out, TIE[:, 0:n], add)
                dve.drain()

            for t in range(TT3):
                w = 128 if t < 2 else 64
                tt(SBI, SCO[:, t, :], RB, add)
                dve.drain()
                for g in range(NG):
                    dve.max(TOP[:, g, :], SBI[:, 8 * g:8 * g + 8])
                dve.drain()
                tt(GSC, TOP[:, :, 0], TOP[:, :, 1], add)
                dve.drain()
                dve.max(TOP[:, 0, :], GSC)
                dve.drain()
                choose(GM, GSC, TOP[:, 0, 3:4], 4, NG)
                ts(GM, GM, -1.0, 1e30, add, mul)
                dve.drain()
                s3 = SBI.rearrange("p (g k) -> p g k", k=8)
                tt(s3, s3, GM.unsqueeze(2).to_broadcast([128, NG, 8]), add)
                dve.drain()
                dve.max(TOP[:, 0, :], SBI)
                dve.drain()
                choose(TIE2, SBI, TOP[:, 0, 7:8], TOPK, NE)
                dve.tensor_copy(CHO[0:w, t, :], TIE2[0:w])
                dve.drain()
                tt(GTE, SCO[:, t, :], CHO[:, t, :], mul)
                dve.drain()
                dve.tensor_reduce(CNT, GTE, AX.X, add)
                dve.drain()
                ts(CNT, CNT, 1e-30, None, mx)
                dve.drain()
                dve.reciprocal(CNT, CNT)
                dve.drain()
                ts(INFO[:, t, 0:2 * NE:2], GTE, CNT, 2.5, mul, mul)
                dve.tensor_tensor_scan(TRK, CHO[:, t, :], CON[:, C_ONE:C_ONE + NE], 0.0, add, mul)
                dve.drain()
                ts(TRK, TRK, VEC[:, V_TOK8 + t:V_TOK8 + t + 1], -1.0 - SKIP, add, add)
                dve.drain()
                dve.tensor_copy(INFO[:, t, 1:2 * NE:2], TRK)
                dve.drain()
            dve.drain().then_inc(sem("chosen"), 1)
            dve.wait_ge(sem("shared_silu"), 1)
            tt(SHID, SHID, PS[:, 6:8, 0:NTOK], mul)
            dve.drain().then_inc(sem("shared_act"), 1)
            nc.vector.sem_inc(sem("shared_free"), 2)
            dve.wait_ge(sem("places"), 1)
            ts(PLACE, bank(3, 8, NE)[:, 0:3], 1.0, None, mul)
            dve.tensor_copy(CTOT, PS[:, 3, 192:192 + NE])
            ts(TIE3, CHO, -1e4, 1e4, mul, add)
            dve.drain()
            tt(PLACE, PLACE, TIE3, add)
            dve.tensor_reduce(CNT, CTOT, AX.X, mx)
            dve.drain()
            ts(CNT, CNT, float(CAP), None, ALU.is_gt)
            dve.drain()
            dve.tensor_copy(FLAG[:, :], CNT)
            dve.drain().then_inc(sem("flag"), 1)
            for t in range(TT3):
                w = 128 if t < 2 else 64
                dve.wait_ge(sem("shared_out"), t + 1)
                stt(ACC[0:w, t, :], H0[0:w, t, :], ALPHA, banks(4 + 2 * (t % 2), 2, D)[0:w], mul, add)
                dve.drain()
                nc.vector.sem_inc(sem("shared_free"), 1)
            nc.vector.sem_inc(sem("y_left"), 1)
            nc.vector.sem_inc(sem("y_right"), 1)
            nc.vector.sem_inc(sem("rows_out"), 2)

            def onehot(m, p, b):
                for t in range(TT3):
                    for i in range(2):
                        ts(OH[:, p, t, 64 * i:64 * i + 64], CON[:, C_IOTA + CAP * b:C_IOTA + CAP * b + CAP],
                           PLACE[:, t, bass.ds(m * 2 + i, 1)], None, ALU.is_equal)
                dve.drain().then_inc(sem("onehot"), 1)

            def x_step(n, p):
                dve.wait_ge(sem("x_done"), n + 1)
                dve.wait_ge(sem("rows_out"), n + 1)
                dve.tensor_copy(XE[:, 4:8], bank(1, 4, 128))
                for i in range(2):
                    q = slice(64 * i, 64 * i + 64)
                    dve.tensor_copy(GA[q, p:p + 1], PS[q, 4, 2 * i:2 * i + 1])
                    ts(IDX[q, p:p + 1], PS[q, 4, 2 * i + 1:2 * i + 2], float(SKIP), None, add)
                dve.drain().then_inc(sem("x_right"), 1)

            def hid_step(n):
                dve.wait_ge(sem("silu_ready"), n + 1)
                tt(HID, SIL, PS[:, 2, 256:512], mul)
                dve.drain().then_inc(sem("hid_ready"), 1)

            def y_step(n, p):
                dve.wait_ge(sem("pair_done"), n + 1)
                ts(Y[:, p, 0:512], PS[:, 5, :], GA[:, p:p + 1], None, mul)
                dve.drain().then_inc(sem("y_left"), 1)

            onehot(0, 0, 0)
            onehot(1, 1, 0)
            x_step(0, 0)

            def steady(n, p, more=True):
                hid_step(n)
                if more:
                    x_step(n + 1, 1 - p)
                    onehot(n + 2, p, 0)
                y_step(n, p)

            with dve.Fori(0, NE // 4 - 1) as m:
                for p in range(2):
                    steady(m * 2 + p, p)
            hid_step(NE // 2 - 2)
            x_step(NE // 2 - 1, 1)
            y_step(NE // 2 - 2, 0)
            steady(NE // 2 - 1, 1, False)
            with overflow(dve):
                with dve.Fori(0, NE // 2) as m:
                    for b in range(NBLK - 1):
                        n = m * (NBLK - 1) + (NE // 2 + b)
                        onehot(m, b % 2, b + 1)
                        x_step(n, b % 2)
                        steady(n, b % 2, False)
            dve.wait_ge(sem("ln_in"), 96)
            for t in range(TT3):
                w = 128 if t < 2 else 64
                dve.wait_ge(sem(f"slots_in{t % 2}"), 16 * (t // 2 + 1))
                rw = ROWS[0:w, t % 2]
                for k in (4, 2, 1):
                    tt(rw[:, 0:k], rw[:, 0:k], rw[:, k:2 * k], add)
                    dve.drain()
                tt(ACC[0:w, t, :], ACC[0:w, t, :], rw[:, 0], add)
                dve.drain().then_inc(sem("rows_summed"), 1)
                layer_norm(ACC, t, LN2[:, 0, :], LN2[:, 1, :], 2 * TT3 + t + 1, BN2, MV2, RS2, w).then_inc(sem("y_ready"), 1)

        @block.gpsimd
        def _(pool):
            meet(pool, 1)
            meet(pool, 2)
            for x in (XTBD, XDBD, XEBD):
                pool.memset(x, 0.0)
            pool.drain().then_inc(sem("zeroed"), 1)
            nc.gpsimd.sem_inc(sem("ss_free_pool"), 1)

            def ssm(c):
                one = c + 1
                pool.wait_ge(sem("ss_bcs"), one)
                pool.wait_ge(sem("rows_in"), one * 32)
                x = XC[:, 16:24]
                def w(k):
                    return VEC[:, V_CW + 24 * k + 16:V_CW + 24 * k + 24].unsqueeze(2).to_broadcast([128, 8, L])
                pool.tensor_tensor(x, UX[:, 16:24, 0:L], w(0), ALU.mult)
                for k in range(1, 4):
                    pool.tensor_tensor(TMP2, UX[:, 16:24, k:k + L], w(k), ALU.mult)
                    pool.drain()
                    pool.tensor_tensor(x, x, TMP2, ALU.add)
                    pool.drain()
                pool.tensor_tensor(x, x, vec(V_CB + 16, 8, L), ALU.add)
                pool.drain().then_inc(sem("ss_cbc"), 1)
                nc.gpsimd.sem_inc(sem("ss_free_pool"), 1)
                pool.wait_ge(sem("ss_xs"), one)
                pool.tensor_tensor(XD, XS_, vec(V_DSK, 16, L), ALU.mult)
                pool.drain().then_inc(sem("ss_xd"), 1)

            with pool.Fori(0, NCH) as c:
                ssm(c)
            meet(pool, 3)
            for x in (VT, SCT, KET):
                pool.memset(x, 0.0)
            pool.drain().then_inc(sem("zeroed"), 1)
            meet(pool, 4)
            meet(pool, 5)

            last_slot = pool.to_reg(SLOTS - 1)

            def scatter(m, p):
                pool.wait_ge(sem("y_left"), m * 2 + (p + 2))
                pool.wait_ge(sem("y_right"), m * 2 + (p + 2))
                nc.gpsimd.sem_inc(sem("rows_taken"), 1)
                pool.indirect_dma_start(slots[:, :], bass.IndirectOffsetOnAxis(ap=IDX[:, p:p + 1], axis=0),
                                        Y[:, p, :], None, bounds_check=last_slot, oob_is_err=False
                                        ).then_inc(sem(f"rows_sent{p}"), 16)
                pool.wait_ge(sem(f"rows_sent{p}"), m * 16 + 16)
                nc.gpsimd.sem_inc(sem("rows_out"), 1)

            with pool.Fori(0, NE // 4) as m:
                for p in range(2):
                    scatter(m, p)
            with overflow(pool):
                with pool.Fori(NE // 4, NE // 4 * NBLK) as m:
                    for p in range(2):
                        scatter(m, p)
            pool.drain().then_inc(sem("rows_over"), 1)


def _tiles(w, ncol):
    import numpy as np
    k, n = w.shape
    return w.reshape(k // 128, 128, n // ncol, ncol).transpose(2, 1, 0, 3)


def _cols(v):
    return v.reshape(-1, 128).T


def _constants():
    import numpy as np
    c = np.zeros((128, NC), np.float32)
    p = np.arange(128)
    s = p % 64
    t = np.arange(64)
    c[:, C_ID:C_ID + 128] = np.eye(128)
    c[:, C_ONE:C_ONE + 128] = 1.0
    c[:, C_BLK:C_BLK + 128] = (p[:, None] // 64) == (p[None] // 64)
    c[:, C_M2:C_M2 + 64] = t[None] > s[:, None]
    c[:, C_M2 + 64:C_M2 + 128] = t[None] >= s[:, None]
    c[:, C_ML:C_ML + 64] = t[None] < s[:, None]
    c[:, C_E:C_E + 64] = t[None] == s[:, None]
    c[:, C_RST:C_RST + 512] = np.arange(512) % 64 != 0
    h = np.arange(32)
    c[32:64, C_LH:C_LH + 128] = (h[:, None] % 2) == (p[None] // 64)
    c[32:64, C_PM:C_PM + 16] = (h[:, None] // 2) == np.arange(16)[None]
    c[32:64, C_SEL:C_SEL + 32] = np.eye(32)
    c[:, C_TRI:C_TRI + 128] = p[:, None] < p[None]
    c[:, C_IOTA:C_IOTA + NTOK] = np.arange(NTOK)
    return c


def _layout(i):
    import numpy as np
    f = np.float32
    g = {k: np.asarray(v)[0] if k not in ('x_prompt', 'x_sample', 'ln_in_g', 'ln_in_b') else np.asarray(v)
         for k, v in i.items()}
    a = {}
    x = np.zeros((384, D), f)
    x[:256] = g['x_prompt'][0]
    x[256:320] = g['x_sample'][0]
    a['x'] = x.reshape(3, 128, D)
    w = g['w_in']
    wp = np.zeros((D, NT * 128), f)
    place = [(T_RW, 6160, 3328), (T_XBC, 11536, 3072), (T_Z, 9488, 2048), (T_GLA, 3072, 3072), (T_GATE, 0, 3072)]
    for tile, col, n in place:
        wp[:, tile * 128:tile * 128 + n] = w[:, col:col + n]
    wp[:, T_MISC * 128:T_MISC * 128 + 16] = w[:, 6144:6160]
    wp[:, T_MISC * 128 + 32:T_MISC * 128 + 64] = w[:, 14608:14640]
    a['w_in'] = np.ascontiguousarray(_tiles(wp, 128))
    hist = np.zeros((128, NT, 2, HIST), f)
    hist[:, T_RW:T_RW + 26, 1, 2] = _cols(g['state_rwkv_shift'][0, 0])
    for k in range(3):
        hist[:, T_XBC:T_XBC + 24, 1, k] = _cols(g['state_ssm_conv'][0, k])
    a['hist'] = hist
    v = np.zeros((128, NV), f)
    for at, name in ((V_MU, 'rwkv_mu'), (V_W0, 'rwkv_w0'), (V_A0, 'rwkv_a0'), (V_KK, 'rwkv_k_k'), (V_KA, 'rwkv_k_a'),
                     (V_RK, 'rwkv_r_k'), (V_LNG, 'rwkv_ln_g'), (V_LNB, 'rwkv_ln_b'), (V_BA, 'gla_ba'),
                     (V_GNG, 'gla_norm_g'), (V_CB, 'ssm_conv_b'), (V_SNG, 'ssm_norm_g')):
        c = _cols(g[name])
        v[:, at:at + c.shape[1]] = c
    for k in range(4):
        v[:, V_CW + 24 * k:V_CW + 24 * k + 24] = _cols(g['ssm_conv_w'][k])
    d = g['ssm_d'].reshape(16, 2).T
    v[0:64, V_DSK:V_DSK + 16] = d[0]
    v[64:128, V_DSK:V_DSK + 16] = d[1]
    v[32:64, V_DTB] = g['ssm_dt_bias']
    v[32:64, V_ALOG] = g['ssm_a_log']
    for k in range(3):
        v[:, V_TOK8 + k] = 8.0 * (np.arange(128) + 128 * k)
    a['vecs'] = v
    a['consts'] = _constants()
    sm = np.zeros((128, 3 * D + 512), f)
    sm[0:64, 0:D] = g['rwkv_w2']
    sm[64:128, D:2 * D] = g['rwkv_a2']
    sm[:, 2 * D:3 * D] = g['rwkv_g2']
    sm[0:16, 3 * D:] = g['gla_wa2']
    a['small_w'] = sm
    wo = np.zeros((8, 4, 128, 8, 128), f)
    wo[:, 0] = _tiles(g['rwkv_wo'], 128)
    wo[:, 1] = _tiles(g['gla_wo'], 128)
    wo[:, 2] = _tiles(g['ssm_wo'][:D], 128)
    wo[:, 3] = _tiles(g['ssm_wo'][D:], 128)
    a['wo'] = wo
    a['w_out'] = np.ascontiguousarray(_tiles(g['w_out'], D)[0])
    a['lnv'] = np.stack([g[k] for k in ('ln_in_g', 'ln_in_b', 'ln1_g', 'ln1_b', 'ln2_g', 'ln2_b')])
    a['w_router'] = np.ascontiguousarray(_tiles(g['w_router'], NE)[0])
    a['router_bias'] = g['router_bias'].reshape(1, NE)

    def expert(w1, w3, w2):
        e = np.empty((128, 6144), f)
        b = e[:, 0:4096].reshape(128, KT, 512)
        b[:, :, 0:256] = _tiles(w1, 256)[0]
        b[:, :, 256:512] = _tiles(w3, 256)[0]
        e[:, 4096:] = _tiles(w2, D)[0].reshape(128, 2 * D)
        return e

    m = np.empty((NE + 1, 128, 6144), f)
    for e in range(NE):
        m[e] = expert(g['exp_w1'][e], g['exp_w3'][e], g['exp_w2'][e])
    m[NE] = expert(g['sh_w1'], g['sh_w3'], g['sh_w2'])
    a['moe_w'] = m
    s = g['state_rwkv'][0].reshape(8, 2, 64, 64)
    a['st_rwkv'] = np.ascontiguousarray(s.transpose(1, 3, 0, 2).reshape(128, 8, 64))
    a['st_gla'] = np.ascontiguousarray(g['state_gla'][0].transpose(1, 0, 2))
    a['st_ssm'] = np.ascontiguousarray(g['state_ssm'][0].transpose(2, 0, 1)).reshape(128, 2048)
    return {k: np.ascontiguousarray(z, dtype=f) for k, z in a.items()}


_OUTS = [('y', (3, 128, D)), ('gla', (2, 128, 4, 256)), ('rwkv', (2, 128, 8, 64)), ('shift', (2, 128, 26)),
         ('ssm', (2, 128, 2048)), ('conv', (2, 128, 24, 3))]


def kernel(**inputs):
    import numpy as _np
    import concourse.bacc as _bacc
    from concourse import mybir as _mybir
    from concourse.bass_utils import run_bass_kernel_spmd as _run

    nc = _bacc.Bacc("TRN2", target_bir_lowering=False, num_devices=1)
    a = _layout(inputs)
    io = {k: nc.dram_tensor(k, v.shape, _mybir.dt.from_np(v.dtype), kind="ExternalInput").ap() for k, v in a.items()}
    for n, s in _OUTS:
        io['out_' + n] = nc.dram_tensor('out_' + n, s, _mybir.dt.float32, kind="ExternalOutput").ap()
    hybrid_layer(nc, io)
    r = _run(nc, [a], core_ids=[0]).results[0]
    y = r['out_y'].reshape(384, D)
    gla = r['out_gla'].transpose(0, 2, 1, 3)
    rw = r['out_rwkv'].reshape(2, 2, 64, 8, 64).transpose(0, 3, 1, 4, 2).reshape(2, 16, 64, 64)
    sh = r['out_shift'].transpose(0, 2, 1).reshape(2, 3328)
    ss = r['out_ssm'].reshape(2, 128, 32, 64).transpose(0, 2, 3, 1)
    cv = r['out_conv'].transpose(0, 3, 2, 1).reshape(2, 3, 3072)
    c = _np.ascontiguousarray

    def states(s):
        return (c(gla[s])[None, None], c(rw[s])[None, None], c(sh[s])[None, None, None], c(ss[s])[None, None],
                c(cv[s])[None, None])

    return (c(y[:256])[None], c(y[256:320])[None]) + states(0) + states(1)
```

```python
import concourse.bass as bass
from concourse import mybir
from contextlib import ExitStack, contextmanager

FP32 = mybir.dt.float32
I32 = mybir.dt.int32
ALU = mybir.AluOpType
ACT = mybir.ActivationFunctionType
AX = mybir.AxisListType

D = 1024
KT = D // 128
NTOK = 320
TT3 = 3
L = 64
NCH = NTOK // L
NPC = NCH - 1
HIST = 3
CW = HIST + L

T_RW = 0
T_MISC = 26
T_XBC = 27
T_Z = 51
T_GLA = 67
T_GATE = 91
NT = 115
RING = 4
PRE = 28
HEAD_R, FILL = 4, 8
HEAD_S, FILL_S = 4, 4
HEAD_G, FILL_G = 3, 4
N_RW = PRE + HEAD_R
N_S0 = N_RW + NCH * FILL
N_SSM = N_S0 + HEAD_S
N_G0 = N_SSM + NCH * FILL_S
N_GLA = N_G0 + HEAD_G
assert N_GLA + NPC * FILL_G == NT and N_S0 >= T_GLA and N_G0 >= T_GATE

V_MU, V_W0, V_A0, V_KK, V_KA, V_RK, V_LNG, V_LNB = 0, 26, 34, 42, 50, 58, 66, 74
V_BA, V_GNG, V_CW, V_CB, V_SNG, V_DSK, V_DTB, V_ALOG, V_TOK8 = 82, 86, 88, 184, 208, 224, 240, 241, 242
NV = 245

C_ID, C_ONE, C_BLK, C_M2, C_ML, C_E, C_RST, C_LH, C_PM, C_SEL, C_TRI, C_IOTA = (
    0, 128, 256, 384, 512, 576, 640, 1152, 1280, 1296, 1328, 1456)
NC = 1456 + NTOK

DECAY = 0.6065306597126334
GLA_SCALE = 128 ** -0.5
ALPHA = 2.0 ** 0.25
NE, TOPK, NG, DE = 64, 8, 8, 256
CAP = 64
NBLK = NTOK // CAP
SLOTS = NTOK * TOPK
MIX_ORDER = (0, 2, 3, 1)
STEP_ORDER = (0, 2, 1, 3)
MERGE_BANKS = ((0, 1, 2, 2), (3, 5, 4, 4))


def hybrid_layer(nc, io):
    ctx = ExitStack()
    with ctx:
        sems = {}

        def sem(name):
            if name not in sems:
                sems[name] = ctx.enter_context(nc.semaphore(name))
            return sems[name]

        ut = nc.dram_tensor("projected", (NT, 128, NCH, CW), FP32, kind="Internal").ap()
        slots = nc.dram_tensor("expert_rows", (SLOTS, D), FP32, kind="Internal").ap()
        PS = ctx.enter_context(nc.psum_tensor("PS", [128, 8, 512], FP32))

        def sb(name, *shape):
            return ctx.enter_context(nc.sbuf_tensor(name, [128, *shape], FP32))

        CON = sb("constants", NC)
        VEC = sb("feature_vectors", NV)
        HISTS = sb("history", NT, 2, HIST)
        H0 = sb("h0", TT3, D)
        H0T = sb("h0T", KT, NTOK)
        REGION = sb("region", 53100 - (NC + NV + NT * 6 + TT3 * D + KT * NTOK))
        ID, ONE, BLK = (CON[:, c:c + 128] for c in (C_ID, C_ONE, C_BLK))
        M2, ML, E = CON[:, C_M2:C_M2 + 128], CON[:, C_ML:C_ML + 64], CON[:, C_E:C_E + 64]
        LH, PM, SEL, TRI = (CON[:, a:a + n] for a, n in ((C_LH, 128), (C_PM, 16), (C_SEL, 32), (C_TRI, 128)))
        at = [0]

        def size(shape):
            n = 1
            for k in shape:
                n *= k
            return n

        def take(*shape):
            n = size(shape)
            v = REGION[:, at[0]:at[0] + n]
            at[0] += n
            return shaped(v, *shape)

        def shaped(v, *shape):
            names = "abcd"[:len(shape)]
            if len(shape) <= 1:
                return v
            return v.rearrange(f"p ({' '.join(names)}) -> p {' '.join(names)}",
                               **{k: s for k, s in zip(names[1:], shape[1:])})

        def vec(a, n, w):
            return VEC[:, a:a + n].unsqueeze(2).to_broadcast([128, n, w])

        def over(ap, n, m, w):
            return ap.unsqueeze(1).to_broadcast([128, n, w])

        def half(ap, h):
            return ap[64 * h:64 * h + 64, :, 64 * h:64 * h + 64]

        def bank(b, *shape, n=512):
            return shaped(PS[:, b, 0:n], *shape)

        def banks(b, k, *shape):
            v = PS[:, b:b + k, :].rearrange("p b n -> p (b n)")
            return shaped(v, *shape)

        WR = take(RING, KT, 128)
        STG = take(RING, NCH, CW)
        OT = take(32, NTOK)
        mixer_base = at[0]

        UR, US = take(26, L + 1), take(26, L)
        LOW, GS = take(L), take(L)
        (WS, AS, CS, GP, G, GI, KK, SQ, K2, KA, TA, BQ, BV, YS) = (take(8, L) for _ in range(14))
        AR = take(8, 2, L)
        ABD, BBD, KBD, VBD, PBD, PTBD, AKBD, SBD, SABD = (take(8, 128) for _ in range(9))
        VS, PSK, XS, SAS, SS = (take(8, L) for _ in range(5))
        SB, SK = take(8, 2, L), take(8, 2, L)
        PTT = take(8, 2, L)
        SHO, GLAST, GSL = take(26), take(8), take(L)
        GATE, BVL = take(8, L), take(8, L)
        assert at[0] <= REGION.shape[1], at[0]
        W2P, A2P, G2 = (OT[:, 16:].rearrange("p a b -> p (a b)")[:, k * D:k * D + D] for k in range(3))

        at[0] = mixer_base
        UX, UZ, UM = take(24, CW), take(16, L), take(L)
        XC, TMP2, XS_, XD = take(24, L), take(12, L), take(16, L), take(16, L)
        XTBD, XDBD, XEBD = take(16, 128), take(16, 128), take(16, 128)
        BT2, CT, BTM, CBM = take(4, 2, L), take(4, L), take(4, 128), take(4, L)
        T1, AB, LB, DT2, AC2, SELL = take(L), take(L), take(L), take(2, L), take(2, L), take(32)
        DTS, ACS, ALS, EL, NA = take(16), take(16), take(16), take(32), take(1)
        RD, SEG, EBC, YO, YC, SN = take(16, L), take(16, L), take(16, L), take(16, L), take(16, L), take(2048)
        RG, CVO = take(4, L), take(24, HIST)
        assert at[0] <= REGION.shape[1], at[0]

        at[0] = mixer_base
        UG, UA, WA2 = take(24, L), take(L), take(512)
        T4, AB4, LB4, CS4, EG, EI, EE, QD, KI, KE, SCT, RG4 = (take(4, L) for _ in range(12))
        VT, KET, SG, O8, SQO, RR = take(8, 128), take(4, 128), take(4, 256), take(8, L), take(8, L), take(8, L)

        mixer_end = at[0]

        at[0] = mixer_base
        GT = take(24, NCH, L)
        GTF = GT.rearrange("p t c w -> p t (c w)")
        EW = shaped(REGION[:, 0:24576], 2, 12288)
        W13 = [shaped(EW[:, p, 0:8192], 2, 4096) for p in range(2)]
        W2 = [shaped(EW[:, p, 8192:12288], 2, 2048) for p in range(2)]
        at[0] = mixer_end
        assert mixer_base + 24 * NTOK <= mixer_end and 24576 <= mixer_end
        WRT, RB, SCO, CHO, PLACE, TIE3 = take(KT, NE), take(NE), take(3, NE), take(3, NE), take(3, NE), take(3, NE)
        SBI, TIE, TIE2, TRK, GTE, CTOT = (take(NE) for _ in range(6))
        TOP, GSC, GM, CNT, FLAGW = take(NG, 8), take(8), take(8), take(1), take(1)
        INFO, OH, XE = take(3, 2 * NE), take(2, 3, 128), take(KT, 128)
        SIL, HID, HIDT, SHID, GA = take(256), take(256), take(2, 128), take(2, NTOK), take(2)
        LN1, BN1, MV1, RS1 = take(2, D), take(3, 2, 6), take(3, 2), take(3)
        late = at[0]
        MG, MTMP, WOUT = take(8, NTOK), take(2, NTOK), take(KT, D)
        assert at[0] <= REGION.shape[1], at[0]
        at[0] = late
        Y, ACC, LN2, BN2, MV2, RS2 = take(2, D), take(3, D), take(2, D), take(3, 2, 6), take(3, 2), take(3)
        assert at[0] <= REGION.shape[1], at[0]
        IDX = ctx.enter_context(nc.sbuf_tensor("row_index", [128, 2], I32))
        FLAG = ctx.enter_context(nc.sbuf_tensor("overflow", [128, 1], I32))
        ROWS = shaped(REGION[:, 0:24576], TT3, TOPK, D)
        SKIP = 4096

        def convolve(e, k, tmp):
            n = k.stop - k.start
            x = XC[:, k]
            for i in range(4):
                e.tensor_tensor(tmp if i else x, UX[:, k, i:i + L], vec(V_CW + 24 * i + k.start, n, L), ALU.mult)
                e.drain()
                if i:
                    e.tensor_tensor(x, x, tmp, ALU.add)
                    e.drain()
            e.tensor_tensor(x, x, vec(V_CB + k.start, n, L), ALU.add)

        def sum_rows(e, t, w, cols):
            rw = ROWS[0:w, t, :, cols]
            for k in (4, 2, 1):
                e.tensor_tensor(rw[:, 0:k], rw[:, 0:k], rw[:, k:2 * k], ALU.add)
                e.drain()
            e.tensor_tensor(ACC[0:w, t, cols], ACC[0:w, t, cols], rw[:, 0], ALU.add)
            return e.drain()

        def mixer_loads(q):
            return (NT + RING - 1 - q) // RING + 8

        @contextmanager
        def overflow(e):
            e.wait_ge(sem("flag"), 1)
            more = e.value_load(FLAG[0:1, 0:1], min_val=0, max_val=1)
            with e.If(more > 0):
                yield

        LNB = shaped(REGION[:, mixer_base:mixer_base + 2 * D], 2, D)
        BN = shaped(REGION[:, mixer_base + 2 * D:mixer_base + 2 * D + 36], 3, 2, 6)
        MV = shaped(REGION[:, mixer_base + 2 * D + 36:mixer_base + 2 * D + 42], 3, 2)
        RS = REGION[:, mixer_base + 2 * D + 42:mixer_base + 2 * D + 45]
        MIX = REGION[:, mixer_base:]

        block = ctx.enter_context(nc.Block())
        ENG = 4

        def meet(e, k):
            e.drain().then_inc(sem("phase_over"), 1)
            e.wait_ge(sem("phase_over"), ENG * k)

        @block.sync
        def _(sp):
            x = io['x'].rearrange("t p d -> p t d")
            sp.dma_start(H0[:, 0, :], x[:, 0, :]).then_inc(sem("x_first"), 16)
            for k in range(2):
                sp.dma_start(LNB[:, k, :], io['lnv'][k:k + 1, :].to_broadcast([128, D])).then_inc(sem("ln_in"), 16)
            sp.dma_start(H0[:, 1:, :], x[:, 1:, :]).then_inc(sem("x_rest"), 16)
            sp.dma_start(CON[:, :], io['consts']).then_inc(sem("consts_in"), 16)

            def weights(m, i, first=False):
                n = m * RING + i
                if not first:
                    sp.wait_ge(sem("tile_done"), n - RING + 1)
                sp.dma_start(WR[:, i, :, :], io['w_in'][n, :, :, :]).then_inc(sem(f"weights_in{i}"), 16)

            for i in range(RING):
                weights(0, i, first=True)
            sp.dma_start(VEC[:, :], io['vecs']).then_inc(sem("vectors_in"), 16)
            sp.dma_start(HISTS[:, :, :, :], io['hist']).then_inc(sem("vectors_in"), 16)
            for k, t in enumerate((W2P, A2P, G2)):
                sp.dma_start(t, io['small_w'][:, k * D:k * D + D]).then_inc(sem("small_w_in"), 16)
            with sp.Fori(1, PRE // RING) as m:
                for i in range(RING):
                    weights(m, i)

            for n in range(PRE, N_RW):
                weights(n // RING, n % RING)

            for i in range(RING):
                sp.wait_ge(sem(f"store_done{i}"), 16 * (PRE // RING + 1))

            def chunk_rows(c):
                sp.wait_ge(sem("rw_ur_free"), c + 1)
                sp.dma_start(UR, ut[0:26, :, c, 2:CW].rearrange("t p w -> p t w")).then_inc(sem("rw_ur_in"), 16)

            def fill_weights(c, fs):
                for f in fs:
                    weights(c * (FILL // RING) + (N_RW + f) // RING, (N_RW + f) % RING)

            def state_out(s):
                sp.wait_ge(sem("rw_state"), NPC + 1 + s)
                sp.dma_start(io['out_rwkv'][s], SS).then_inc(sem("state_out"), 16)
                sp.wait_ge(sem("state_out"), 16 * (s + 1))

            def shift_out(s):
                sp.wait_ge(sem("last_rows"), 1 + s)
                sp.dma_start(io['out_shift'][s], SHO).then_inc(sem("last_rows_out"), 16)

            chunk_rows(0)
            with sp.Fori(0, NPC - 1) as c:
                chunk_rows(c + 1)
                fill_weights(c, range(FILL))
            shift_out(0)
            chunk_rows(NPC)
            fill_weights(NPC - 1, range(FILL))
            fill_weights(NPC, range(RING))
            state_out(0)
            sp.dma_start(SS, io['st_rwkv']).then_inc(sem("state_in"), 16)
            fill_weights(NPC, range(RING, FILL))

            def conv_rows(c):
                sp.wait_ge(sem("ss_free_pool"), c + 1)
                sp.dma_start(UX, ut[T_XBC:T_XBC + 24, :, c, :].rearrange("t p w -> p t w")).then_inc(sem("conv_in"), 16)

            def dt_rows(c):
                sp.wait_ge(sem("rows_free"), c + 1)
                sp.dma_start(UM, ut[T_MISC, :, c, HIST:CW]).then_inc(sem("rows_in"), 16)

            for i in range(RING):
                sp.wait_ge(sem(f"store_done{i}"), 16 * ((T_XBC + 24) // RING + 2))
            sp.wait_ge(sem("rw_ur_free"), NCH + 1)
            conv_rows(0)
            sp.wait_ge(sem("rw_ops"), NCH)
            sp.wait_ge(sem("rw_vbd"), NCH)
            dt_rows(0)
            for n in range(N_S0, N_S0 + HEAD_S // 2):
                weights(n // RING, n % RING)
            state_out(1)
            shift_out(1)
            sp.wait_ge(sem("last_rows_out"), 32)
            for n in range(N_S0 + HEAD_S // 2, N_SSM):
                weights(n // RING, n % RING)
            for i in range(RING):
                sp.wait_ge(sem(f"store_done{i}"), 16 * (N_S0 // RING + 1))

            def z_rows(c):
                sp.wait_ge(sem("ss_z_free"), c + 1)
                sp.dma_start(UZ, ut[T_Z:T_Z + 16, :, c, HIST:CW].rearrange("t p w -> p t w")).then_inc(sem("ss_z_in"), 16)

            def ssm_weights(c):
                for f in range(FILL_S):
                    weights(c * (FILL_S // RING) + (N_SSM + f) // RING, (N_SSM + f) % RING)

            def ssm_out(s):
                sp.wait_ge(sem("ss_state"), (NPC if s == 0 else NCH) + 1)
                sp.dma_start(io['out_ssm'][s], SN).then_inc(sem("state_out"), 16)
                sp.wait_ge(sem("state_out"), 32 + 16 * (s + 1))

            def conv_out(s):
                sp.wait_ge(sem("last_rows"), 3 + s)
                sp.dma_start(io['out_conv'][s], CVO).then_inc(sem("last_rows_out"), 16)

            with sp.Fori(0, NPC - 1) as c:
                z_rows(c)
                ssm_weights(c)
                conv_rows(c + 1)
                dt_rows(c + 1)
            z_rows(NPC - 1)
            conv_out(0)
            conv_rows(NPC)
            ssm_weights(NPC - 1)
            dt_rows(NPC)
            z_rows(NPC)
            ssm_weights(NPC)
            ssm_out(0)
            sp.dma_start(SN, io['st_ssm']).then_inc(sem("state_in"), 16)
            ssm_out(1)
            conv_out(1)
            sp.wait_ge(sem("last_rows_out"), 64)
            for n in range(N_G0, N_GLA):
                weights(n // RING, n % RING)

            sp.wait_ge(sem("phase_over"), ENG * 3)
            sp.dma_start(WA2, io['small_w'][:, 3 * D:3 * D + 512]).then_inc(sem("small_w_in"), 16)
            for i in range(RING):
                sp.wait_ge(sem(f"store_done{i}"), 16 * ((N_G0 + RING - 1 - i) // RING + 1))

            def gla(c):
                sp.wait_ge(sem("rows_free"), c + (NCH + 2))
                sp.dma_start(UA, ut[T_MISC, :, c, HIST:CW]).then_inc(sem("rows_in"), 16)
                sp.wait_ge(sem("gate_silu"), c + NCH)
                sp.dma_start(UG, ut[T_GLA:T_GLA + 24, :, c, HIST:CW].rearrange("t p w -> p t w")).then_inc(sem("rows_in"), 16)
                for f in range(FILL_G if c is not NPC else 0):
                    weights(c * (FILL_G // RING) + (N_GLA + f) // RING, (N_GLA + f) % RING)

            def gla_out(s):
                sp.wait_ge(sem("gl_state"), (NPC if s == 0 else NCH) + 1)
                sp.dma_start(io['out_gla'][s], SG).then_inc(sem("state_out"), 16)
                sp.wait_ge(sem("state_out"), 64 + 16 * (s + 1))

            with sp.Fori(0, NPC) as c:
                gla(c)
            gla(NPC)

            def mixer_weights(d, q, done):
                sp.wait_ge(sem("tile_done"), done)
                sp.dma_start(WR[:, q, :, :], io['wo'][d, q, :, :, :]).then_inc(sem(f"weights_in{q}"), 16)

            mixer_weights(0, 0, NT)
            gla_out(0)
            sp.dma_start(SG, io['st_gla']).then_inc(sem("state_in"), 16)
            for q in MIX_ORDER[1:]:
                mixer_weights(0, q, NT)
            for k, q in enumerate(MIX_ORDER[:3]):
                mixer_weights(1, q, NT + 1 + k)
            sp.dma_start(WOUT, io['w_out']).then_inc(sem("w_out_in"), 16)
            for k in range(2):
                sp.dma_start(LN1[:, k, :], io['lnv'][2 + k:3 + k, :].to_broadcast([128, D])).then_inc(sem("ln_in"), 16)
            gla_out(1)

            sp.wait_ge(sem("phase_over"), ENG * 4)
            for i in range(RING):
                sp.wait_ge(sem(f"store_done{i}"), 16 * ((NT + RING - 1 - i) // RING + 1))
            def gates(d, p):
                for g in range(3):
                    sp.dma_start(GT[:, 8 * g + d, :, :], ut[T_GATE + 8 * g + d, :, :, HIST:CW]).then_inc(sem(f"gates_in{p}"), 16)

            def merge_weights(d, of):
                for q in of:
                    k = STEP_ORDER.index(q)
                    mixer_weights(d + (q != 1), q, d * 4 + (NT + k))

            def merge_loads(d, p):
                sp.wait_ge(sem("gates_ready"), d)
                gates(d, p)
                merge_weights(d, STEP_ORDER)

            gates(0, 0)
            merge_weights(1, STEP_ORDER[:2])
            gates(1, 1)
            merge_weights(1, STEP_ORDER[2:])
            with sp.Fori(1, 3) as d2:
                for p in range(2):
                    merge_loads(d2 * 2 + p, p)
            merge_loads(6, 0)
            sp.wait_ge(sem("gates_ready"), 7)
            gates(7, 1)
            merge_weights(7, (1,))

            sp.dma_start(WRT, io['w_router']).then_inc(sem("router_in"), 16)
            sp.dma_start(RB, io['router_bias'].to_broadcast([128, NE])).then_inc(sem("router_in"), 16)
            sp.wait_ge(sem("merged"), 8)
            sp.dma_start(W13[1][:, 1, :], io['moe_w'][NE, :, 0:4096]).then_inc(sem("shared_in"), 16)
            sp.dma_start(W2[1][:, 1, :], io['moe_w'][NE, :, 4096:6144]).then_inc(sem("shared_in"), 16)

            def up_weights(e, p, i):
                sp.dma_start(W13[p][:, i, :], io['moe_w'][e, :, 0:4096]).then_inc(sem(f"weights_in{p}"), 16)

            def down_weights(e, p, i):
                sp.dma_start(W2[p][:, i, :], io['moe_w'][e, :, 4096:6144]).then_inc(sem(f"weights_in{2 + p}"), 16)

            for e in range(4):
                if e == 3:
                    sp.wait_ge(sem("w_out_done"), TT3)
                    for k in range(2):
                        sp.dma_start(LN2[:, k, :], io['lnv'][4 + k:5 + k, :].to_broadcast([128, D])).then_inc(sem("ln_in"), 16)
                    sp.wait_ge(sem("shared_used"), 1)
                up_weights(e, e // 2, e % 2)
                down_weights(e, e // 2, e % 2)
            with sp.Fori(1, NE // 4) as m:
                for p in range(2):
                    sp.wait_ge(sem("hid_done"), m * 2 + (p - 1))
                    for i in range(2):
                        up_weights(m * 4 + (2 * p + i), p, i)
                    sp.wait_ge(sem("pair_done"), m * 2 + (p - 1))
                    for i in range(2):
                        down_weights(m * 4 + (2 * p + i), p, i)
            sp.wait_ge(sem("pair_done"), NE // 2)
            with overflow(sp):
                with sp.Fori(0, NE // 2) as m:
                    sp.wait_ge(sem("pair_done"), m * (NBLK - 1) + NE // 2)
                    for i in range(2):
                        up_weights(m * 2 + i, 0, i)
                        down_weights(m * 2 + i, 0, i)
            sp.wait_ge(sem("rows_over"), 1)
            for t in range(TT3):
                w = 128 if t < 2 else 64
                sp.dma_start(ROWS[0:w, t, :, :], slots[t * 1024:t * 1024 + w * 8, :].rearrange("(p k) d -> p k d", k=8)
                             ).then_inc(sem(f"slots_in{t}"), 16)
            for t in range(TT3):
                sp.wait_ge(sem("y_ready"), t + 1)
                w = 128 if t < 2 else 64
                sp.dma_start(io['out_y'][t, 0:w], ACC[0:w, t, :]).then_inc(sem("y_out"), 16)
            sp.wait_ge(sem("y_out"), 16 * TT3)

        @block.tensor
        def _(pe):
            mm, turned = nc.tensor.matmul, nc.tensor.transpose

            def project(m, i):
                n = m * RING + i
                pe.wait_ge(sem(f"weights_in{i}"), (m + 1) * 16)
                pe.wait_ge(sem("tile_moved"), n + 1)
                for k in range(KT):
                    last = mm(PS[:, 6 + i % 2, 0:NTOK], WR[:, i, k, :], H0T[:, k, :], start=(k == 0), stop=(k == KT - 1))
                last.then_inc(sem("tile_done"), 1)

            pe.wait_ge(sem("consts_in"), 16)
            for t in range(TT3):
                w = 128 if t < 2 else 64
                pe.wait_ge(sem("h_ready"), t + 1)
                for k in range(KT):
                    last = turned(bank(2 * t + k // 4, 4, 128)[:, k % 4], H0[:, t, k * 128:k * 128 + 128], ID)
                last.then_inc(sem("h_turned"), 1)
            pe.wait_ge(sem("h0T_ready"), TT3)
            with pe.Fori(0, PRE // RING) as m:
                for i in range(RING):
                    project(m, i)
            meet(pe, 1)
            pe.wait_ge(sem("small_w_in"), 48)

            def pairs(out, lhs, rhs, **kw):
                for j in range(8):
                    last = mm(out(j), lhs(j), rhs(j), **kw)
                return last

            full = dict(start=True, stop=True)

            b = [bank(k, 8, L) for k in range(6)]

            def front_lora(c):
                pe.wait_ge(sem("rw_low"), c + 1)
                pairs(lambda j: b[2][:, j], lambda j: W2P[:, j * 128:j * 128 + 128], lambda j: LOW, **full)
                pairs(lambda j: b[3][:, j], lambda j: A2P[:, j * 128:j * 128 + 128], lambda j: LOW,
                      **full).then_inc(sem("rw_pre"), 1)
                pe.wait_ge(sem("rw_sq"), c + 1)
                mm(bank(5), BLK, SQ.rearrange("p a b -> p (a b)"), **full).then_inc(sem("rw_ss"), 1)

            def front_bonus(c):
                pe.wait_ge(sem("rw_bq"), c + 1)
                mm(bank(3), BLK, BQ.rearrange("p a b -> p (a b)"), **full).then_inc(sem("rw_bonus"), 1)

            def rwkv(c, ahead):
                def fill(f):
                    project(c * (FILL // RING) + (N_RW + f) // RING, (N_RW + f) % RING)

                one = c + 1
                pe.wait_ge(sem("rw_vbd"), one)
                pairs(lambda j: b[5][:, j], lambda j: VBD[:, j], lambda j: E, **full).then_inc(sem("rw_vtok"), 1)
                fill(0)
                pe.wait_ge(sem("rw_ops"), one)
                w = banks(0, 2, 8, 2, L)
                for u, lhs in ((w, BBD), (banks(2, 2, 8, 2, L), KBD)):
                    pairs(lambda j: u[:, j], lambda j: lhs[:, j], lambda j: AR[:, j], **full).then_inc(sem("rw_scores"), 1)
                fill(1)
                pe.wait_ge(sem("rw_lva"), c * 5 + 1)
                pairs(lambda j: b[4][:, j], lambda j: PTBD[:, j], lambda j: E, **full).then_inc(sem("rw_p0"), 1)
                pe.wait_ge(sem("rw_masked"), c * 2 + 2)
                pairs(lambda j: b[2][:, j], lambda j: BBD[:, j], lambda j: E, **full)
                pairs(lambda j: b[3][:, j], lambda j: KBD[:, j], lambda j: E, **full).then_inc(sem("rw_bktok"), 1)
                for r in range(6):
                    pe.wait_ge(sem("rw_pbd"), c * 6 + (r + 1))
                    if r < 5:
                        pe.wait_ge(sem("rw_lva"), c * 5 + (r + 1))
                        pairs(lambda j: b[4][:, j], lambda j: PTBD[:, j], lambda j: PSK[:, j],
                              **full).then_inc(sem("rw_power"), 1)
                    pe.wait_ge(sem("rw_lv"), c * 6 + (r + 1))
                    cols = slice(0, 1) if r == 0 else slice(0, 2) if r < 4 else slice(1, 2)
                    pairs(lambda j: w[:, j, cols], lambda j: PBD[:, j], lambda j: PTT[:, j, cols],
                          **full).then_inc(sem("rw_inverse"), 1)
                    if r < 3:
                        fill(2 + r)
                    if r == 4:
                        fill(5)
                    if r == 0:
                        pe.wait_ge(sem("rw_sbd"), one)
                        if ahead:
                            front_lora(c + 1)
                    if r == 3:
                        if ahead:
                            pe.wait_ge(sem("rw_ssc"), c + 2)
                        pairs(lambda j: b[5][:, j], lambda j: G2[:, j * 128:j * 128 + 128], lambda j: GSL,
                              **full).then_inc(sem("rw_gate"), 1)
                pe.wait_ge(sem("rw_gated"), one)
                for j in range(8):
                    mm(b[5][:, j], AKBD[:, j], VS[:, j], start=True, stop=False)
                    last = mm(b[5][:, j], ABD[:, j], SS[:, j], start=False, stop=True)
                last.then_inc(sem("rw_x"), 1)
                fill(6)
                pe.wait_ge(sem("rw_xs"), one)
                pairs(lambda j: b[4][:, j], lambda j: PTBD[:, j], lambda j: XS[:, j], **full).then_inc(sem("rw_sa"), 1)
                if ahead:
                    front_bonus(c + 1)
                pe.wait_ge(sem("rw_sas"), one)
                for j in range(8):
                    mm(b[2][:, j], BBD[:, j], SAS[:, j], start=True, stop=False)
                    last = mm(b[2][:, j], KBD[:, j], VS[:, j], start=False, stop=True)
                last.then_inc(sem("rw_st"), 1)
                pe.wait_ge(sem("rw_sabd"), one)
                for j in range(8):
                    mm(b[0][:, j], SBD[:, j], AR[:, j, 1], start=True, stop=False)
                    mm(b[0][:, j], VBD[:, j], SK[:, j, 1], start=False, stop=False)
                    last = mm(b[0][:, j], SABD[:, j], SB[:, j, 1], start=False, stop=True)
                last.then_inc(sem("rw_y"), 1)
                fill(7)
                for f in range(8, FILL):
                    fill(f)
                pe.wait_ge(sem("rw_ys"), one)
                mm(bank(3), BLK, YS.rearrange("p a b -> p (a b)"), **full).then_inc(sem("rw_mean"), 1)
                pe.wait_ge(sem("rw_ysq"), one)
                mm(bank(4), BLK, SQ.rearrange("p a b -> p (a b)"), **full).then_inc(sem("rw_var"), 1)

            for n in range(PRE, N_RW):
                project(n // RING, n % RING)
            front_lora(0)
            front_bonus(0)
            with pe.Fori(0, NPC) as c:
                rwkv(c, True)
            rwkv(NPC, False)
            for n in range(N_S0, N_S0 + HEAD_S // 2):
                project(n // RING, n % RING)
            meet(pe, 2)
            def ssm(c):
                def fill(f):
                    project(c * (FILL_S // RING) + (N_SSM + f) // RING, (N_SSM + f) % RING)

                one = c + 1
                pe.wait_ge(sem("ss_ac"), one)
                pe.wait_ge(sem("ss_state"), one)
                mm(PS[:, 2, 0:32], DT2, SEL, **full)
                mm(PS[:, 2, 32:64], AC2, SEL, **full)
                mm(PS[:, 2, 64:96], ONE, SELL, **full)
                for k in range(2):
                    last = mm(bank(3 + k, 8, L), LH, RD[:, 8 * k:8 * k + 8, :], **full)
                last.then_inc(sem("ss_bc"), 1)
                fill(0)
                pe.wait_ge(sem("ss_xs"), one)
                w = banks(0, 2, 16, L)
                for j in range(16):
                    last = mm(w[:, j], XTBD[:, j], E, **full)
                last.then_inc(sem("ss_xtok"), 1)
                pe.wait_ge(sem("ss_bcs"), one + 1)
                w = bank(5, 4, L, n=256)
                for g in range(4):
                    last = mm(w[:, g], BT2[:, g], CT[:, g], **full)
                pe.wait_ge(sem("ss_seg"), one)
                w = bank(2, 4, 128)
                for g in range(4):
                    last = turned(w[:, g], BT2[:, g].rearrange("p a b -> p (a b)"), ID)
                last.then_inc(sem("ss_cb"), 1)
                fill(1)
                pe.wait_ge(sem("decays"), one)
                pe.wait_ge(sem("ss_state"), one)
                if c is NPC:
                    pe.wait_ge(sem("state_in"), 32)
                w = banks(3, 2, 16, L)
                for j in range(16):
                    last = mm(w[:, j], SN[:, j * 128:j * 128 + 128], CT[:, j // 4], **full)
                pe.wait_ge(sem("ss_mt"), one)
                w = banks(0, 2, 16, L)
                for j in range(16):
                    last = mm(w[:, j], XDBD[:, j], SEG[:, j], **full)
                last.then_inc(sem("mixed"), 1)
                fill(2)
                pe.wait_ge(sem("ss_yr"), one)
                pe.wait_ge(sem("ss_btm"), one)
                w = banks(0, 4, 16, 128)
                for j in range(16):
                    last = mm(w[:, j], BTM[:, j // 4], XEBD[:, j], **full)
                last.then_inc(sem("state_sums"), 1)
                pe.wait_ge(sem("squares"), one)
                w = bank(5, 4, L, n=256)
                for k in range(4):
                    last = mm(w, ONE, YO.rearrange("p (g i) b -> p g i b", i=4)[:, :, k, :], start=(k == 0), stop=(k == 3))
                last.then_inc(sem("square_sums"), 1)
                fill(3)

            for n in range(N_S0 + HEAD_S // 2, N_SSM):
                project(n // RING, n % RING)
            with pe.Fori(0, NPC) as c:
                ssm(c)
            ssm(NPC)
            project(N_G0 // RING, N_G0 % RING)
            meet(pe, 3)
            for n in range(N_G0 + 1, N_GLA):
                project(n // RING, n % RING)

            def gla(c):
                def fill(f):
                    if c is not NPC:
                        project(c * (FILL_G // RING) + (N_GLA + f) // RING, (N_GLA + f) % RING)

                one = c + 1
                pe.wait_ge(sem("rows_in"), one * 32 + 16 * NCH)
                pe.wait_ge(sem("gl_state"), one)
                for j in range(4):
                    last = mm(bank(0, 4, L, n=256)[:, j], WA2[:, j * 128:j * 128 + 128], UA, **full)
                last.then_inc(sem("gl_pre"), 1)
                w = banks(1, 2, 8, 128)
                for j in range(8):
                    last = turned(w[0:64, j], UG[:, 8 + j], ID)
                last.then_inc(sem("gl_v"), 1)
                for f in range(3):
                    fill(f)
                if c is NPC:
                    pe.wait_ge(sem("tile_moved"), NT + 2)
                    for q, b in ((0, 6), (2, 7), (3, 7)):
                        merge_part(0, q, b)
                pe.wait_ge(sem("gl_ops"), one)
                for h in range(4):
                    last = mm(bank(0, 4, L, n=256)[0:64, h], KI[:, h], QD[:, h], **full)
                for h in range(4):
                    last = turned(bank(3, 4, 128)[0:64, h], KE[:, h], ID)
                last.then_inc(sem("gl_sc"), 1)
                pe.wait_ge(sem("gl_scm"), one)
                pe.wait_ge(sem("gl_vt"), one)
                if c is NPC:
                    pe.wait_ge(sem("state_in"), 48)
                for j in range(8):
                    mm(bank(4, 8, L)[:, j], VT[:, j], SCT[:, j // 2], start=True, stop=False)
                    last = mm(bank(4, 8, L)[:, j], SG[:, j // 2, (j % 2) * 128:(j % 2) * 128 + 128], QD[:, j // 2],
                              start=False, stop=True)
                last.then_inc(sem("mixed"), 1)
                w = banks(1, 2, 4, 256)
                for h in range(4):
                    last = mm(w[:, h], KET[:, h], VT[:, 2 * h:2 * h + 2], **full)
                last.then_inc(sem("state_sums"), 1)
                fill(3)
                pe.wait_ge(sem("squares"), NCH + one)
                for k in range(2):
                    last = mm(bank(5, 4, L, n=256), ONE, SQO.rearrange("p (g i) b -> p g i b", i=2)[:, :, k, :],
                              start=(k == 0), stop=(k == 1))
                last.then_inc(sem("square_sums"), 1)
                if c is NPC:
                    pe.drain().then_inc(sem("phase_over"), 1)
                    merge_part(1, 0, 3)
                    merge_part(1, 2, 4)

            pe.wait_ge(sem("small_w_in"), 64)
            def merge_part(d, q, b):
                pe.wait_ge(sem(f"weights_in{q}"), d * 16 + 16 * ((NT + RING - 1 - q) // RING + 1))
                for k in range(KT):
                    last = mm(PS[:, b, 0:NTOK], WR[:, q, k, :], OT[:, 8 * q + k, :],
                              start=(k == 0 and q < 3), stop=(k == KT - 1 and q != 2))
                last.then_inc(sem("tile_done"), 1)

            with pe.Fori(0, NPC) as c:
                gla(c)
            gla(NPC)
            pe.wait_ge(sem("phase_over"), ENG * 4)

            def merge_step(d, p):
                pe.wait_ge(sem("merged"), d)
                for q in STEP_ORDER:
                    merge_part(d + (q != 1), q, (MERGE_BANKS[p] if q == 1 else MERGE_BANKS[1 - p])[q])

            merge_part(0, 1, 1)
            merge_part(1, 3, 4)
            for q in STEP_ORDER:
                merge_part(1 + (q != 1), q, MERGE_BANKS[q == 1][q])
            with pe.Fori(1, 3) as d2:
                for p in range(2):
                    merge_step(d2 * 2 + p, p)
            merge_step(6, 0)
            merge_part(7, 1, MERGE_BANKS[1][1])
            pe.wait_ge(sem("merged"), 8)
            pe.wait_ge(sem("w_out_in"), 16)
            pe.wait_ge(sem("router_in"), 32)

            def w_out(t):
                w = 128 if t < 2 else 64
                for h in range(2):
                    for k in range(KT):
                        last = mm(PS[0:w, 2 * t + h, :], MG[:, k, t * 128:t * 128 + w], WOUT[:, k, h * 512:h * 512 + 512],
                                  start=(k == 0), stop=(k == KT - 1))
                last.then_inc(sem("w_out_done"), 1)

            def route(t):
                w = 128 if t < 2 else 64
                pe.wait_ge(sem("h_ready"), TT3 + t + 1)
                for k in range(KT):
                    last = turned(bank(2 * t + k // 4, 4, 128)[:, k % 4], H0[:, t, k * 128:k * 128 + 128], ID)
                last.then_inc(sem("h_turned"), 1)
                pe.wait_ge(sem("h0T_ready"), TT3 + t + 1)
                for k in range(KT):
                    last = mm(PS[0:w, 2 * t, 0:NE], H0T[:, k, t * 128:t * 128 + w], WRT[:, k, :], start=(k == 0), stop=(k == KT - 1))
                last.then_inc(sem("logits"), 1)

            w_out(0)
            w_out(1)
            route(0)
            w_out(2)
            route(1)
            route(2)
            pe.wait_ge(sem("shared_in"), 32)
            w13 = shaped(W13[1][:, 1, :], KT, 512)
            for f in (2, 3, 0, 1):
                if f == 0:
                    pe.wait_ge(sem("scores"), TT3)
                for k in range(KT):
                    last = mm(PS[:, 4 + f, 0:NTOK], w13[:, k, f * 128:f * 128 + 128], H0T[:, k, :],
                              start=(k == 0), stop=(k == KT - 1))
            last.then_inc(sem("shared_hid"), 1)
            pe.wait_ge(sem("chosen"), 1)
            for t in range(TT3):
                for u in range(t + 1):
                    last = mm(PS[:, 3, t * NE:t * NE + NE], TRI if u == t else ONE, CHO[:, u, :], start=(u == 0), stop=(u == t))
            for u in range(TT3):
                last = mm(PS[:, 3, 192:192 + NE], ONE, CHO[:, u, :], start=(u == 0), stop=(u == TT3 - 1))
            last.then_inc(sem("places"), 1)
            pe.wait_ge(sem("shared_act"), 1)
            w2 = shaped(W2[1][:, 1, :], 2, D)
            for t in range(TT3):
                w = 128 if t < 2 else 64
                pe.wait_ge(sem("shared_free"), t + 1)
                for h in range(2):
                    for f in range(2):
                        last = mm(PS[0:w, 4 + 2 * (t % 2) + h, :], SHID[:, f, t * 128:t * 128 + w],
                                  w2[:, f, h * 512:h * 512 + 512], start=(f == 0), stop=(f == 1))
                last.then_inc(sem("shared_out"), 1)
            pe.drain().then_inc(sem("shared_used"), 1)
            pe.wait_ge(sem("shared_free"), TT3 + 2)

            def tiles(i):
                return slice(64 * i, 64 * i + 64)

            def gather(n, m, p, h):
                if h == 0:
                    pe.wait_ge(sem("onehot"), n + 1)
                    pe.wait_ge(sem("x_left"), n + 1)
                for k in range(4):
                    for t in range(TT3):
                        last = mm(bank(h, 4, 128)[:, k], H0[:, t, (4 * h + k) * 128:(4 * h + k) * 128 + 128], OH[:, p, t, :],
                                  start=(t == 0), stop=(t == TT3 - 1))
                if h == 0:
                    last.then_inc(sem("x_half"), 1)
                else:
                    for t in range(TT3):
                        last = mm(PS[:, 4, 0:4], OH[:, p, t, :], INFO[:, t, bass.ds(m * 4, 4)], start=(t == 0), stop=(t == TT3 - 1))
                    last.then_inc(sem("x_done"), 1)

            def hidden(n, p, loads):
                pe.wait_ge(sem("x_left"), n + 2)
                pe.wait_ge(sem("x_right"), n + 1)
                pe.wait_ge(sem(f"weights_in{p}"), loads * 32 + 16 * mixer_loads(p))
                for k in range(KT):
                    for i in range(2):
                        last = mm(PS[tiles(i), 2, :], XE[:, k, tiles(i)], W13[p][:, i, k * 512:k * 512 + 512],
                                  start=(k == 0), stop=(k == KT - 1))
                last.then_inc(sem("hid_done"), 1)

            def turn(n):
                pe.wait_ge(sem("hid_ready"), n + 1)
                for f in range(2):
                    last = turned(PS[:, 3, f * 128:f * 128 + 128], HID[:, f * 128:f * 128 + 128], ID)
                last.then_inc(sem("hid_turned"), 1)

            def down(n, p, loads):
                pe.wait_ge(sem("hidt_ready"), n + 1)
                pe.wait_ge(sem(f"weights_in{2 + p}"), loads * 32 + 16 * mixer_loads(2 + p))
                pe.wait_ge(sem("y_left"), n + 1)
                pe.wait_ge(sem("y_right"), n + 1)
                for h in range(2):
                    for f in range(2):
                        for i in range(2):
                            last = mm(PS[tiles(i), 5 + h, :], HIDT[:, f, tiles(i)],
                                      W2[p][:, i, f * D + h * 512:f * D + h * 512 + 512], start=(f == 0), stop=(f == 1))
                last.then_inc(sem("pair_done"), 1)

            for h in range(2):
                gather(0, 0, 0, h)

            def steady(m, p):
                n = m * 2 + p
                hidden(n, p, m + 1)
                gather(n + 1, n + 1, 1 - p, 0)
                turn(n)
                gather(n + 1, n + 1, 1 - p, 1)
                down(n, p, m + 1)

            with pe.Fori(0, NE // 4 - 1) as m:
                for p in range(2):
                    steady(m, p)
            steady(NE // 4 - 1, 0)
            hidden(NE // 2 - 1, 1, NE // 4)
            turn(NE // 2 - 1)
            down(NE // 2 - 1, 1, NE // 4)
            with overflow(pe):
                with pe.Fori(0, NE // 2) as m:
                    for b in range(NBLK - 1):
                        n = m * (NBLK - 1) + (NE // 2 + b)
                        for h in range(2):
                            gather(n, m, b % 2, h)
                        hidden(n, 0, m + (NE // 4 + 1))
                        turn(n)
                        down(n, 0, m + (NE // 4 + 1))

        @block.scalar
        def _(act):
            def a_(out, in_, f, **kw):
                return nc.scalar.activation(out, in_, f, **kw)

            def root(x, asked, n, done):
                act.wait_ge(sem(asked), n)
                a_(x, x, ACT.Sqrt)
                act.drain().then_inc(sem(done), 1)

            for t in range(TT3):
                w = 128 if t < 2 else 64
                root(RS[:, t:t + 1], "ln_var", t + 1, "ln_rstd")
                act.wait_ge(sem("h_turned"), t + 1)
                src = banks(2 * t, 2, KT, 128)
                a_(H0T[:, :, t * 128:t * 128 + w], src[:, :, 0:w], ACT.Copy).then_inc(sem("h0T_ready"), 1)
            act.wait_ge(sem("vectors_in"), 32)
            act.wait_ge(sem("stage_zero"), 1)
            for i in range(RING):
                nc.scalar.sem_inc(sem(f"store_done{i}"), 16)
            nc.scalar.sem_inc(sem("tile_moved"), 2)

            def move(m, i):
                n = m * RING + i
                act.wait_ge(sem("tile_done"), n + 1)
                act.wait_ge(sem(f"store_done{i}"), (m + 1) * 16)
                src = bank(6 + i % 2, NCH, L, n=NTOK)
                a_(STG[:, i, 1:NPC, 0:HIST], src[:, 0:NPC - 1, L - HIST:L], ACT.Copy)
                a_(STG[:, i, 0:NCH:NPC, 0:HIST], HISTS[:, n, :, :], ACT.Copy)
                a_(STG[:, i, :, HIST:CW], src, ACT.Copy)
                act.drain().then_inc(sem("tile_moved"), 1)
                act.wait_ge(sem("tile_moved"), n + 3)
                act.dma_start(ut[n, :, :, :], STG[:, i, :, :]).then_inc(sem(f"store_done{i}"), 16)

            with act.Fori(0, PRE // RING) as m:
                for i in range(RING):
                    move(m, i)
            meet(act, 1)

            def diag(out, src, func=ACT.Copy):
                for h in range(2):
                    last = a_(half(out, h), src[64 * h:64 * h + 64, :, :], func)
                return last

            b = [bank(k, 8, L) for k in range(6)]

            def front_low(c):
                act.wait_ge(sem("rw_us"), c + 1)
                a_(LOW[0:64, :], US[0:64, 24, :], ACT.Tanh)
                a_(LOW[64:128, :], US[64:128, 24, :], ACT.Copy)
                a_(GS, US[:, 25, :], ACT.Sigmoid)
                act.drain().then_inc(sem("rw_low"), 1)

            def front_decay(c):
                act.wait_ge(sem("rw_wa"), c + 1)
                a_(WS, WS, ACT.Sigmoid)
                a_(AS, AS, ACT.Sigmoid)
                act.drain().then_inc(sem("rw_sig"), 1)

            def front_exp(c):
                act.wait_ge(sem("rw_cs"), c + 1)
                a_(G, CS, ACT.Exp, scale=-DECAY)
                a_(GI, CS, ACT.Exp, scale=DECAY)
                a_(GP, GP, ACT.Exp, scale=-DECAY)
                act.drain().then_inc(sem("rw_exp"), 1)

            def rwkv(c, late, ahead):
                def fill(f):
                    move(c * (FILL // RING) + (N_RW + f) // RING, (N_RW + f) % RING)

                one, w = c + 1, banks(0, 2, 8, 2, L)
                diag(VBD, US[:, 16:24, :])
                a_(GSL, GS, ACT.Copy)
                act.drain().then_inc(sem("rw_vbd"), 1)
                act.wait_ge(sem("rw_vtok"), one)
                a_(VS, b[5], ACT.Copy)
                diag(VBD, b[5])
                act.wait_ge(sem("rw_ar"), one)
                diag(ABD, AR[:, :, 0, :])
                fill(0)
                act.wait_ge(sem("rw_masked"), c * 2 + 1)
                diag(PTBD, SB[:, :, 0, :])
                act.drain().then_inc(sem("rw_lva"), 1)
                fill(1)
                act.wait_ge(sem("rw_masked"), c * 2 + 2)
                diag(AKBD, SK[:, :, 0, :])
                act.wait_ge(sem("rw_bktok"), one)
                diag(BBD, b[2])
                diag(KBD, b[3])
                act.drain()
                act.wait_ge(sem("rw_state"), one)
                if c is NPC:
                    act.wait_ge(sem("state_in"), 16)
                diag(SBD, SS)
                act.drain().then_inc(sem("rw_sbd"), 1)
                for r in range(4):
                    act.wait_ge(sem("rw_inverse"), c * 6 + (r + 1))
                    diag(PTBD, w[:, :, 0])
                    a_(PTT[:, :, 0, :], w[:, :, 0], ACT.Copy)
                    act.drain().then_inc(sem("rw_lva"), 1)
                    if r == 0 and ahead:
                        front_low(c + 1)
                    if r == 2 and ahead:
                        root(SAS, "rw_ssc", c + 2, "rw_rn")
                    if r < 3:
                        fill(2 + r)
                    if r == 0 and late:
                        root(TA, "rw_varc", c, "rw_rstd")
                    if r == 1 and ahead:
                        front_decay(c + 1)
                act.wait_ge(sem("rw_late"), one)
                act.wait_ge(sem("rw_gate"), one)
                a_(GATE, b[5], ACT.Copy)
                act.drain().then_inc(sem("rw_gated"), 1)
                if ahead:
                    front_exp(c + 1)
                fill(5)
                fill(6)
                act.wait_ge(sem("rw_sas"), one)
                diag(SABD, SAS)
                act.drain().then_inc(sem("rw_sabd"), 1)
                for f in range(7, FILL):
                    fill(f)

            for n in range(PRE, N_RW):
                move(n // RING, n % RING)
            front_low(0)
            front_decay(0)
            root(SAS, "rw_ssc", 1, "rw_rn")
            front_exp(0)
            rwkv(0, False, True)
            with act.Fori(1, NPC) as c:
                rwkv(c, True, True)
            rwkv(NPC, True, False)
            root(TA, "rw_varc", NCH, "rw_rstd")
            for n in range(N_S0, N_S0 + HEAD_S // 2):
                move(n // RING, n % RING)
            meet(act, 2)
            a_(NA, VEC[:, V_ALOG:V_ALOG + 1], ACT.Exp)
            act.drain().then_inc(sem("gates_ready"), 1)
            nc.scalar.sem_inc(sem("ss_bcs"), 1)

            def softplus(c):
                act.wait_ge(sem("softplus_in"), c + 1)
                a_(LB, AB, ACT.Exp, scale=-1.0)
                act.drain()
                a_(LB, LB, ACT.Ln, bias=1.0)
                act.drain().then_inc(sem("softplus_out"), 1)

            def ssm(c):
                def fill(f):
                    move(c * (FILL_S // RING) + (N_SSM + f) // RING, (N_SSM + f) % RING)

                one = c + 1
                act.wait_ge(sem("ss_conv"), one)
                a_(XS_, XC[:, 0:16], ACT.Silu)
                diag(XTBD, XC[:, 0:16], ACT.Silu)
                act.drain().then_inc(sem("ss_xs"), 1)
                for k in range(2):
                    a_(BT2[:, :, k, :], XC[:, 16:20], ACT.Silu)
                a_(CT, XC[:, 20:24], ACT.Silu)
                act.drain().then_inc(sem("ss_bcs"), 1)
                fill(0)
                act.wait_ge(sem("ss_z_in"), one * 16)
                a_(UZ, UZ, ACT.Silu)
                act.drain().then_inc(sem("gate_silu"), 1)
                act.wait_ge(sem("ss_seg"), one)
                a_(EBC, banks(3, 2, 16, L), ACT.Exp)
                a_(SEG, SEG, ACT.Exp)
                a_(EL, EL, ACT.Exp)
                a_(ALS, ALS, ACT.Exp)
                act.drain().then_inc(sem("decays"), 1)
                if c is not NPC:
                    softplus(c + 1)
                fill(1)
                act.wait_ge(sem("ss_cb"), one)
                a_(BTM, bank(2, 4, 128), ACT.Copy)
                act.drain().then_inc(sem("ss_btm"), 1)
                fill(2)
                act.wait_ge(sem("ss_yz"), one)
                a_(YO, YC, ACT.Square)
                act.drain().then_inc(sem("squares"), 1)
                root(RG, "variance", one, "rstd")
                fill(3)

            softplus(0)
            for n in range(N_S0 + HEAD_S // 2, N_SSM):
                move(n // RING, n % RING)
            with act.Fori(0, NPC) as c:
                ssm(c)
            ssm(NPC)
            move(N_G0 // RING, N_G0 % RING)
            meet(act, 3)
            for n in range(N_G0 + 1, N_GLA):
                move(n // RING, n % RING)
            act.wait_ge(sem("zeroed"), 2)

            def gla(c):
                def fill(f):
                    if c is not NPC:
                        move(c * (FILL_G // RING) + (N_GLA + f) // RING, (N_GLA + f) % RING)

                one = c + 1
                act.wait_ge(sem("rows_in"), one * 32 + 16 * NCH)
                act.wait_ge(sem("gl_out"), one)
                act.wait_ge(sem("softplus_in"), NCH + one)
                a_(LB4, AB4, ACT.Exp, scale=-1.0)
                act.drain()
                a_(LB4, LB4, ACT.Ln, bias=1.0)
                act.drain().then_inc(sem("softplus_out"), 1)
                act.wait_ge(sem("gl_v"), one)
                a_(VT[0:64], banks(1, 2, 8, 128)[0:64], ACT.Copy)
                act.drain().then_inc(sem("gl_vt"), 1)
                fill(0)
                act.wait_ge(sem("gl_cs"), one)
                a_(EG, CS4, ACT.Exp, scale=1.0 / 16)
                a_(EI, CS4, ACT.Exp, scale=-1.0 / 16)
                a_(EE, EE, ACT.Exp, scale=1.0 / 16)
                act.drain().then_inc(sem("decays"), 1)
                fill(1)
                a_(RR, UG[:, 16:24, :], ACT.Silu)
                act.drain().then_inc(sem("gate_silu"), 1)
                fill(2)
                root(RG4, "variance", NCH + one, "rstd")
                fill(3)

            with act.Fori(0, NPC) as c:
                gla(c)
            gla(NPC)
            meet(act, 4)

            with act.Fori(0, 4) as d2:
                for p in range(2):
                    act.wait_ge(sem(f"gates_in{p}"), d2 * 48 + 48)
                    g = GTF.rearrange("p (g d) w -> p g d w", g=3)[:, :, d2 * 2 + p, :]
                    a_(g, g, ACT.Sigmoid)
                    act.drain().then_inc(sem("gates_ready"), 1)

            def h1_root(t):
                root(RS1[:, t:t + 1], "ln_var", TT3 + t + 1, "ln_rstd")

            def route(t):
                w = 128 if t < 2 else 64
                act.wait_ge(sem("h_turned"), TT3 + t + 1)
                a_(H0T[:, :, t * 128:t * 128 + w], banks(2 * t, 2, KT, 128)[:, :, 0:w], ACT.Copy)
                act.drain().then_inc(sem("h0T_ready"), 1)
                act.wait_ge(sem("logits"), t + 1)
                a_(SCO[0:w, t, :], PS[0:w, 2 * t, 0:NE], ACT.Sigmoid)
                act.drain().then_inc(sem("scores"), 1)

            h1_root(0)
            act.wait_ge(sem("score_room"), 1)
            h1_root(1)
            route(0)
            h1_root(2)
            route(1)
            route(2)
            act.wait_ge(sem("shared_hid"), 1)
            a_(SHID, PS[:, 4:6, 0:NTOK], ACT.Silu)
            act.drain().then_inc(sem("shared_silu"), 1)
            nc.scalar.sem_inc(sem("x_left"), 1)

            def x_step(n):
                act.wait_ge(sem("x_half"), n + 1)
                a_(XE[:, 0:4], bank(0, 4, 128), ACT.Copy)
                act.drain().then_inc(sem("x_left"), 1)

            def silu_step(n):
                act.wait_ge(sem("hid_done"), n + 1)
                a_(SIL, PS[:, 2, 0:256], ACT.Silu)
                act.drain().then_inc(sem("silu_ready"), 1)

            def turn_step(n):
                act.wait_ge(sem("hid_turned"), n + 1)
                a_(HIDT, bank(3, 2, 128, n=256), ACT.Copy)
                act.drain().then_inc(sem("hidt_ready"), 1)

            def y_step(n, p):
                act.wait_ge(sem("pair_done"), n + 1)
                act.wait_ge(sem("rows_out"), n + 1)
                a_(Y[:, p, 512:D], PS[:, 6, :], ACT.Copy, scale=GA[:, p:p + 1])
                act.drain().then_inc(sem("y_right"), 1)

            def steady(n, p, more=True):
                silu_step(n)
                if more:
                    x_step(n + 1)
                turn_step(n)
                y_step(n, p)

            x_step(0)
            with act.Fori(0, NE // 4 - 1) as m:
                for p in range(2):
                    steady(m * 2 + p, p)
            steady(NE // 2 - 2, 0)
            steady(NE // 2 - 1, 1, False)
            with overflow(act):
                with act.Fori(0, NE // 2) as m:
                    for b in range(NBLK - 1):
                        n = m * (NBLK - 1) + (NE // 2 + b)
                        x_step(n)
                        steady(n, b % 2, False)
            for t in range(TT3):
                w = 128 if t < 2 else 64
                root(RS2[0:w, t:t + 1], "ln_var", 2 * TT3 + t + 1, "ln_rstd")

        @block.vector
        def _(dve):
            def tt(out, a, b, op):
                return dve.tensor_tensor(out, a, b, op)

            def ts(out, a, s1, s2, op0, op1=None):
                return dve.tensor_scalar(out, a, s1, s2, op0, op1) if op1 is not None else \
                    dve.tensor_scalar(out, a, s1, s2, op0)

            def stt(out, a, s, b, op0, op1):
                return dve.scalar_tensor_tensor(out=out, in0=a, scalar=s, in1=b, op0=op0, op1=op1)

            mul, add, sub, mx = ALU.mult, ALU.add, ALU.subtract, ALU.max

            def layer_norm(X, t, g, b, n_ln, BN=BN, MV=MV, RS=RS, w=128, eps=1e-5):
                X, BN, MV, RS, g, b = X[0:w], BN[0:w], MV[0:w], RS[0:w], g[0:w], b[0:w]
                for k in range(2):
                    dve.bn_stats(BN[:, t, k, :], X[:, t, k * 512:k * 512 + 512])
                dve.drain()
                dve.bn_aggr(MV[:, t, :], BN[:, t, :, :].rearrange("p a b -> p (a b)"))
                dve.drain()
                ts(RS[:, t:t + 1], MV[:, t, 1:2], eps, None, add)
                dve.drain()
                dve.reciprocal(RS[:, t:t + 1], RS[:, t:t + 1])
                dve.drain().then_inc(sem("ln_var"), 1)
                dve.wait_ge(sem("ln_rstd"), n_ln)
                ts(X[:, t, :], X[:, t, :], MV[:, t, 0:1], RS[:, t:t + 1], sub, mul)
                dve.drain()
                tt(X[:, t, :], X[:, t, :], g, mul)
                dve.drain()
                tt(X[:, t, :], X[:, t, :], b, add)
                return dve.drain()

            dve.memset(STG, 0.0)
            dve.drain().then_inc(sem("stage_zero"), 1)
            dve.wait_ge(sem("ln_in"), 32)
            for t in range(TT3):
                if t < 2:
                    dve.wait_ge(sem("x_rest" if t else "x_first"), 16)
                layer_norm(H0, t, LNB[:, 0, :], LNB[:, 1, :], t + 1).then_inc(sem("h_ready"), 1)
            dve.memset(MIX, 0.0)
            dve.wait_ge(sem("consts_in"), 16)
            dve.wait_ge(sem("vectors_in"), 32)
            dve.drain().then_inc(sem("rw_ur_free"), 1)
            meet(dve, 1)
            nc.vector.sem_inc(sem("rw_state"), 1)
            dve.wait_ge(sem("consts_in"), 16)
            dve.wait_ge(sem("vectors_in"), 32)

            b = [bank(k, 8, L) for k in range(6)]
            r, k, v = US[:, 0:8, :], US[:, 8:16, :], US[:, 16:24, :]

            def front_rates(c):
                dve.wait_ge(sem("rw_pre"), c + 1)
                tt(WS, b[2], vec(V_W0, 8, L), add)
                tt(AS, b[3], vec(V_A0, 8, L), add)
                dve.drain().then_inc(sem("rw_wa"), 1)
                dve.wait_ge(sem("rw_ss"), c + 1)
                ts(SAS, b[5], 1e-24, None, mx)
                dve.drain()
                dve.reciprocal(SAS, SAS)
                dve.drain().then_inc(sem("rw_ssc"), 1)

            def front_sums(c):
                dve.wait_ge(sem("rw_sig"), c + 1)
                dve.tensor_tensor_scan(CS.rearrange("p a b -> p (a b)"), CON[:, C_RST:C_RST + 512],
                                       WS.rearrange("p a b -> p (a b)"), 0.0, mul, add)
                dve.drain()
                tt(GP, CS, WS, sub)
                dve.drain().then_inc(sem("rw_cs"), 1)

            def front_keys(c):
                dve.wait_ge(sem("rw_rn"), c + 1)
                tt(KK, KK, SAS, mul)
                dve.drain()
                tt(KA, KK, AS, mul)
                stt(SAS, AS, -1.0, vec(V_KA, 8, L), add, mul)
                dve.drain()
                stt(K2, SAS, 1.0, k, add, mul)
                dve.drain()
                tt(BQ, r, K2, mul)
                dve.drain()
                tt(BQ, BQ, vec(V_RK, 8, L), mul)
                dve.drain().then_inc(sem("rw_bq"), 1)

            def front_bonus(c):
                dve.wait_ge(sem("rw_bonus"), c + 1)
                tt(BV, b[3], v, mul)

            def late_root():
                dve.reciprocal(TA, TA)
                dve.drain().then_inc(sem("rw_varc"), 1)

            def rwkv(c, late, ahead):
                one = c + 1
                dve.wait_ge(sem("rw_exp"), one)
                stt(AR[:, :, 0, :], KK, -1.0, GP, mul, mul)
                tt(AR[:, :, 1, :], r, G, mul)
                dve.drain().then_inc(sem("rw_ar"), 1)
                for h in range(2):
                    q = slice(64 * h, 64 * h + 64)
                    tt(half(BBD, h), KA[q], GI[q], mul)
                    tt(half(KBD, h), K2[q], GI[q], mul)
                dve.drain().then_inc(sem("rw_ops"), 1)
                dve.tensor_copy(GLAST, G[:, :, L - 1])
                dve.wait_ge(sem("rw_scores"), c * 2 + 1)
                for k2 in range(2):
                    tt(SB[:, 4 * k2:4 * k2 + 4].rearrange("p a b c -> p a (b c)"),
                       bank(k2, 4, 128), over(M2, 4, 0, 128), mul)
                dve.drain().then_inc(sem("rw_masked"), 1)
                dve.wait_ge(sem("rw_scores"), c * 2 + 2)
                for k2 in range(2):
                    tt(SK[:, 4 * k2:4 * k2 + 4].rearrange("p a b c -> p a (b c)"),
                       bank(2 + k2, 4, 128), over(M2, 4, 0, 128), mul)
                dve.drain().then_inc(sem("rw_masked"), 1)
                dve.tensor_copy(PTT[:, :, 0, :], SB[:, :, 0, :])
                tt(PTT[:, :, 1, :], SB[:, :, 0, :], over(E, 8, 0, L), add)
                dve.wait_ge(sem("rw_p0"), one)

                def power():
                    for h in range(2):
                        dve.tensor_copy(half(PBD, h), b[4][64 * h:64 * h + 64])

                w = banks(0, 2, 8, 2, L)
                dve.tensor_copy(PSK, b[4])
                power()
                dve.drain().then_inc(sem("rw_pbd"), 1)
                nc.vector.sem_inc(sem("rw_lv"), 1)
                for rd in range(5):
                    if rd < 4:
                        dve.wait_ge(sem("rw_power"), c * 5 + (rd + 1))
                        dve.tensor_copy(PSK, b[4])
                    dve.wait_ge(sem("rw_inverse"), c * 6 + (rd + 1))
                    power()
                    dve.drain().then_inc(sem("rw_pbd"), 1)
                    if rd:
                        if rd < 4:
                            dve.wait_ge(sem("rw_lva"), c * 5 + (rd + 2))
                        tt(PTT[:, :, 1, :], PTT[:, :, 1, :], w[:, :, 1], add)
                        dve.drain().then_inc(sem("rw_lv"), 1)
                    else:
                        nc.vector.sem_inc(sem("rw_lv"), 1)
                    if rd == 0 and late:
                        late_root()
                    if rd == 1 and ahead:
                        front_rates(c + 1)
                    if rd == 2 and ahead:
                        front_sums(c + 1)
                dve.wait_ge(sem("rw_inverse"), c * 6 + 6)
                for h in range(2):
                    q = slice(64 * h, 64 * h + 64)
                    tt(half(PTBD, h), w[q, :, 1], PTT[q, :, 1, :], add)
                if ahead:
                    front_keys(c + 1)
                dve.wait_ge(sem("rw_x"), one)
                dve.tensor_copy(XS, b[5])
                dve.drain().then_inc(sem("rw_xs"), 1)
                dve.wait_ge(sem("rw_sa"), one)
                dve.tensor_copy(SAS, b[4])
                dve.drain().then_inc(sem("rw_sas"), 1)
                if ahead:
                    front_bonus(c + 1)
                dve.wait_ge(sem("rw_st"), one)
                tt(SS, SS, b[2], add)
                dve.drain()
                tt(SS, SS, GLAST.unsqueeze(2).to_broadcast([128, 8, L]), mul)
                dve.drain().then_inc(sem("rw_state"), 1)
                dve.wait_ge(sem("rw_y"), one)
                dve.tensor_copy(YS, b[0])
                dve.drain().then_inc(sem("rw_ys"), 1)
                dve.wait_ge(sem("rw_mean"), one)
                stt(YS, b[3], -1.0 / 64, YS, mul, add)
                dve.drain()
                tt(SQ, YS, YS, mul)
                dve.drain().then_inc(sem("rw_ysq"), 1)
                dve.wait_ge(sem("rw_var"), one)
                ts(TA, b[4], 1.0 / 64, 64e-5, mul, add)
                dve.drain()

            front_rates(0)
            front_sums(0)
            front_keys(0)
            front_bonus(0)
            rwkv(0, False, True)
            with dve.Fori(1, NPC) as c:
                rwkv(c, True, True)
            dve.wait_ge(sem("state_in"), 16)
            rwkv(NPC, True, False)
            late_root()
            dve.wait_ge(sem("state_out"), 32)
            meet(dve, 2)
            def neg_exp_a():
                dve.wait_ge(sem("gates_ready"), 1)
                ts(NA, NA, -1.0, None, mul)

            neg_exp_a()
            dve.memset(SN, 0.0)
            dve.drain().then_inc(sem("ss_state"), 1)
            nc.vector.sem_inc(sem("ss_z_free"), 1)
            dve.wait_ge(sem("zeroed"), 1)
            def step_in(c):
                dve.wait_ge(sem("rows_in"), c * 16 + 16)
                ts(T1, UM, VEC[:, V_DTB:V_DTB + 1], None, add)
                dve.drain()
                stt(AB, T1, -1.0, T1, mul, mx)
                dve.drain().then_inc(sem("softplus_in"), 1)

            def step_out(c):
                dve.wait_ge(sem("softplus_out"), c + 1)
                for k in range(2):
                    stt(DT2[:, k], T1, 0.0, LB, mx, add)
                dve.drain().then_inc(sem("rows_free"), 1)
                ts(T1, DT2[:, 0], NA, None, mul)
                dve.drain()
                dve.tensor_tensor_scan(AC2[:, 0], CON[:, C_RST:C_RST + L], T1, 0.0, mul, add)
                dve.drain()
                dve.tensor_copy(AC2[:, 1], AC2[:, 0])
                ts(SELL, SEL, AC2[:, 0, L - 1:L], None, mul)
                tt(RD, over(AC2[:, 0], 16, 0, L), PM.unsqueeze(2).to_broadcast([128, 16, L]), mul)
                dve.drain().then_inc(sem("ss_ac"), 1)

            def ssm(c):
                one = c + 1
                dve.wait_ge(sem("ss_bc"), one)
                for h in range(2):
                    q = slice(64 * h, 64 * h + 64)
                    for out, a in ((DTS, 0), (ACS, 32), (ALS, 64)):
                        dve.tensor_copy(out[q], PS[q, 2, a + h:a + 32:2])
                dve.tensor_copy(EL, PS[:, 2, 64:96])
                dve.drain()
                tt(ALS, ALS, ACS, sub)
                tt(SEG, banks(3, 2, 16, L), ACS.unsqueeze(2).to_broadcast([128, 16, L]), sub)
                dve.drain()
                ts(SEG, SEG, 0.0, None, ALU.min)
                dve.drain().then_inc(sem("ss_seg"), 1)
                dve.wait_ge(sem("ss_xtok"), one)
                for h in range(2):
                    q = slice(64 * h, 64 * h + 64)
                    tt(half(XDBD, h), banks(0, 2, 16, L)[q], DTS[q].unsqueeze(2).to_broadcast([64, 16, L]), mul)
                if c is not NPC:
                    step_in(c + 1)
                dve.wait_ge(sem("ss_cb"), one)
                tt(CBM, bank(5, 4, L, n=256), over(M2[:, L:2 * L], 4, 0, L), mul)
                dve.drain()
                dve.wait_ge(sem("decays"), one)
                for g in range(4):
                    tt(SEG[:, 4 * g:4 * g + 4], SEG[:, 4 * g:4 * g + 4], over(CBM[:, g], 4, 0, L), mul)
                dve.drain().then_inc(sem("ss_mt"), 1)
                for h in range(2):
                    q = slice(64 * h, 64 * h + 64)
                    tt(half(XEBD, h), half(XDBD, h), ALS[q].unsqueeze(2).to_broadcast([64, 16, L]), mul)
                if c is not NPC:
                    step_out(c + 1)
                dve.wait_ge(sem("mixed"), one)
                tt(YO, banks(3, 2, 16, L), EBC, mul)
                dve.drain()
                tt(YC, banks(0, 2, 16, L), YO, add)
                dve.drain().then_inc(sem("ss_yr"), 1)
                dve.wait_ge(sem("ss_xd"), one)
                tt(YC, YC, XD, add)
                dve.drain()
                dve.wait_ge(sem("gate_silu"), one)
                tt(YC, YC, UZ, mul)
                dve.drain().then_inc(sem("ss_yz"), 1)
                nc.vector.sem_inc(sem("ss_z_free"), 1)
                sn = SN.rearrange("p (h v) -> p h v", v=64)
                if c is NPC:
                    dve.wait_ge(sem("state_in"), 32)
                tt(sn, sn, EL.unsqueeze(2).to_broadcast([128, 32, 64]), mul)
                dve.drain()
                dve.wait_ge(sem("state_sums"), one)
                tt(SN, SN, banks(0, 4, 2048), add)
                dve.drain().then_inc(sem("ss_state"), 1)
                dve.wait_ge(sem("square_sums"), one)
                ts(RG, bank(5, 4, L, n=256), 1.0 / 512, 1e-5, mul, add)
                dve.drain()
                dve.reciprocal(RG, RG)
                dve.drain().then_inc(sem("variance"), 1)
                dve.wait_ge(sem("rstd"), one)
                for g in range(4):
                    tt(YC[:, 4 * g:4 * g + 4], YC[:, 4 * g:4 * g + 4], over(RG[:, g], 4, 0, L), mul)
                dve.drain()
                tt(OT[:, 16:32, bass.ds(c * L, L)], YC, vec(V_SNG, 16, L), mul)
                dve.drain()

            step_in(0)
            step_out(0)
            with dve.Fori(0, NPC) as c:
                ssm(c)
            ssm(NPC)
            dve.wait_ge(sem("state_out"), 64)
            meet(dve, 3)

            dve.memset(SG, 0.0)
            dve.drain().then_inc(sem("gl_state"), 1)
            nc.vector.sem_inc(sem("rows_free"), 1)
            nc.vector.sem_inc(sem("gl_out"), 1)
            dve.wait_ge(sem("zeroed"), 2)

            def gla(c):
                one = c + 1
                dve.wait_ge(sem("gl_pre"), one)
                tt(T4, bank(0, 4, L, n=256), vec(V_BA, 4, L), add)
                dve.drain()
                stt(AB4, T4, -1.0, T4, mul, mx)
                dve.drain().then_inc(sem("softplus_in"), 1)
                dve.wait_ge(sem("softplus_out"), NCH + one)
                stt(T4, T4, 0.0, LB4, ALU.min, sub)
                dve.drain()
                flat = lambda x: x.rearrange("p a b -> p (a b)")
                dve.tensor_tensor_scan(flat(CS4), CON[:, C_RST:C_RST + 4 * L], flat(T4), 0.0, mul, add)
                dve.drain()
                tt(EE, CS4[:, :, L - 1:L].to_broadcast([128, 4, L]), CS4, sub)
                dve.drain().then_inc(sem("gl_cs"), 1)
                dve.wait_ge(sem("decays"), NCH + one)
                stt(QD, UG[:, 0:4], GLA_SCALE, EG, mul, mul)
                tt(KI, UG[:, 4:8], EI, mul)
                tt(KE, UG[:, 4:8], EE, mul)
                dve.drain().then_inc(sem("gl_ops"), 1)
                dve.wait_ge(sem("gl_sc"), one)
                tt(SCT[0:64], bank(0, 4, L, n=256)[0:64], M2[0:64, L:2 * L].unsqueeze(1).to_broadcast([64, 4, L]), mul)
                dve.tensor_copy(KET[0:64], bank(3, 4, 128)[0:64])
                dve.drain().then_inc(sem("gl_scm"), 1)
                nc.vector.sem_inc(sem("rows_free"), 1)
                dve.wait_ge(sem("mixed"), NCH + one)
                dve.tensor_copy(O8, bank(4, 8, L))
                dve.drain()
                tt(SQO, O8, O8, mul)
                dve.drain().then_inc(sem("squares"), 1)
                if c is NPC:
                    dve.wait_ge(sem("state_in"), 48)
                tt(SG, SG, EG[:, :, L - 1:L].to_broadcast([128, 4, 256]), mul)
                dve.drain()
                dve.wait_ge(sem("state_sums"), NCH + one)
                tt(SG, SG, banks(1, 2, 4, 256), add)
                dve.drain().then_inc(sem("gl_state"), 1)
                dve.wait_ge(sem("square_sums"), NCH + one)
                ts(RG4, bank(5, 4, L, n=256), 1.0 / 256, 1e-5, mul, add)
                dve.drain()
                dve.reciprocal(RG4, RG4)
                dve.drain().then_inc(sem("variance"), 1)
                dve.wait_ge(sem("rstd"), NCH + one)
                o4 = O8.rearrange("p (h i) b -> p h i b", i=2)
                for i in range(2):
                    tt(o4[:, :, i], o4[:, :, i], RG4, mul)
                dve.drain()
                for i in range(2):
                    ts(o4[:, :, i], o4[:, :, i], VEC[:, V_GNG + i:V_GNG + i + 1], None, mul)
                dve.drain()
                tt(OT[:, 8:16, bass.ds(c * L, L)], O8, RR, mul)
                dve.drain().then_inc(sem("gl_out"), 1)

            with dve.Fori(0, NPC) as c:
                gla(c)
            gla(NPC)
            dve.wait_ge(sem("state_out"), 96)
            meet(dve, 4)

            def merge(d, of, done):
                dve.wait_ge(sem("tile_done"), done)
                dve.wait_ge(sem("gates_ready"), d + 2)
                b = [PS[:, k, 0:NTOK] for k in of]
                tt(MG[:, d, :], b[0], GTF[:, d + 8, :], mul)
                tt(MTMP[:, 0], b[1], GTF[:, d, :], mul)
                tt(MTMP[:, 1], b[2], GTF[:, d + 16, :], mul)
                dve.drain()
                tt(MG[:, d, :], MG[:, d, :], MTMP[:, 0], add)
                dve.drain()
                tt(MG[:, d, :], MG[:, d, :], MTMP[:, 1], add)
                dve.drain().then_inc(sem("merged"), 1)

            merge(0, (6, 1, 7), NT + 6)
            with dve.Fori(0, 3) as d2:
                for p in range(2):
                    merge(d2 * 2 + (p + 1), MERGE_BANKS[1 - p], d2 * 8 + (4 * p + NT + 10))
            merge(7, MERGE_BANKS[1], NT + 32)
            dve.wait_ge(sem("ln_in"), 64)
            dve.memset(SCO, 0.0)
            dve.memset(CHO, 0.0)
            dve.memset(PLACE, 0.0)
            dve.drain().then_inc(sem("score_room"), 1)

            def h1(t):
                w = 128 if t < 2 else 64
                dve.wait_ge(sem("w_out_done"), t + 1)
                stt(H0[0:w, t, :], H0[0:w, t, :], ALPHA, banks(2 * t, 2, D)[0:w], mul, add)
                dve.drain()
                layer_norm(H0, t, LN1[:, 0, :], LN1[:, 1, :], TT3 + t + 1, BN1, MV1, RS1).then_inc(sem("h_ready"), 1)

            def choose(out, x, th, k, n):
                ts(out, x, th, None, ALU.is_gt)
                ts(TIE[:, 0:n], x, th, None, ALU.is_equal)
                dve.drain()
                dve.tensor_reduce(CNT, out, AX.X, add)
                dve.tensor_tensor_scan(TRK[:, 0:n], TIE[:, 0:n], CON[:, C_ONE:C_ONE + n], 0.0, add, mul)
                dve.drain()
                tt(TRK[:, 0:n], TRK[:, 0:n], CNT.to_broadcast([128, n]), add)
                dve.drain()
                ts(TRK[:, 0:n], TRK[:, 0:n], float(k), None, ALU.is_le)
                dve.drain()
                tt(TIE[:, 0:n], TIE[:, 0:n], TRK[:, 0:n], mul)
                dve.drain()
                tt(out, out, TIE[:, 0:n], add)
                dve.drain()

            def route(t):
                w = 128 if t < 2 else 64
                dve.wait_ge(sem("scores"), t + 1)
                tt(SBI, SCO[:, t, :], RB, add)
                dve.drain()
                for g in range(NG):
                    dve.max(TOP[:, g, :], SBI[:, 8 * g:8 * g + 8])
                dve.drain()
                tt(GSC, TOP[:, :, 0], TOP[:, :, 1], add)
                dve.drain()
                dve.max(TOP[:, 0, :], GSC)
                dve.drain()
                choose(GM, GSC, TOP[:, 0, 3:4], 4, NG)
                ts(GM, GM, -1.0, 1e30, add, mul)
                dve.drain()
                s3 = SBI.rearrange("p (g k) -> p g k", k=8)
                tt(s3, s3, GM.unsqueeze(2).to_broadcast([128, NG, 8]), add)
                dve.drain()
                dve.max(TOP[:, 0, :], SBI)
                dve.drain()
                choose(TIE2, SBI, TOP[:, 0, 7:8], TOPK, NE)
                dve.tensor_copy(CHO[0:w, t, :], TIE2[0:w])
                dve.drain()
                tt(GTE, SCO[:, t, :], CHO[:, t, :], mul)
                dve.drain()
                dve.tensor_reduce(CNT, GTE, AX.X, add)
                dve.drain()
                ts(CNT, CNT, 1e-30, None, mx)
                dve.drain()
                dve.reciprocal(CNT, CNT)
                dve.drain()
                ts(INFO[:, t, 0:2 * NE:2], GTE, CNT, 2.5, mul, mul)
                dve.tensor_tensor_scan(TRK, CHO[:, t, :], CON[:, C_ONE:C_ONE + NE], 0.0, add, mul)
                dve.drain()
                ts(TRK, TRK, VEC[:, V_TOK8 + t:V_TOK8 + t + 1], -1.0 - SKIP, add, add)
                dve.drain()
                dve.tensor_copy(INFO[:, t, 1:2 * NE:2], TRK)
                dve.drain()

            h1(0)
            h1(1)
            route(0)
            h1(2)
            route(1)
            route(2)
            dve.drain().then_inc(sem("chosen"), 1)
            dve.wait_ge(sem("shared_silu"), 1)
            tt(SHID, SHID, PS[:, 6:8, 0:NTOK], mul)
            dve.drain().then_inc(sem("shared_act"), 1)
            nc.vector.sem_inc(sem("shared_free"), 2)
            dve.wait_ge(sem("places"), 1)
            ts(PLACE, bank(3, 8, NE)[:, 0:3], 1.0, None, mul)
            dve.tensor_copy(CTOT, PS[:, 3, 192:192 + NE])
            ts(TIE3, CHO, -1e4, 1e4, mul, add)
            dve.drain()
            tt(PLACE, PLACE, TIE3, add)
            dve.tensor_reduce(CNT, CTOT, AX.X, mx)
            dve.drain()
            ts(CNT, CNT, float(CAP), None, ALU.is_gt)
            dve.drain()
            dve.tensor_copy(FLAG[:, :], CNT)
            dve.drain().then_inc(sem("flag"), 1)
            for t in range(TT3):
                w = 128 if t < 2 else 64
                dve.wait_ge(sem("shared_out"), t + 1)
                stt(ACC[0:w, t, :], H0[0:w, t, :], ALPHA, banks(4 + 2 * (t % 2), 2, D)[0:w], mul, add)
                dve.drain()
                nc.vector.sem_inc(sem("shared_free"), 1)
            nc.vector.sem_inc(sem("y_left"), 1)
            nc.vector.sem_inc(sem("y_right"), 1)
            nc.vector.sem_inc(sem("rows_out"), 2)

            def onehot(m, p, b):
                for t in range(TT3):
                    for i in range(2):
                        ts(OH[:, p, t, 64 * i:64 * i + 64], CON[:, C_IOTA + CAP * b:C_IOTA + CAP * b + CAP],
                           PLACE[:, t, bass.ds(m * 2 + i, 1)], None, ALU.is_equal)
                dve.drain().then_inc(sem("onehot"), 1)

            def x_step(n, p):
                dve.wait_ge(sem("x_done"), n + 1)
                dve.wait_ge(sem("rows_out"), n + 1)
                dve.tensor_copy(XE[:, 4:8], bank(1, 4, 128))
                for i in range(2):
                    q = slice(64 * i, 64 * i + 64)
                    dve.tensor_copy(GA[q, p:p + 1], PS[q, 4, 2 * i:2 * i + 1])
                    ts(IDX[q, p:p + 1], PS[q, 4, 2 * i + 1:2 * i + 2], float(SKIP), None, add)
                dve.drain().then_inc(sem("x_right"), 1)

            def hid_step(n):
                dve.wait_ge(sem("silu_ready"), n + 1)
                tt(HID, SIL, PS[:, 2, 256:512], mul)
                dve.drain().then_inc(sem("hid_ready"), 1)

            def y_step(n, p):
                dve.wait_ge(sem("pair_done"), n + 1)
                ts(Y[:, p, 0:512], PS[:, 5, :], GA[:, p:p + 1], None, mul)
                dve.drain().then_inc(sem("y_left"), 1)

            onehot(0, 0, 0)
            onehot(1, 1, 0)
            x_step(0, 0)

            def steady(n, p, more=True):
                hid_step(n)
                if more:
                    x_step(n + 1, 1 - p)
                    onehot(n + 2, p, 0)
                y_step(n, p)

            with dve.Fori(0, NE // 4 - 1) as m:
                for p in range(2):
                    steady(m * 2 + p, p)
            hid_step(NE // 2 - 2)
            x_step(NE // 2 - 1, 1)
            y_step(NE // 2 - 2, 0)
            steady(NE // 2 - 1, 1, False)
            with overflow(dve):
                with dve.Fori(0, NE // 2) as m:
                    for b in range(NBLK - 1):
                        n = m * (NBLK - 1) + (NE // 2 + b)
                        onehot(m, b % 2, b + 1)
                        x_step(n, b % 2)
                        steady(n, b % 2, False)
            dve.wait_ge(sem("ln_in"), 96)
            for t in range(TT3):
                w = 128 if t < 2 else 64
                dve.wait_ge(sem(f"slots_in{t}"), 16)
                sum_rows(dve, t, w, slice(0, 640))
                dve.wait_ge(sem("rows_summed"), t + 1)
                layer_norm(ACC, t, LN2[:, 0, :], LN2[:, 1, :], 2 * TT3 + t + 1, BN2, MV2, RS2, w).then_inc(sem("y_ready"), 1)

        @block.gpsimd
        def _(pool):
            meet(pool, 1)
            nc.gpsimd.sem_inc(sem("ss_free_pool"), 1)
            nc.gpsimd.sem_inc(sem("rows_free"), 1)
            r, k, v = US[:, 0:8, :], US[:, 8:16, :], US[:, 16:24, :]
            ptt, mul, add, sub = pool.tensor_tensor, ALU.mult, ALU.add, ALU.subtract

            def front_shift(c, sample=False):
                pool.wait_ge(sem("rw_ur_in"), c * 16 + 16)
                ptt(US, UR[:, :, 0:L], UR[:, :, 1:L + 1], sub)
                pool.drain()
                ptt(US, US, vec(V_MU, 26, L), mul)
                pool.drain()
                ptt(US, US, UR[:, :, 1:L + 1], add)
                if sample:
                    pool.wait_ge(sem("last_rows_out"), 16)
                pool.tensor_copy(SHO, UR[:, :, L])
                pool.drain().then_inc(sem("rw_us"), 1)
                nc.gpsimd.sem_inc(sem("rw_ur_free"), 1)
                ptt(KK, k, vec(V_KK, 8, L), mul)
                pool.drain()
                ptt(SQ, KK, KK, mul)
                pool.drain().then_inc(sem("rw_sq"), 1)

            def late_out(c):
                pool.wait_ge(sem("rw_rstd"), c + 1)
                ptt(YS, YS, TA, mul)
                pool.drain()
                ptt(YS, YS, vec(V_LNG, 8, L), mul)
                pool.drain()
                ptt(YS, YS, vec(V_LNB, 8, L), add)
                pool.drain()
                ptt(YS, YS, BVL, add)
                pool.drain()
                pool.wait_ge(sem("rw_gated"), c + 1)
                ptt(OT[:, 0:8, bass.ds(c * L, L)], YS, GATE, mul)
                pool.drain()

            def rwkv(c, late, ahead, sample=False):
                pool.wait_ge(sem("rw_ops"), c + 1)
                pool.wait_ge(sem("rw_vbd"), c + 1)
                if ahead:
                    front_shift(c + 1, sample)
                if late:
                    late_out(c - 1)
                pool.tensor_copy(BVL, BV)
                pool.drain().then_inc(sem("rw_late"), 1)

            front_shift(0)
            rwkv(0, False, True)
            with pool.Fori(1, NPC - 1) as c:
                rwkv(c, True, True)
            nc.gpsimd.sem_inc(sem("last_rows"), 1)
            rwkv(NPC - 1, True, True, True)
            nc.gpsimd.sem_inc(sem("last_rows"), 1)
            rwkv(NPC, True, False)
            pool.wait_ge(sem("conv_in"), 16)
            for g in range(2):
                convolve(pool, slice(12 * g, 12 * g + 12), TMP2)
            pool.drain().then_inc(sem("ss_conv"), 1)
            nc.gpsimd.sem_inc(sem("ss_free_pool"), 1)
            late_out(NPC)
            meet(pool, 2)
            for x in (XTBD, XDBD, XEBD):
                pool.memset(x, 0.0)
            pool.drain().then_inc(sem("zeroed"), 1)

            def last_rows():
                pool.tensor_copy(CVO, UX[:, :, L:CW])

            def ssm(c, ahead=True, sample=False):
                pool.wait_ge(sem("ss_xs"), c + 1)
                pool.tensor_tensor(XD, XS_, vec(V_DSK, 16, L), ALU.mult)
                pool.drain().then_inc(sem("ss_xd"), 1)
                if ahead:
                    pool.wait_ge(sem("conv_in"), c * 16 + 32)
                    pool.wait_ge(sem("ss_bcs"), c + 2)
                    for g in range(2):
                        convolve(pool, slice(12 * g, 12 * g + 12), TMP2)
                    if sample:
                        pool.wait_ge(sem("last_rows_out"), 48)
                    last_rows()
                    pool.drain().then_inc(sem("ss_conv"), 1)
                    nc.gpsimd.sem_inc(sem("ss_free_pool"), 1)

            with pool.Fori(0, NPC - 1) as c:
                ssm(c)
            nc.gpsimd.sem_inc(sem("last_rows"), 1)
            ssm(NPC - 1, True, True)
            nc.gpsimd.sem_inc(sem("last_rows"), 1)
            ssm(NPC, False)
            meet(pool, 3)
            for x in (VT, SCT, KET):
                pool.memset(x, 0.0)
            pool.drain().then_inc(sem("zeroed"), 1)
            meet(pool, 4)

            last_slot = pool.to_reg(SLOTS - 1)

            def scatter(m, p):
                pool.wait_ge(sem("y_left"), m * 2 + (p + 2))
                pool.wait_ge(sem("y_right"), m * 2 + (p + 2))
                nc.gpsimd.sem_inc(sem("rows_taken"), 1)
                pool.indirect_dma_start(slots[:, :], bass.IndirectOffsetOnAxis(ap=IDX[:, p:p + 1], axis=0),
                                        Y[:, p, :], None, bounds_check=last_slot, oob_is_err=False
                                        ).then_inc(sem(f"rows_sent{p}"), 16)
                pool.wait_ge(sem(f"rows_sent{p}"), m * 16 + 16)
                nc.gpsimd.sem_inc(sem("rows_out"), 1)

            with pool.Fori(0, NE // 4) as m:
                for p in range(2):
                    scatter(m, p)
            with overflow(pool):
                with pool.Fori(NE // 4, NE // 4 * NBLK) as m:
                    for p in range(2):
                        scatter(m, p)
            pool.drain().then_inc(sem("rows_over"), 1)
            for t in range(TT3):
                w = 128 if t < 2 else 64
                pool.wait_ge(sem(f"slots_in{t}"), 16)
                sum_rows(pool, t, w, slice(640, D)).then_inc(sem("rows_summed"), 1)


def _tiles(w, ncol):
    import numpy as np
    k, n = w.shape
    return w.reshape(k // 128, 128, n // ncol, ncol).transpose(2, 1, 0, 3)


def _cols(v):
    return v.reshape(-1, 128).T


def _constants():
    import numpy as np
    c = np.zeros((128, NC), np.float32)
    p = np.arange(128)
    s = p % 64
    t = np.arange(64)
    c[:, C_ID:C_ID + 128] = np.eye(128)
    c[:, C_ONE:C_ONE + 128] = 1.0
    c[:, C_BLK:C_BLK + 128] = (p[:, None] // 64) == (p[None] // 64)
    c[:, C_M2:C_M2 + 64] = t[None] > s[:, None]
    c[:, C_M2 + 64:C_M2 + 128] = t[None] >= s[:, None]
    c[:, C_ML:C_ML + 64] = t[None] < s[:, None]
    c[:, C_E:C_E + 64] = t[None] == s[:, None]
    c[:, C_RST:C_RST + 512] = np.arange(512) % 64 != 0
    h = np.arange(32)
    c[32:64, C_LH:C_LH + 128] = (h[:, None] % 2) == (p[None] // 64)
    c[32:64, C_PM:C_PM + 16] = (h[:, None] // 2) == np.arange(16)[None]
    c[32:64, C_SEL:C_SEL + 32] = np.eye(32)
    c[:, C_TRI:C_TRI + 128] = p[:, None] < p[None]
    c[:, C_IOTA:C_IOTA + NTOK] = np.arange(NTOK)
    return c


def _layout(i):
    import numpy as np
    f = np.float32
    g = {k: np.asarray(v)[0] if k not in ('x_prompt', 'x_sample', 'ln_in_g', 'ln_in_b') else np.asarray(v)
         for k, v in i.items()}
    a = {}
    x = np.zeros((384, D), f)
    x[:256] = g['x_prompt'][0]
    x[256:320] = g['x_sample'][0]
    a['x'] = x.reshape(3, 128, D)
    w = g['w_in']
    wp = np.zeros((D, NT * 128), f)
    place = [(T_RW, 6160, 3328), (T_XBC, 11536, 3072), (T_Z, 9488, 2048), (T_GLA, 3072, 3072), (T_GATE, 0, 3072)]
    for tile, col, n in place:
        wp[:, tile * 128:tile * 128 + n] = w[:, col:col + n]
    wp[:, T_MISC * 128:T_MISC * 128 + 16] = w[:, 6144:6160]
    wp[:, T_MISC * 128 + 32:T_MISC * 128 + 64] = w[:, 14608:14640]
    a['w_in'] = np.ascontiguousarray(_tiles(wp, 128))
    hist = np.zeros((128, NT, 2, HIST), f)
    hist[:, T_RW:T_RW + 26, 1, 2] = _cols(g['state_rwkv_shift'][0, 0])
    for k in range(3):
        hist[:, T_XBC:T_XBC + 24, 1, k] = _cols(g['state_ssm_conv'][0, k])
    a['hist'] = hist
    v = np.zeros((128, NV), f)
    for at, name in ((V_MU, 'rwkv_mu'), (V_W0, 'rwkv_w0'), (V_A0, 'rwkv_a0'), (V_KK, 'rwkv_k_k'), (V_KA, 'rwkv_k_a'),
                     (V_RK, 'rwkv_r_k'), (V_LNG, 'rwkv_ln_g'), (V_LNB, 'rwkv_ln_b'), (V_BA, 'gla_ba'),
                     (V_GNG, 'gla_norm_g'), (V_CB, 'ssm_conv_b'), (V_SNG, 'ssm_norm_g')):
        c = _cols(g[name])
        v[:, at:at + c.shape[1]] = c
    for k in range(4):
        v[:, V_CW + 24 * k:V_CW + 24 * k + 24] = _cols(g['ssm_conv_w'][k])
    d = g['ssm_d'].reshape(16, 2).T
    v[0:64, V_DSK:V_DSK + 16] = d[0]
    v[64:128, V_DSK:V_DSK + 16] = d[1]
    v[32:64, V_DTB] = g['ssm_dt_bias']
    v[32:64, V_ALOG] = g['ssm_a_log']
    for k in range(3):
        v[:, V_TOK8 + k] = 8.0 * (np.arange(128) + 128 * k)
    a['vecs'] = v
    a['consts'] = _constants()
    sm = np.zeros((128, 3 * D + 512), f)
    sm[0:64, 0:D] = g['rwkv_w2']
    sm[64:128, D:2 * D] = g['rwkv_a2']
    sm[:, 2 * D:3 * D] = g['rwkv_g2']
    sm[0:16, 3 * D:] = g['gla_wa2']
    a['small_w'] = sm
    wo = np.zeros((8, 4, 128, 8, 128), f)
    wo[:, 0] = _tiles(g['rwkv_wo'], 128)
    wo[:, 1] = _tiles(g['gla_wo'], 128)
    wo[:, 2] = _tiles(g['ssm_wo'][:D], 128)
    wo[:, 3] = _tiles(g['ssm_wo'][D:], 128)
    a['wo'] = wo
    a['w_out'] = np.ascontiguousarray(_tiles(g['w_out'], D)[0])
    a['lnv'] = np.stack([g[k] for k in ('ln_in_g', 'ln_in_b', 'ln1_g', 'ln1_b', 'ln2_g', 'ln2_b')])
    a['w_router'] = np.ascontiguousarray(_tiles(g['w_router'], NE)[0])
    a['router_bias'] = g['router_bias'].reshape(1, NE)

    def expert(w1, w3, w2):
        e = np.empty((128, 6144), f)
        b = e[:, 0:4096].reshape(128, KT, 512)
        b[:, :, 0:256] = _tiles(w1, 256)[0]
        b[:, :, 256:512] = _tiles(w3, 256)[0]
        e[:, 4096:] = _tiles(w2, D)[0].reshape(128, 2 * D)
        return e

    m = np.empty((NE + 1, 128, 6144), f)
    for e in range(NE):
        m[e] = expert(g['exp_w1'][e], g['exp_w3'][e], g['exp_w2'][e])
    m[NE] = expert(g['sh_w1'], g['sh_w3'], g['sh_w2'])
    a['moe_w'] = m
    s = g['state_rwkv'][0].reshape(8, 2, 64, 64)
    a['st_rwkv'] = np.ascontiguousarray(s.transpose(1, 3, 0, 2).reshape(128, 8, 64))
    a['st_gla'] = np.ascontiguousarray(g['state_gla'][0].transpose(1, 0, 2))
    a['st_ssm'] = np.ascontiguousarray(g['state_ssm'][0].transpose(2, 0, 1)).reshape(128, 2048)
    return {k: np.ascontiguousarray(z, dtype=f) for k, z in a.items()}


_OUTS = [('y', (3, 128, D)), ('gla', (2, 128, 4, 256)), ('rwkv', (2, 128, 8, 64)), ('shift', (2, 128, 26)),
         ('ssm', (2, 128, 2048)), ('conv', (2, 128, 24, 3))]


def kernel(**inputs):
    import numpy as _np
    import concourse.bacc as _bacc
    from concourse import mybir as _mybir
    from concourse.bass_utils import run_bass_kernel_spmd as _run

    nc = _bacc.Bacc("TRN2", target_bir_lowering=False, num_devices=1)
    a = _layout(inputs)
    io = {k: nc.dram_tensor(k, v.shape, _mybir.dt.from_np(v.dtype), kind="ExternalInput").ap() for k, v in a.items()}
    for n, s in _OUTS:
        io['out_' + n] = nc.dram_tensor('out_' + n, s, _mybir.dt.float32, kind="ExternalOutput").ap()
    hybrid_layer(nc, io)
    r = _run(nc, [a], core_ids=[0]).results[0]
    y = r['out_y'].reshape(384, D)
    gla = r['out_gla'].transpose(0, 2, 1, 3)
    rw = r['out_rwkv'].reshape(2, 2, 64, 8, 64).transpose(0, 3, 1, 4, 2).reshape(2, 16, 64, 64)
    sh = r['out_shift'].transpose(0, 2, 1).reshape(2, 3328)
    ss = r['out_ssm'].reshape(2, 128, 32, 64).transpose(0, 2, 3, 1)
    cv = r['out_conv'].transpose(0, 3, 2, 1).reshape(2, 3, 3072)
    c = _np.ascontiguousarray

    def states(s):
        return (c(gla[s])[None, None], c(rw[s])[None, None], c(sh[s])[None, None, None], c(ss[s])[None, None],
                c(cv[s])[None, None])

    return (c(y[:256])[None], c(y[256:320])[None]) + states(0) + states(1)
```
